# Optimizing a Trainium2 kernel written in Bass

```python
import math
import jax
import jax.numpy as jnp
from jax import lax
import numpy as np

D_MODEL = 1024
BATCH = 1
SEQ = 256
DEPTH = 2

HEAD_DIM = 64
MOBA_HEADS = 8
MOBA_BLOCK = 256
MOBA_TOPK = 3
MOBA_Q_CHUNK = 32
SSM_D_INNER = D_MODEL
SSM_HEADDIM = 64
SSM_HEADS = SSM_D_INNER // SSM_HEADDIM
SSM_GROUPS = 4
SSM_STATE = 128
SSM_CONV = 4
SSM_CHUNK = 128
DT_MIN = 0.001
DT_MAX = 0.1
A_INIT_MAX = 16.0
DIL_HEADS = D_MODEL // HEAD_DIM
DIL_BRANCHES = ((128, 1), (512, 4), (2048, 16))
DIL_BLOCK = 128
REL_BUCKETS = 32
REL_MAX_DIST = 2048
REL_HEADS = max(MOBA_HEADS, DIL_HEADS)
FFN_DENSE = 2816
N_EXPERTS = 8
MOE_TOPK = 2
FFN_EXPERT = 3584
DEEPNORM_ALPHA = (2.0 * DEPTH) ** 0.25
DEEPNORM_BETA = (8.0 * DEPTH) ** -0.25
LN_EPS = 1e-5
RMS_EPS = 1e-5
N_EVEN = (DEPTH + 1) // 2
N_ODD = DEPTH // 2
MOBA_W = MOBA_HEADS * HEAD_DIM
SSM_BC = SSM_GROUPS * SSM_STATE
SSM_XBC = SSM_D_INNER + 2 * SSM_BC
EVEN_SPLITS = (MOBA_W, 2 * MOBA_W, 3 * MOBA_W, 3 * MOBA_W + SSM_D_INNER, 3 * MOBA_W + SSM_D_INNER + SSM_XBC)
EVEN_IN = 3 * MOBA_W + SSM_D_INNER + SSM_XBC + SSM_HEADS
EVEN_MIX = MOBA_W + SSM_D_INNER
DIL_W = DIL_HEADS * HEAD_DIM

kernel_name = "hybrid_moba_ssd_dilated_moe_trunk"

def layer_norm(x, g, b):
    xf = x.astype(jnp.float32)
    mu = jnp.mean(xf, axis=-1, keepdims=True)
    var = jnp.mean(jnp.square(xf - mu), axis=-1, keepdims=True)
    return ((xf - mu) * lax.rsqrt(var + LN_EPS) * g.astype(jnp.float32) + b.astype(jnp.float32)).astype(x.dtype)

def gated_rms_norm(y, z, g):
    B, S, Din = y.shape
    yf = (y.astype(jnp.float32) * jax.nn.silu(z.astype(jnp.float32))).reshape(B, S, SSM_GROUPS, Din // SSM_GROUPS)
    yf = yf * lax.rsqrt(jnp.mean(yf * yf, axis=-1, keepdims=True) + RMS_EPS)
    return (yf.reshape(B, S, Din) * g.astype(jnp.float32)).astype(y.dtype)

def rel_bucket(dist):
    max_exact = REL_BUCKETS // 2
    d = jnp.maximum(dist, 0)
    df = jnp.maximum(d, 1).astype(jnp.float32)
    large = max_exact + (jnp.log(df / max_exact) / math.log(REL_MAX_DIST / max_exact)
                         * (REL_BUCKETS - max_exact)).astype(jnp.int32)
    large = jnp.minimum(large, REL_BUCKETS - 1)
    return jnp.where(d < max_exact, d, large)

def moba_attention(q, k, v, rel_bias):
    B, S, H, hd = q.shape
    nblk = -(-S // MOBA_BLOCK)
    pad = nblk * MOBA_BLOCK - S
    kk = min(MOBA_TOPK, nblk)
    scale = hd ** -0.5
    qh = q.transpose(0, 2, 1, 3)

    def blocks(a):
        a = jnp.pad(a, ((0, 0), (0, pad), (0, 0), (0, 0))).transpose(0, 2, 1, 3)
        return a.reshape(B, H, nblk, MOBA_BLOCK, hd)

    kb, vb = blocks(k), blocks(v)
    k_mean = jnp.mean(kb.astype(jnp.float32), axis=3)
    pos = jnp.arange(S, dtype=jnp.int32)
    gate = jnp.einsum('bhsd,bhnd->bhsn', qh.astype(jnp.float32), k_mean)
    fully_past = jnp.arange(nblk, dtype=jnp.int32)[None, :] < (pos // MOBA_BLOCK)[:, None]
    gate = jnp.where(fully_past, gate, -jnp.inf)
    sel_val, sel_idx = lax.top_k(gate, kk)
    sel_ok = sel_val > -jnp.inf
    bias_h = rel_bias[:, :H].T.astype(jnp.float32)
    n_chunks = S // MOBA_Q_CHUNK
    b_ix = jnp.arange(B)[:, None, None, None]
    h_ix = jnp.arange(H)[None, :, None, None]
    key_off = jnp.arange(MOBA_BLOCK, dtype=jnp.int32)

    def to_chunks(a):
        a = a.reshape(B, H, n_chunks, MOBA_Q_CHUNK, *a.shape[3:])
        return jnp.moveaxis(a, 2, 0)

    def attend_chunk(args):
        c, qc, idx, ok = args
        qpos = c * MOBA_Q_CHUNK + jnp.arange(MOBA_Q_CHUNK, dtype=jnp.int32)
        own = (c * MOBA_Q_CHUNK) // MOBA_BLOCK
        k_own = lax.dynamic_index_in_dim(kb, own, axis=2, keepdims=False)
        v_own = lax.dynamic_index_in_dim(vb, own, axis=2, keepdims=False)
        dist_own = qpos[:, None] - (own * MOBA_BLOCK + key_off)[None, :]
        s_own = jnp.einsum('bhqd,bhjd->bhqj', qc, k_own).astype(jnp.float32) * scale
        s_own = s_own + bias_h[:, rel_bucket(dist_own)]
        s_own = jnp.where(dist_own >= 0, s_own, -jnp.inf)
        k_sel = kb[b_ix, h_ix, idx]
        v_sel = vb[b_ix, h_ix, idx]
        dist_sel = qpos[:, None, None] - (idx[..., None] * MOBA_BLOCK + key_off)
        s_sel = jnp.einsum('bhqd,bhqkjd->bhqkj', qc, k_sel).astype(jnp.float32) * scale
        s_sel = s_sel + bias_h[h_ix[..., None], rel_bucket(dist_sel)]
        s_sel = jnp.where(ok[..., None], s_sel, -jnp.inf)
        n_q = qc.shape[2]
        scores = jnp.concatenate([s_own, s_sel.reshape(B, H, n_q, kk * MOBA_BLOCK)], axis=-1)
        p = jax.nn.softmax(scores, axis=-1).astype(v.dtype)
        p_own = p[..., :MOBA_BLOCK]
        p_sel = p[..., MOBA_BLOCK:].reshape(B, H, n_q, kk, MOBA_BLOCK)
        return (jnp.einsum('bhqj,bhjd->bhqd', p_own, v_own)
                + jnp.einsum('bhqkj,bhqkjd->bhqd', p_sel, v_sel))

    out = lax.map(attend_chunk, (jnp.arange(n_chunks, dtype=jnp.int32), to_chunks(qh),
                                 to_chunks(sel_idx), to_chunks(sel_ok)))
    out = jnp.moveaxis(out, 0, 2).reshape(B, H, S, hd)
    return out.transpose(0, 2, 1, 3)

def causal_depthwise_conv(u, w, b):
    out = lax.conv_general_dilated(u, w[:, None, :].astype(u.dtype), window_strides=(1,),
                                   padding=((SSM_CONV - 1, 0),),
                                   dimension_numbers=('NWC', 'WIO', 'NWC'),
                                   feature_group_count=u.shape[-1])
    return out + b.astype(u.dtype)

def ssd_scan(xh, dt, A, Bg, Cg):
    Bsz, S, H, P = xh.shape
    G, N = Bg.shape[2], Bg.shape[3]
    R = H // G
    L = SSM_CHUNK
    nc = S // L
    x = (xh * dt[..., None]).reshape(Bsz, nc, L, G, R, P)
    a = (dt * A).reshape(Bsz, nc, L, G, R)
    Bc = Bg.reshape(Bsz, nc, L, G, N)
    Cc = Cg.reshape(Bsz, nc, L, G, N)
    a_cs = jnp.cumsum(a, axis=2)
    causal = jnp.tril(jnp.ones((L, L), dtype=bool))
    seg = a_cs[:, :, :, None] - a_cs[:, :, None]
    decay = jnp.exp(jnp.where(causal[:, :, None, None], seg, -jnp.inf))
    cb = jnp.einsum('bclgn,bcsgn->bclsg', Cc, Bc)
    y_diag = jnp.einsum('bclsg,bclsgr,bcsgrp->bclgrp', cb, decay, x)
    decay_to_end = jnp.exp(a_cs[:, :, -1:] - a_cs)
    chunk_states = jnp.einsum('bclgn,bclgr,bclgrp->bcgrpn', Bc, decay_to_end, x)
    chunk_decay = jnp.exp(a_cs[:, :, -1])

    def step(h, inp):
        st, dec = inp
        return h * dec[..., None, None] + st, h

    h0 = jnp.zeros((Bsz, G, R, P, N), jnp.float32)
    _, h_in = lax.scan(step, h0, (jnp.moveaxis(chunk_states, 1, 0), jnp.moveaxis(chunk_decay, 1, 0)))
    h_in = jnp.moveaxis(h_in, 0, 1)
    y_off = jnp.einsum('bclgn,bcgrpn,bclgr->bclgrp', Cc, h_in, jnp.exp(a_cs))
    return (y_diag + y_off).reshape(Bsz, S, H, P)

def mamba2_mixer(z, xbc, dt_raw, conv_w, conv_b, dt_bias, A_log, D_skip, norm_g):
    Bsz, S, _ = z.shape
    xbc = jax.nn.silu(causal_depthwise_conv(xbc, conv_w, conv_b))
    xs, Bm, Cm = jnp.split(xbc, (SSM_D_INNER, SSM_D_INNER + SSM_BC), axis=-1)
    xs = xs.reshape(Bsz, S, SSM_HEADS, SSM_HEADDIM).astype(jnp.float32)
    dt = jax.nn.softplus(dt_raw.astype(jnp.float32) + dt_bias.astype(jnp.float32))
    A = -jnp.exp(A_log.astype(jnp.float32))
    y = ssd_scan(xs, dt, A,
                 Bm.reshape(Bsz, S, SSM_GROUPS, SSM_STATE).astype(jnp.float32),
                 Cm.reshape(Bsz, S, SSM_GROUPS, SSM_STATE).astype(jnp.float32))
    y = y + D_skip.astype(jnp.float32)[:, None] * xs
    return gated_rms_norm(y.reshape(Bsz, S, SSM_D_INNER).astype(z.dtype), z, norm_g)

def dilated_attention(q, k, v, rel_bias):
    B, S, H, hd = q.shape
    scale = hd ** -0.5
    bias_h = rel_bias[:, :H].T.astype(jnp.float32)
    qi = jnp.arange(DIL_BLOCK, dtype=jnp.int32)[:, None]
    ki = jnp.arange(2 * DIL_BLOCK, dtype=jnp.int32)[None, :]
    steps = qi + DIL_BLOCK - ki
    outs, lses = [], []
    for window, dil in DIL_BRANCHES:
        span = window // dil
        L = S // dil
        nb = -(-L // DIL_BLOCK)
        Lp = nb * DIL_BLOCK

        def by_residue(a):
            a = a.reshape(B, L, dil, H, hd).transpose(0, 3, 2, 1, 4)
            return jnp.pad(a, ((0, 0), (0, 0), (0, 0), (0, Lp - L), (0, 0)))

        def banded(a):
            a = jnp.pad(by_residue(a), ((0, 0), (0, 0), (0, 0), (DIL_BLOCK, 0), (0, 0)))
            a = a.reshape(B, H, dil, nb + 1, DIL_BLOCK, hd)
            return jnp.concatenate([a[:, :, :, :-1], a[:, :, :, 1:]], axis=-2)

        qb = by_residue(q).reshape(B, H, dil, nb, DIL_BLOCK, hd)
        kb, vb = banded(k), banded(v)
        key_idx = jnp.arange(nb, dtype=jnp.int32)[:, None, None] * DIL_BLOCK + ki[None] - DIL_BLOCK
        valid = (steps >= 0) & (steps <= span) & (key_idx >= 0)
        s = jnp.einsum('bhrnqd,bhrnkd->bhrnqk', qb, kb).astype(jnp.float32) * scale
        s = s + bias_h[:, rel_bucket(steps * dil)][None, :, None, None]
        s = jnp.where(valid, s, -jnp.inf)
        m = jnp.max(s, axis=-1, keepdims=True)
        e = jnp.exp(s - m)
        den = jnp.sum(e, axis=-1)
        o = jnp.einsum('bhrnqk,bhrnkd->bhrnqd', e.astype(v.dtype), vb).astype(jnp.float32) / den[..., None]
        lse = m[..., 0] + jnp.log(den)
        o = o.reshape(B, H, dil, Lp, hd)[:, :, :, :L].transpose(0, 3, 2, 1, 4).reshape(B, S, H, hd)
        lse = lse.reshape(B, H, dil, Lp)[:, :, :, :L].transpose(0, 3, 2, 1).reshape(B, S, H)
        outs.append(o)
        lses.append(lse)
    w = jax.nn.softmax(jnp.stack(lses), axis=0)
    return jnp.sum(w[..., None] * jnp.stack(outs), axis=0).astype(q.dtype)

def even_mixer(x, w_in, conv_w, conv_b, dt_bias, A_log, D_skip, norm_g, w_out, rel_bias):
    B, S, _ = x.shape
    proj = x @ w_in
    q, k, v, z, xbc, dt_raw = jnp.split(proj, EVEN_SPLITS, axis=-1)
    shp = (B, S, MOBA_HEADS, HEAD_DIM)
    attn = moba_attention(q.reshape(shp), k.reshape(shp), v.reshape(shp), rel_bias).reshape(B, S, MOBA_W)
    ssm = mamba2_mixer(z, xbc, dt_raw, conv_w, conv_b, dt_bias, A_log, D_skip, norm_g)
    return jnp.concatenate([attn, ssm], axis=-1) @ w_out

def odd_mixer(x, w_qkv, w_out, rel_bias):
    B, S, _ = x.shape
    q, k, v = jnp.split(x @ w_qkv, 3, axis=-1)
    shp = (B, S, DIL_HEADS, HEAD_DIM)
    o = dilated_attention(q.reshape(shp), k.reshape(shp), v.reshape(shp), rel_bias)
    return o.reshape(B, S, DIL_W) @ w_out

def swiglu(x, w_in, w_down):
    g, u = jnp.split(x @ w_in, 2, axis=-1)
    return (jax.nn.silu(g) * u) @ w_down

def moe_swiglu(x, w_router, w_in, w_down):
    logits = (x @ w_router).astype(jnp.float32)
    top_val, top_idx = lax.top_k(logits, MOE_TOPK)
    gates = jax.nn.softmax(top_val, axis=-1)
    combine = jnp.sum(jax.nn.one_hot(top_idx, N_EXPERTS, dtype=jnp.float32) * gates[..., None], axis=-2)

    def per_row(args):
        xr, cr = args
        g, u = jnp.split(jnp.einsum('sd,edf->sef', xr, w_in), 2, axis=-1)
        act = jax.nn.silu(g) * u * cr.astype(xr.dtype)[..., None]
        return jnp.einsum('sef,efd->sd', act, w_down)

    return lax.map(per_row, (x, combine))

def setup_inputs(seed: int = 0) -> dict:
    key = jax.random.key(seed)
    ks = iter(jax.random.split(key, 32))

    def nrm(shape, scale):
        return jax.random.normal(next(ks), shape, jnp.float32) * scale

    D = D_MODEL
    x = nrm((BATCH, SEQ, D), 1.0)
    rel_bias = nrm((REL_BUCKETS, REL_HEADS), 0.5)
    ln_mix_g = 1.0 + nrm((DEPTH, D), 0.02)
    ln_mix_b = nrm((DEPTH, D), 0.02)
    ln_ffn_g = 1.0 + nrm((DEPTH, D), 0.02)
    ln_ffn_b = nrm((DEPTH, D), 0.02)
    even_w_in = nrm((N_EVEN, D, EVEN_IN), D ** -0.5)
    even_conv_w = nrm((N_EVEN, SSM_CONV, SSM_XBC), SSM_CONV ** -0.5)
    even_conv_b = nrm((N_EVEN, SSM_XBC), 0.02)
    u = jax.random.uniform(next(ks), (N_EVEN, SSM_HEADS), jnp.float32)
    dt0 = jnp.exp(u * (math.log(DT_MAX) - math.log(DT_MIN)) + math.log(DT_MIN))
    even_dt_bias = dt0 + jnp.log(-jnp.expm1(-dt0))
    even_A_log = jnp.log(jax.random.uniform(next(ks), (N_EVEN, SSM_HEADS), jnp.float32, 1.0, A_INIT_MAX))
    even_D = 1.0 + nrm((N_EVEN, SSM_HEADS), 0.02)
    even_norm_g = 1.0 + nrm((N_EVEN, SSM_D_INNER), 0.02)
    even_w_out = nrm((N_EVEN, EVEN_MIX, D), EVEN_MIX ** -0.5 * DEEPNORM_BETA)
    ffn_w_in = nrm((N_EVEN, D, 2 * FFN_DENSE), D ** -0.5)
    ffn_w_down = nrm((N_EVEN, FFN_DENSE, D), FFN_DENSE ** -0.5 * DEEPNORM_BETA)
    odd_w_qkv = nrm((N_ODD, D, 3 * DIL_W), D ** -0.5)
    odd_w_out = nrm((N_ODD, DIL_W, D), DIL_W ** -0.5 * DEEPNORM_BETA)
    moe_router = nrm((N_ODD, D, N_EXPERTS), D ** -0.5)
    moe_w_in = nrm((N_ODD, N_EXPERTS, D, 2 * FFN_EXPERT), D ** -0.5)
    moe_w_down = nrm((N_ODD, N_EXPERTS, FFN_EXPERT, D), FFN_EXPERT ** -0.5 * DEEPNORM_BETA)
    return {"x": x, "rel_bias": rel_bias, "ln_mix_g": ln_mix_g, "ln_mix_b": ln_mix_b,
            "ln_ffn_g": ln_ffn_g, "ln_ffn_b": ln_ffn_b, "even_w_in": even_w_in,
            "even_conv_w": even_conv_w, "even_conv_b": even_conv_b, "even_dt_bias": even_dt_bias,
            "even_A_log": even_A_log, "even_D": even_D, "even_norm_g": even_norm_g,
            "even_w_out": even_w_out, "ffn_w_in": ffn_w_in, "ffn_w_down": ffn_w_down,
            "odd_w_qkv": odd_w_qkv, "odd_w_out": odd_w_out, "moe_router": moe_router,
            "moe_w_in": moe_w_in, "moe_w_down": moe_w_down}

def reference(x, rel_bias, ln_mix_g, ln_mix_b, ln_ffn_g, ln_ffn_b, even_w_in, even_conv_w,
              even_conv_b, even_dt_bias, even_A_log, even_D, even_norm_g, even_w_out,
              ffn_w_in, ffn_w_down, odd_w_qkv, odd_w_out, moe_router, moe_w_in, moe_w_down):
    for l in range(DEPTH):
        e = l // 2
        if l % 2 == 0:
            h = even_mixer(x, even_w_in[e], even_conv_w[e], even_conv_b[e], even_dt_bias[e],
                           even_A_log[e], even_D[e], even_norm_g[e], even_w_out[e], rel_bias)
        else:
            h = odd_mixer(x, odd_w_qkv[e], odd_w_out[e], rel_bias)
        x = layer_norm(DEEPNORM_ALPHA * x + h, ln_mix_g[l], ln_mix_b[l])
        if l % 2 == 0:
            f = swiglu(x, ffn_w_in[e], ffn_w_down[e])
        else:
            f = moe_swiglu(x, moe_router[e], moe_w_in[e], moe_w_down[e])
        x = layer_norm(DEEPNORM_ALPHA * x + f, ln_ffn_g[l], ln_ffn_b[l])
    return x


_drawn_inputs = setup_inputs


def setup_inputs(seed=0):
    import zlib

    import numpy as np

    out = dict(_drawn_inputs(seed))
    spreads = {}
    factors = {'even_conv_b': 5.419, 'even_D': 8.0, 'even_norm_g': 8.0}
    for name, (base, spread) in spreads.items():
        noise = np.random.default_rng([zlib.crc32(name.encode()), seed]).standard_normal(out[name].shape)
        drawn = base * np.exp(spread * noise) if base else spread * noise
        out[name] = jnp.asarray(drawn.astype(out[name].dtype))
    for name, factor in factors.items():
        out[name] = (out[name] * factor).astype(out[name].dtype)
    return out
```

```python
import math
from contextlib import ExitStack, contextmanager

import numpy as np

import concourse.bass as bass
from concourse import mybir

F32 = mybir.dt.float32
F32R = mybir.dt.float32r
BF16 = mybir.dt.bfloat16
ALU = mybir.AluOpType
ACT = mybir.ActivationFunctionType
AX_X = mybir.AxisListType.X

P = 128
SEQ = 256
D = 1024
TT = SEQ // P
KC = D // P
HD = 64
EH = 8
OH = 16
SH = 16
SG = 4
CONV = 4
XBC_T = 16
FFN = 2816
NE = 8
FE = 3584
BUCKETS = 32
ALPHA = (2.0 * 2) ** 0.25
EPS = 1e-5
QSCALE = HD ** -0.5
MASKED = -1.0e30

RAW = 6
CUT = 3
UNIT = 2048
FFN_STEPS = FFN // 256
FE_STEPS = FE // 512
ROUNDS = SEQ // P

C_ID, C_UP, C_ONE, C_SU, C_JROW, C_REV, C_IDX, C_IDX8 = 0, 128, 256, 384, 512, 640, 768, 776
C_W = 784


def shape_constants():
    c = np.zeros((P, C_W), np.float32)
    i = np.arange(P)
    c[:, C_ID:C_ID + P] = np.eye(P)
    c[:, C_UP:C_UP + P] = i[:, None] <= i[None, :]
    c[:, C_ONE:C_ONE + P] = 1.0
    c[:, C_SU:C_SU + P] = i[:, None] < i[None, :]
    c[:, C_JROW:C_JROW + P] = i[None, :]
    c[:, C_REV:C_REV + P] = i[:, None] + i[None, :] == P - 1
    c[:, C_IDX:C_IDX + NE] = np.arange(NE)
    c[:, C_IDX8:C_IDX8 + NE] = np.arange(NE) + NE
    hot = np.zeros((BUCKETS + 1, 2, 512), np.float32)
    for col in range(2 * SEQ - 1):
        d = SEQ - 1 - col
        if d < 0:
            hot[BUCKETS, :, col] = MASKED
            continue
        half = BUCKETS // 2
        b = d if d < half else min(BUCKETS - 1, half + int(math.log(d / half) / math.log(2048 / half) * half))
        hot[b, :, col] = 1.0 / QSCALE
        seen = (d <= 128) + (d % 4 == 0) + (d % 16 == 0)
        hot[BUCKETS, 1, col] = math.log(seen) / QSCALE if seen else MASKED
    return c, hot


class Tally:

    def __init__(self, n=0):
        self.n = n
        self.loops = []

    def at(self, back=0):
        v = self.n - back
        for i, k in self.loops:
            v = i * k + v
        return v

    def up(self, k=1):
        self.n += k
        return self.at()

    def started(self, back=0):
        return bool(self.loops) or self.n - back > 0


@contextmanager
def rounds(eng, count, steps):
    first = {t: t.n for t in steps}
    with eng.Fori(0, count) as i:
        for t, k in steps.items():
            t.loops.append((i, k))
        yield i
    for t, k in steps.items():
        assert t.n - first[t] == k, (t.n - first[t], k)
        t.loops.pop()
        if isinstance(count, int):
            t.n = first[t] + k * count
        else:
            t.n = first[t]
            t.loops.append((count, k))


def trunk(nc, x, rel_bias, ln_mix_g, ln_mix_b, ln_ffn_g, ln_ffn_b, even_w_in, even_conv_w,
          even_conv_b, even_dt_bias, even_A_log, even_D, even_norm_g, even_w_out,
          ffn_w_in, ffn_w_down, odd_w_qkv, odd_w_out, moe_router, moe_w_in, moe_w_down,
          const_in, hot_in, out):
    with ExitStack() as ctx:
        def sb(name, shape, dt=F32):
            return ctx.enter_context(nc.sbuf_tensor(name, shape, dt))

        def sem(name):
            return ctx.enter_context(nc.semaphore(name))

        raw = sb("raw", [P, RAW, UNIT])
        w_hi = sb("w_hi", [P, CUT, UNIT], F32R)
        w_lo = sb("w_lo", [P, CUT, UNIT], F32R)
        t_hi = sb("t_hi", [P, 12 * SEQ], F32R)
        t_lo = sb("t_lo", [P, 12 * SEQ], F32R)
        aT_hi = sb("aT_hi", [P, 512], F32R)
        aT_lo = sb("aT_lo", [P, 512], F32R)
        xn = sb("xn", [P, TT, D])
        con = sb("con", [P, C_W])
        zt = sb("zt", [P, 512], BF16)
        arena = sb("arena", [P, 17200])
        rel33 = sb("rel33", [BUCKETS + 1, OH])
        pcol = sb("pcol", [P, 80])
        w_dt = sb("w_dt", [P, KC, SH])
        hpar = sb("hpar", [P, 3, SH])
        dts = sb("dts", [P, 8, TT * SH])
        acs = sb("acs", [P, TT, SH])
        rmx = sb("rmx", [P, 2, 4])
        rneg = sb("rneg", [P, 2, 4])
        rsum = sb("rsum", [P, TT, OH])
        rinv = sb("rinv", [P, TT, OH])
        stat = sb("stat", [P, TT, 2, 6])
        mv = sb("mv", [P, TT, 2])
        rstd = sb("rstd", [P, TT, 3])
        gss = sb("gss", [P, 3, TT * SG])
        rout = sb("rout", [P, KC, NE])
        lg = sb("lg", [P, 10, TT * NE])
        l1 = sb("l1", [P, 8, TT])
        rot = sb("rot", [P, NE, 4])
        rtm = sb("rtm", [P, NE, 4])
        cj = sb("cj", [P, 1])
        runs = sb("runs", [1, 1], mybir.dt.int32)

        def area(at, n, **kw):
            return arena[:, at:at + n]

        ident = con[:, C_ID:C_ID + P]
        upper = con[:, C_UP:C_UP + P]
        upper_ones = con[:, C_UP:C_UP + 2 * P]
        ones = con[:, C_ONE:C_ONE + P]
        strict = con[:, C_SU:C_SU + P]
        jrow = con[:, C_JROW:C_JROW + P]
        rev = con[:, C_REV:C_REV + P]

        PADW = SEQ + CONV - 1
        xp = area(0, XBC_T * PADW).rearrange("p (c s) -> p c s", c=XBC_T)
        cv = area(4144, XBC_T * SEQ).rearrange("p (c s) -> p c s", c=XBC_T)
        zs = area(8240, TT * D).rearrange("p (t c) -> p t c", t=TT)
        v_e = area(10288, TT * 512).rearrange("p (t c) -> p t c", t=TT)
        kT_e = area(11312, 4 * SEQ).rearrange("p (c s) -> p c s", c=4)
        F_e = area(12336, EH * SEQ).rearrange("p (h s) -> p h s", h=EH)
        mix_e = area(12336, TT * 1536).rearrange("p (t c) -> p t c", t=TT)
        hot = arena[0:BUCKETS + 1, 12336:12336 + 1024].rearrange("p (l s) -> p l s", l=2)
        crow = arena[0:80, 16432:16560]
        tbs = arena[0:OH, 13360:14384].rearrange("p (l s) -> p l s", l=2)
        qz_e = area(14384, EH * SEQ).rearrange("p (h s) -> p h s", h=EH)
        normg = area(15408, D)
        work_e = area(0, 2048)
        xs = area(0, TT * D).rearrange("p (t c) -> p t c", t=TT)
        xdt = area(2048, TT * D).rearrange("p (t c) -> p t c", t=TT)
        tmpd = area(10288, 768).rearrange("p (b s) -> p b s", b=2)
        decay = area(11056, 768).rearrange("p (b s) -> p b s", b=2)
        cbm = area(16432, 768).rearrange("p (b s) -> p b s", b=2)
        gb = area(12288, 2 * D).rearrange("p (g c) -> p g c", g=2)
        F_o = area(0, OH * SEQ).rearrange("p (h s) -> p h s", h=OH)
        qz_o = area(4096, OH * SEQ).rearrange("p (h s) -> p h s", h=OH)
        kT_o = area(8192, 8 * SEQ).rearrange("p (c s) -> p c s", c=8)
        v_o = area(10240, TT * D).rearrange("p (t c) -> p t c", t=TT)
        work_o = area(14336, 2048)
        mix_o = area(4096, TT * D).rearrange("p (t c) -> p t c", t=TT)
        a_sb = area(14336, 512)
        s_sb = area(14848, 512)
        acc = area(0, TT * D).rearrange("p (t c) -> p t c", t=TT)
        Pm = area(2048, TT * P).rearrange("p (t j) -> p t j", t=TT)
        y_hi = t_hi[:, 1024:2048]
        y_lo = t_lo[:, 1024:2048]
        PmT = t_hi[:, 2048:2048 + SEQ]
        r_hi = t_hi[:, 2304:2304 + KC * NE]
        r_lo = t_lo[:, 2304:2304 + KC * NE]
        xT_hi = t_hi[:, 0:KC * SEQ].rearrange("p (c s) -> p c s", c=KC)
        xT_lo = t_lo[:, 0:KC * SEQ].rearrange("p (c s) -> p c s", c=KC)
        mT_hi = t_hi[:, :].rearrange("p (c s) -> p c s", c=12)
        mT_lo = t_lo[:, :].rearrange("p (c s) -> p c s", c=12)
        xg_hi = t_hi[:, 0:D].rearrange("p (c j) -> p c j", c=KC)
        xg_lo = t_lo[:, 0:D].rearrange("p (c j) -> p c j", c=KC)

        ps = ctx.enter_context(nc.psum_tensor("ps", [P, 8, 512], F32))
        table = nc.dram_tensor("bias_by_distance", [2, OH, 512], F32, kind="Internal").ap()

        raw_in = [sem(f"raw_in{i}") for i in range(RAW)]
        hi_done = sem("hi_done")
        lo_done = sem("lo_done")
        w_used = sem("w_used")
        con_in = sem("con_in")
        x_in = sem("x_in")
        par_in = sem("par_in")
        set_up = sem("set_up")
        tab_ps = sem("tab_ps")
        tab_sb = sem("tab_sb")
        tab_out = sem("tab_out")
        F_in = sem("F_in")
        tr_ps = sem("tr_ps")
        tr_hi = sem("tr_hi")
        tr_lo = sem("tr_lo")
        proj_ps = sem("proj_ps")
        proj_sb = sem("proj_sb")
        conv_raw = sem("conv_raw")
        conv_act = sem("conv_act")
        wdt_cut = sem("wdt_cut")
        rout_cut = sem("rout_cut")
        dt_ps = sem("dt_ps")
        dt_dve = sem("dt_dve")
        dt_act = sem("dt_act")
        acs_ps = sem("acs_ps")
        acs_sb = sem("acs_sb")
        s_ps = sem("s_ps")
        neg_max = sem("neg_max")
        p_sb = sem("p_sb")
        pT_ps = sem("pT_ps")
        pT_sb = sem("pT_sb")
        pv_ps = sem("pv_ps")
        att_sb = sem("att_sb")
        xs_ps = sem("xs_ps")
        xs_sb = sem("xs_sb")
        xdt_sb = sem("xdt_sb")
        cb_ps = sem("cb_ps")
        cb_sb = sem("cb_sb")
        seg_ps = sem("seg_ps")
        seg_sb = sem("seg_sb")
        dec_sb = sem("dec_sb")
        m_sb = sem("m_sb")
        y_ps = sem("y_ps")
        mix_sb = sem("mix_sb")
        wout_ps = sem("wout_ps")
        ln_var = sem("ln_var")
        ln_sd = sem("ln_sd")
        x_new = sem("x_new")
        dve_seq = sem("dve_seq")
        ln_seq = sem("ln_seq")
        h_ps = sem("h_ps")
        s_act = sem("s_act")
        a_dve = sem("a_dve")
        aT_ps = sem("aT_ps")
        aT_h = sem("aT_h")
        aT_l = sem("aT_l")
        rt_ps = sem("rt_ps")
        rt_dve = sem("rt_dve")
        rt_act = sem("rt_act")
        pm_sb = sem("pm_sb")
        ga_ps = sem("ga_ps")
        xg_h = sem("xg_h")
        xg_l = sem("xg_l")
        pmT_ps = sem("pmT_ps")
        pmT_sb = sem("pmT_sb")
        down_ps = sem("down_ps")
        yh = sem("yh")
        yl = sem("yl")
        sc_ps = sem("sc_ps")
        sc_add = sem("sc_add")
        zeroed = sem("zeroed")
        done = sem("done")

        EVEN = [("v", 1024), ("z", 1536), ("z", 2048), ("k", 512), ("q", 0),
                ("x", 2560), ("x", 3072), ("x", 3584), ("x", 4096)]
        ODD = [("k", 1024), ("k", 1536), ("q", 0), ("q", 512), ("v", 2048), ("v", 2560)]
        PIECES = {"v": 2, "z": 2, "k": 2, "q": 4, "x": 2}
        pieces = [PIECES[k] for k, _ in EVEN + ODD]
        pieces_by = [sum(pieces[:n + 1]) for n in range(len(pieces))]
        TRANSPOSED = "kqx"

        def groups(heads):
            return ([(0, list(range(h, h + 4))) for h in range(0, heads, 4)]
                    + [(1, list(range(h, h + 2))) for h in range(0, heads, 2)])

        TR_BANKS = [[4, 5, 6, 7], [4, 5, 6, 7, 4, 5], [4, 5, 6, 7], [4, 5, 6, 7], [0, 1, 2, 3], [0, 1, 2, 3]]
        TR_BEFORE = [sum(len(b) for b in TR_BANKS[:n]) for n in range(7)]
        OUT_BANKS = [0, 0, 4]

        block = ctx.enter_context(nc.Block())

        @block.sync
        def _(sp):
            unit = Tally()

            def load(src, chunks):
                slot = unit.n % RAW
                if unit.started(RAW - 1) and (unit.loops or unit.n >= RAW):
                    sp.wait_ge(lo_done, unit.at(RAW - 1))
                dst = raw[:, slot, :].rearrange("p (k n) -> p k n", k=chunks)
                sp.dma_start(dst, src).then_inc(raw_in[slot], 16)
                unit.up()

            sp.dma_start(con[:, :], const_in[:, :]).then_inc(x_in, 16)
            sp.dma_start(xn[:, :, :], x[0].rearrange("(t p) c -> p t c", p=P)).then_inc(x_in, 16)
            w_in = even_w_in[0].rearrange("(k p) n -> p k n", p=P)
            for _, c0 in EVEN:
                for half in range(2):
                    load(w_in[:, 4 * half:4 * half + 4, c0:c0 + 512], 4)
            w_o = even_w_out[0].rearrange("(k p) n -> p k n", p=P)
            for u in range(6):
                load(w_o[:, 2 * u:2 * u + 2, :], 2)

            f_in = ffn_w_in[0].rearrange("(k p) n -> p k n", p=P)
            f_dn = ffn_w_down[0].rearrange("(k p) n -> p k n", p=P)

            def ffn_in(c):
                load(f_in[:, :, bass.ds(c, 256)], KC)
                load(f_in[:, :, bass.ds(c + FFN, 256)], KC)

            ffn_in(0)
            with rounds(sp, (FFN_STEPS - 1) // 2, {unit: 6}) as i:
                for j in range(2):
                    ffn_in(i * 512 + (j + 1) * 256)
                    load(f_dn[:, bass.ds(i * 4 + j * 2, 2), :], 2)
            load(f_dn[:, 2 * (FFN_STEPS - 1):2 * FFN_STEPS, :], 2)

            w_qkv = odd_w_qkv[0].rearrange("(k p) n -> p k n", p=P)
            for _, c0 in ODD:
                for half in range(2):
                    load(w_qkv[:, 4 * half:4 * half + 4, c0:c0 + 512], 4)
            w_o = odd_w_out[0].rearrange("(k p) n -> p k n", p=P)
            for u in range(4):
                load(w_o[:, 2 * u:2 * u + 2, :], 2)

            e_in = moe_w_in[0].rearrange("e (k p) n -> p e k n", p=P)
            e_dn = moe_w_down[0].rearrange("e (k p) n -> p e k n", p=P)

            def up_block(e, c):
                for half in range(2):
                    load(e_in[:, bass.ds(e, 1), 4 * half:4 * half + 4, bass.ds(c, 512)]
                         .rearrange("p e k n -> p (e k) n"), 4)

            def down_block(e, k):
                for half in range(2):
                    load(e_dn[:, bass.ds(e, 1), bass.ds(k + 2 * half, 2), :]
                         .rearrange("p e k n -> p (e k) n"), 2)

            def all_experts():
                with rounds(sp, NE, {unit: 42}) as e:
                    up_block(e, 0)
                    up_block(e, FE)
                    with rounds(sp, FE_STEPS - 1, {unit: 6}) as f:
                        up_block(e, f * 512 + 512)
                        up_block(e, f * 512 + 512 + FE)
                        down_block(e, f * 4)
                    down_block(e, 4 * (FE_STEPS - 1))

            all_experts()
            sp.wait_ge(rt_dve, 4)
            with sp.If(sp.value_load(runs[0:1, 0:1], min_val=NE, max_val=NE * ROUNDS) > NE):
                all_experts()

            sp.wait_ge(x_new, 4 * TT)
            sp.dma_start(out[0].rearrange("(t p) c -> p t c", p=P), xn[:, :, :]).then_inc(done, 16)
            sp.wait_ge(done, 16)

        @block.gpsimd
        def _(pool):
            def everywhere(src, n):
                return bass.AP(src.tensor, src.offset, [[0, P], [1, n]])

            pool.memset(zt[:, :], 0.0).then_inc(set_up, 1)
            pool.memset(rel33[:, :], 1.0).then_inc(set_up, 1)
            pool.wait_ge(set_up, 2)
            pool.dma_start(rel33[0:BUCKETS, :], rel_bias[:, :]).then_inc(con_in, 16)
            pool.dma_start(hot, hot_in[:, :, :]).then_inc(con_in, 16)
            pool.dma_start(crow[0:64, :], even_conv_w[0].rearrange("k (c p) -> (k c) p", p=P)).then_inc(con_in, 16)
            pool.dma_start(crow[64:80, :], even_conv_b[0].rearrange("(c p) -> c p", p=P)).then_inc(con_in, 16)
            pool.dma_start(w_dt[:, :, :], even_w_in[0].rearrange("(k p) n -> p k n", p=P)[:, :, 4608:4624]).then_inc(con_in, 16)
            for n, src in enumerate((even_dt_bias, even_A_log, even_D)):
                pool.dma_start(hpar[:, n, :], everywhere(src[0], SH)).then_inc(con_in, 16)
            pool.memset(qz_e, 0.0).then_inc(set_up, 1)
            pool.memset(xp, 0.0).then_inc(set_up, 1)

            pool.wait_ge(tab_sb, 2)
            pool.dma_start(table.rearrange("l h s -> h l s"), tbs).then_inc(tab_out, 16)
            pool.wait_ge(tab_out, 16)
            pool.dma_start(F_e, bass.AP(table.tensor, table.offset, [[1, P], [512, EH], [1, SEQ]])).then_inc(F_in, 16)
            pool.wait_ge(att_sb, 2)
            pool.dma_start(normg, everywhere(even_norm_g[0], D)).then_inc(par_in, 16)
            pool.wait_ge(mix_sb, 1)
            pool.dma_start(F_o, bass.AP(table.tensor, table.offset + OH * 512, [[1, P], [512, OH], [1, SEQ]])).then_inc(F_in, 16)
            pool.memset(qz_o, 0.0).then_inc(set_up, 1)
            pool.wait_ge(tr_hi, TR_BEFORE[2])
            pool.dma_start(gb[:, 0, :], everywhere(ln_mix_g[0], D)).then_inc(par_in, 16)
            pool.dma_start(gb[:, 1, :], everywhere(ln_mix_b[0], D)).then_inc(par_in, 16)
            pool.dma_start(rout[:, :, :], moe_router[0].rearrange("(k p) e -> p k e", p=P)).then_inc(con_in, 16)
            for n, (g, b) in enumerate(((ln_ffn_g[0], ln_ffn_b[0]), (ln_mix_g[1], ln_mix_b[1]), (ln_ffn_g[1], ln_ffn_b[1]))):
                pool.wait_ge(x_new, TT * (n + 1))
                pool.dma_start(gb[:, 0, :], everywhere(g, D)).then_inc(par_in, 16)
                pool.dma_start(gb[:, 1, :], everywhere(b, D)).then_inc(par_in, 16)

        @block.scalar
        def _(act):
            unit = Tally()

            def hi():
                n = unit.n
                turn = 16 * (n // RAW + 1)
                for i, k in unit.loops:
                    turn = i * (16 * k // RAW) + turn
                act.wait_ge(raw_in[n % RAW], turn)
                if unit.loops or n >= CUT:
                    act.wait_ge(w_used, unit.at(CUT - 1))
                act.activation(w_hi[:, n % CUT, :], raw[:, n % RAW, :], ACT.Copy).then_inc(hi_done, 1)
                unit.up()

            def transposed_hi(n):
                dst = mT_hi if len(TR_BANKS[n]) == 6 else xT_hi
                for j, b in enumerate(TR_BANKS[n]):
                    act.wait_ge(tr_ps, TR_BEFORE[n] + j + 1)
                    act.activation(dst[:, 2 * j:2 * j + 2, :].rearrange("p c s -> p (c s)"), ps[:, b, :], ACT.Copy).then_inc(tr_hi, 1)

            def project_evac(n):
                kind, c0 = (EVEN + ODD)[n]
                even = n < len(EVEN)
                act.wait_ge(proj_ps, n + 1)
                for b in range(2):
                    src = ps[:, 2 * (n % 2) + b, :]
                    if kind == "z":
                        act.activation(zs[:, b, c0 - 1536:c0 - 1024], src, ACT.Silu).then_inc(proj_sb, 1)
                    elif kind == "v":
                        at = c0 - (1024 if even else 2048)
                        act.activation((v_e if even else v_o)[:, b, at:at + 512], src, ACT.Copy).then_inc(proj_sb, 1)
                    elif kind == "k":
                        at = (c0 - (512 if even else 1024)) // P + 2 * b
                        act.activation((kT_e if even else kT_o)[:, at:at + 2, :], src.rearrange("p (c s) -> p c s", c=2), ACT.Copy).then_inc(proj_sb, 1)
                    elif kind == "x":
                        at = (c0 - 2560) // P + 2 * b
                        act.activation(xp[:, at:at + 2, CONV - 1:], src.rearrange("p (c s) -> p c s", c=2), ACT.Copy).then_inc(proj_sb, 1)
                    else:
                        if b == 0:
                            act.wait_ge(set_up, 4 if even else 5)
                        h0 = 2 * (c0 // P + 2 * b)
                        q = qz_e if even else qz_o
                        for s in range(2):
                            rows = slice(HD * s, HD * s + HD)
                            act.activation(q[rows, h0 + s:h0 + s + 3:2, :], src[rows, :].rearrange("p (c s) -> p c s", c=2), ACT.Copy).then_inc(proj_sb, 1)

            def silu_conv(j):
                act.wait_ge(conv_raw, j + 1)
                act.activation(cv[:, 4 * j:4 * j + 4, :], cv[:, 4 * j:4 * j + 4, :], ACT.Silu).then_inc(conv_act, 1)

            p_count = Tally()

            def attention(heads, work, first):
                p = work[:, 0:1024].rearrange("p (b s) -> p b s", b=2)
                for g, (t, hs) in enumerate(groups(heads)):
                    act.wait_ge(neg_max, first + g + 1)
                    if g >= 2:
                        act.wait_ge(pT_ps, first + g - 1)
                    w = 512 // len(hs)
                    for m, h in enumerate(hs):
                        act.activation(p[:, g % 2, m * w:(m + 1) * w], ps[:, g % 2, m * w:(m + 1) * w], ACT.Exp,
                                       bias=rneg[:, g % 2, m:m + 1], scale=QSCALE,
                                       accum_out=rsum[:, t, h:h + 1]).then_inc(p_sb, 1)

            def norm_root(n):
                act.wait_ge(ln_var, n + 1)
                act.activation(rstd[:, :, 1], rstd[:, :, 0], ACT.Sqrt).then_inc(ln_sd, 1)

            transposed_hi(0)
            for n, (kind, _) in enumerate(EVEN):
                hi()
                hi()
                if n >= 1:
                    if n == 6:
                        act.wait_ge(set_up, 4)
                    project_evac(n - 1)
                if n == 3:
                    act.wait_ge(dt_dve, 1)
                    act.activation(dts[:, 2, :], dts[:, 1, :], ACT.Exp).then_inc(dt_act, 1)
                    act.activation(hpar[:, 1, :], hpar[:, 1, :], ACT.Exp).then_inc(dt_act, 1)
                if n == 4:
                    act.wait_ge(dt_dve, 2)
                    act.activation(dts[:, 4, :], dts[:, 3, :], ACT.Ln).then_inc(dt_act, 1)
                if n >= 8:
                    silu_conv(n - 8)
            project_evac(len(EVEN) - 1)
            for j in range(1, 4):
                silu_conv(j)
            attention(EH, work_e, 0)
            for _ in range(CUT):
                hi()
            for b in range(4):
                act.wait_ge(xs_ps, b + 1)
                act.activation(xs[:, b // 2, 512 * (b % 2):512 * (b % 2) + 512], ps[:, b, :], ACT.Copy).then_inc(xs_sb, 1)
            for h in range(SH):
                act.wait_ge(seg_sb, 2 * h + 2)
                if h >= 2:
                    act.wait_ge(y_ps, h - 1)
                act.activation(decay[:, h % 2, :], tmpd[:, h % 2, :], ACT.Exp).then_inc(dec_sb, 1)
            act.wait_ge(dt_dve, 5)
            act.activation(gss[:, 1, :], gss[:, 0, :], ACT.Sqrt).then_inc(dt_act, 1)
            transposed_hi(1)
            for _ in range(3):
                hi()
            norm_root(0)
            hi()
            transposed_hi(2)

            h_c, a_c, t_c = Tally(), Tally(), Tally()

            def ffn_silu():
                act.wait_ge(h_ps, h_c.up())
                if a_c.started():
                    act.wait_ge(a_dve, a_c.at())
                a_c.up()
                act.activation(s_sb, ps[:, 4, :], ACT.Silu).then_inc(s_act, 1)

            def ffn_hi(first=False):
                act.wait_ge(a_dve, a_c.at())
                if not first:
                    act.wait_ge(w_used, unit.at(1))
                act.activation(aT_hi[:, :], a_sb, ACT.Copy).then_inc(aT_h, 1)

            def turned():
                act.wait_ge(aT_ps, t_c.up())
                act.activation(aT_hi[:, :], ps[:, 2, :], ACT.Copy).then_inc(aT_h, 1)

            hi()
            ffn_silu()
            hi()
            ffn_hi(first=True)
            with rounds(act, (FFN_STEPS - 1) // 2, {unit: 6, h_c: 2, a_c: 2}):
                for _ in range(2):
                    hi()
                    hi()
                    ffn_silu()
                    hi()
                    ffn_hi()
            norm_root(1)
            hi()
            hi()
            transposed_hi(3)

            for n in range(len(ODD)):
                if n:
                    hi()
                    hi()
                    project_evac(len(EVEN) + n - 1)
            project_evac(len(EVEN) + len(ODD) - 1)
            attention(OH, work_o, len(groups(EH)))
            for _ in range(2):
                hi()
            transposed_hi(4)
            hi()
            hi()
            norm_root(2)
            transposed_hi(5)

            act.wait_ge(rt_dve, 1)
            act.activation(l1[:, 5, :], l1[:, 4, :], ACT.Exp).then_inc(rt_act, 1)

            ga_c, yd_c = Tally(), Tally()

            def gathered():
                for b in range(2):
                    act.wait_ge(ga_ps, ga_c.up())
                    act.activation(xg_hi[:, 4 * b:4 * b + 4, :].rearrange("p c j -> p (c j)"), ps[:, 6 + b, :], ACT.Copy).then_inc(xg_h, 1)

            def out_parts():
                act.wait_ge(down_ps, yd_c.up())
                for b in range(2):
                    act.activation(y_hi[:, 512 * b:512 * b + 512], ps[:, 4 + b, :], ACT.Copy, scale=cj[:, 0:1]).then_inc(yh, 1)

            def silu():
                act.wait_ge(h_ps, h_c.up())
                act.wait_ge(a_dve, a_c.at())
                a_c.up()
                h_c.up()
                act.activation(s_sb, ps[:, 0, :], ACT.Silu).then_inc(s_act, 1)

            act.wait_ge(zeroed, 2)
            gathered()
            act.wait_ge(rt_dve, 4)
            n_runs = act.value_load(runs[0:1, 0:1], min_val=NE, max_val=NE * ROUNDS)
            with rounds(act, n_runs, {unit: 42, h_c: 2 * FE_STEPS, a_c: FE_STEPS, t_c: FE_STEPS, ga_c: 2, yd_c: 1}):
                hi()
                hi()
                out_parts()
                hi()
                hi()
                silu()
                hi()
                hi()
                turned()
                with rounds(act, FE_STEPS - 1, {unit: 6, h_c: 2, a_c: 1, t_c: 1}):
                    hi()
                    hi()
                    silu()
                    for _ in range(4):
                        hi()
                    turned()
                gathered()
            out_parts()
            norm_root(3)

        @block.vector
        def _(dve):
            unit = Tally()
            own = Tally()
            own_sem = [dve_seq]

            def mine(ins):
                ins.then_inc(own_sem[0], 1)
                own.up()

            def settle():
                dve.wait_ge(own_sem[0], own.at())

            def lo():
                n = unit.n
                unit.up()
                dve.wait_ge(hi_done, unit.at())
                dve.tensor_tensor(w_lo[:, n % CUT, :], raw[:, n % RAW, :], w_hi[:, n % CUT, :].bitcast(F32), ALU.subtract).then_inc(lo_done, 1)

            def transposed_lo(n):
                hi_t, lo_t = (mT_hi, mT_lo) if len(TR_BANKS[n]) == 6 else (xT_hi, xT_lo)
                for j, b in enumerate(TR_BANKS[n]):
                    dve.wait_ge(tr_hi, TR_BEFORE[n] + j + 1)
                    dve.tensor_tensor(lo_t[:, 2 * j:2 * j + 2, :].rearrange("p c s -> p (c s)"), ps[:, b, :],
                                      hi_t[:, 2 * j:2 * j + 2, :].rearrange("p c s -> p (c s)").bitcast(F32),
                                      ALU.subtract).then_inc(tr_lo, 1)

            def conv(j):
                dve.wait_ge(proj_sb, pieces_by[5 + j])
                for c in range(4 * j, 4 * j + 4):
                    mine(dve.tensor_scalar(cv[:, c, :], xp[:, c, 0:SEQ], pcol[:, c:c + 1], pcol[:, 64 + c:65 + c], ALU.mult, ALU.add))
                for k in range(1, CONV):
                    settle()
                    for c in range(4 * j, 4 * j + 4):
                        ins = dve.scalar_tensor_tensor(out=cv[:, c, :], in0=xp[:, c, k:k + SEQ], scalar=pcol[:, 16 * k + c:16 * k + c + 1],
                                                       in1=cv[:, c, :], op0=ALU.mult, op1=ALU.add)
                        if k == CONV - 1 and c == 4 * j + 3:
                            ins.then_inc(conv_raw, 1)
                        else:
                            mine(ins)

            def attention(heads, work, first, banks):
                pT = work[:, 1024:2048].rearrange("p (b s) -> p b s", b=2)
                gs = groups(heads)

                def maxima(g):
                    t, hs = gs[g]
                    dve.wait_ge(s_ps, first + g + 1)
                    if g >= 2:
                        dve.wait_ge(p_sb, exps[g - 2])
                    mine(dve.tensor_reduce(rmx[:, g % 2, 0:len(hs)], ps[:, g % 2, :].rearrange("p (h s) -> p h s", h=len(hs)), AX_X, ALU.max))
                    settle()
                    dve.tensor_scalar(rneg[:, g % 2, 0:len(hs)], rmx[:, g % 2, 0:len(hs)], -QSCALE, None, ALU.mult).then_inc(neg_max, 1)

                def turned(g):
                    dve.wait_ge(pT_ps, first + g + 1)
                    if g >= 2:
                        dve.wait_ge(pv_ps, first + g - 1)
                    dve.tensor_copy(pT[:, g % 2, :], ps[:, 2 + g % 2, :]).then_inc(pT_sb, 1)

                base = 0 if heads == EH else EXPS_EVEN
                exps, n = [], base
                for t, hs in gs:
                    n += len(hs)
                    exps.append(n)
                maxima(0)
                for g in range(len(gs)):
                    if g + 1 < len(gs):
                        maxima(g + 1)
                    turned(g)
                dve.wait_ge(p_sb, exps[-1])
                mine(dve.reciprocal(rinv[:, :, 0:heads], rsum[:, :, 0:heads]))
                settle()
                dve.wait_ge(pv_ps, first + len(gs))
                mix = mix_e if heads == EH else mix_o
                for t in range(TT):
                    for half in range(heads // 8):
                        dve.tensor_tensor(mix[:, t, 512 * half:512 * half + 512].rearrange("p (h c) -> p h c", h=8),
                                          ps[:, banks + t * (heads // 8) + half, :].rearrange("p (h c) -> p h c", h=8),
                                          rinv[:, t, 8 * half:8 * half + 8].rearrange("p (h o) -> p h o", o=1).to_broadcast([P, 8, HD]),
                                          ALU.mult).then_inc(att_sb, 1)

            def layer_norm(n, parts):
                if n == 3:
                    own_sem[0] = ln_seq
                    own.n, own.loops = 0, []
                for t in range(TT):
                    for half in range(2):
                        cols = slice(512 * half, 512 * half + 512)
                        mine(dve.scalar_tensor_tensor(out=xn[:, t, cols], in0=xn[:, t, cols], scalar=ALPHA, in1=parts(t, half),
                                                      op0=ALU.mult, op1=ALU.add))
                settle()
                for t in range(TT):
                    for half in range(2):
                        mine(dve.bn_stats(stat[:, t, half, :], xn[:, t, 512 * half:512 * half + 512]))
                settle()
                for t in range(TT):
                    mine(dve.bn_aggr(mv[:, t, :], stat[:, t, :, :].rearrange("p a b -> p (a b)")))
                settle()
                dve.tensor_scalar(rstd[:, :, 0], mv[:, :, 1], EPS, None, ALU.add).then_inc(ln_var, 1)
                dve.wait_ge(ln_sd, n + 1)
                mine(dve.reciprocal(rstd[:, :, 2], rstd[:, :, 1]))
                settle()
                for t in range(TT):
                    mine(dve.tensor_scalar(xn[:, t, :], xn[:, t, :], mv[:, t, 0:1], rstd[:, t, 2:3], ALU.subtract, ALU.mult))
                settle()
                dve.wait_ge(par_in, 16 * (3 + 2 * n))
                for t in range(TT):
                    mine(dve.tensor_tensor(xn[:, t, :], xn[:, t, :], gb[:, 0, :], ALU.mult))
                settle()
                for t in range(TT):
                    dve.tensor_tensor(xn[:, t, :], xn[:, t, :], gb[:, 1, :], ALU.add).then_inc(x_new, 1)

            EXPS_EVEN = sum(len(hs) for _, hs in groups(EH))

            def softplus_a():
                dve.wait_ge(dt_ps, 1)
                mine(dve.tensor_tensor(dts[:, 0, :].rearrange("p (t h) -> p t h", t=TT), ps[:, 4, 0:TT * SH].rearrange("p (t h) -> p t h", t=TT),
                                       hpar[:, 0:1, :].to_broadcast([P, TT, SH]), ALU.add))
                settle()
                mine(dve.tensor_scalar(dts[:, 1, :], dts[:, 0, :], -1.0, None, ALU.mult))
                settle()
                dve.tensor_tensor(dts[:, 1, :], dts[:, 0, :], dts[:, 1, :], ALU.min).then_inc(dt_dve, 1)

            def softplus_b():
                dve.wait_ge(dt_act, 2)
                dve.tensor_scalar(dts[:, 3, :], dts[:, 2, :], 1.0, None, ALU.add).then_inc(dt_dve, 1)

            def softplus_c():
                dve.wait_ge(dt_dve, 2)
                mine(dve.tensor_scalar(dts[:, 5, :], dts[:, 3, :], 1.0, None, ALU.subtract))
                settle()
                mine(dve.tensor_scalar(dts[:, 6, :], dts[:, 5, :], 0.0, None, ALU.is_equal))
                mine(dve.tensor_scalar(dts[:, 5, :], dts[:, 5, :], 1e-30, None, ALU.max))
                settle()
                mine(dve.reciprocal(dts[:, 7, :], dts[:, 5, :]))
                mine(dve.tensor_tensor(dts[:, 6, :], dts[:, 6, :], dts[:, 2, :], ALU.mult))
                settle()
                mine(dve.tensor_tensor(dts[:, 7, :], dts[:, 7, :], dts[:, 2, :], ALU.mult))
                settle()
                dve.wait_ge(dt_act, 3)
                mine(dve.tensor_tensor(dts[:, 7, :], dts[:, 7, :], dts[:, 4, :], ALU.mult))
                settle()
                mine(dve.tensor_tensor(dts[:, 7, :], dts[:, 7, :], dts[:, 6, :], ALU.add))
                settle()
                mine(dve.tensor_scalar(dts[:, 0, :], dts[:, 0, :], 0.0, None, ALU.max))
                settle()
                mine(dve.tensor_tensor(dts[:, 0, :], dts[:, 0, :], dts[:, 7, :], ALU.add))
                settle()
                mine(dve.tensor_tensor(dts[:, 1, :].rearrange("p (t h) -> p t h", t=TT), dts[:, 0, :].rearrange("p (t h) -> p t h", t=TT),
                                       hpar[:, 1:2, :].to_broadcast([P, TT, SH]), ALU.mult))
                settle()
                dve.tensor_scalar(dts[:, 1, :], dts[:, 1, :], -1.0, None, ALU.mult).then_inc(dt_dve, 1)


            def small_parts(src, at_hi, at_lo, done):
                dve.tensor_copy(at_hi, src).then_inc(done, 1)
                dve.wait_ge(done, 1)
                dve.tensor_tensor(at_lo, src, at_hi.bitcast(F32), ALU.subtract).then_inc(done, 1)

            transposed_lo(0)
            for n in range(len(EVEN)):
                lo()
                lo()
                if n == 0:
                    dve.wait_ge(con_in, 128)
                    small_parts(w_dt[:, :, :].rearrange("p k h -> p (k h)"), aT_hi[:, 0:KC * SH], aT_lo[:, 0:KC * SH], wdt_cut)
                if n == 2:
                    dve.wait_ge(tab_ps, 1)
                    dve.tensor_copy(tbs, ps[0:OH, 6:8, :]).then_inc(tab_sb, 1)
                    dve.tensor_copy(pcol[:, :], ps[:, 5, 0:80]).then_inc(tab_sb, 1)
                if n == 3:
                    softplus_a()
                if n == 4:
                    softplus_b()
                if n == 5:
                    softplus_c()
                if n >= 7:
                    if n == 7:
                        dve.wait_ge(tab_sb, 2)
                        dve.wait_ge(acs_ps, 1)
                        dve.tensor_copy(acs[:, :, :].rearrange("p t h -> p (t h)"), ps[:, 5, 0:TT * SH]).then_inc(acs_sb, 1)
                    conv(n - 7)
            conv(2)
            conv(3)

            attention(EH, work_e, 0, 6)
            for _ in range(CUT):
                lo()

            dve.wait_ge(acs_sb, 1)

            def per_head(a):
                return a.rearrange("p (h o) -> p h o", o=1).to_broadcast([P, SH, HD])

            for t in range(TT):
                dve.wait_ge(xs_sb, 2 * t + 2)
                dve.tensor_tensor(xdt[:, t, :].rearrange("p (h c) -> p h c", h=SH), xs[:, t, :].rearrange("p (h c) -> p h c", h=SH),
                                  per_head(dts[:, 0, SH * t:SH * t + SH]), ALU.mult).then_inc(xdt_sb, 1)
            dve.wait_ge(xdt_sb, 2)
            for t in range(TT):
                mine(dve.tensor_tensor(xs[:, t, :].rearrange("p (h c) -> p h c", h=SH), xs[:, t, :].rearrange("p (h c) -> p h c", h=SH),
                                       per_head(hpar[:, 2, :]), ALU.mult))

            def differences(h):
                dve.wait_ge(seg_ps, h + 1)
                if h >= 2:
                    dve.wait_ge(dec_sb, h - 1)
                b = 4 + h % 2
                dve.tensor_scalar(tmpd[:, h % 2, 0:256], ps[:, b, 0:256], acs[:, 0, h:h + 1], 0.0, ALU.subtract, ALU.min).then_inc(seg_sb, 1)
                dve.tensor_scalar(tmpd[:, h % 2, 256:384], ps[:, b, 128:256], acs[:, 1, h:h + 1], 0.0, ALU.subtract, ALU.min).then_inc(seg_sb, 1)

            def masked_cb(g):
                dve.wait_ge(cb_ps, g + 1)
                if g >= 2:
                    dve.wait_ge(m_sb, 4 * g - 4)
                b = 6 + g % 2
                dve.tensor_tensor(cbm[:, g % 2, 0:128], ps[:, b, 0:128], upper, ALU.mult).then_inc(cb_sb, 1)
                dve.tensor_copy(cbm[:, g % 2, 128:256], ps[:, b, 128:256]).then_inc(cb_sb, 1)
                dve.tensor_tensor(cbm[:, g % 2, 256:384], ps[:, b, 256:384], upper, ALU.mult).then_inc(cb_sb, 1)

            differences(0)
            for h in range(SH):
                if h % 4 == 0:
                    masked_cb(h // 4)
                if h + 1 < SH:
                    differences(h + 1)
                dve.wait_ge(dec_sb, h + 1)
                dve.wait_ge(cb_sb, 3 * (h // 4) + 3)
                dve.tensor_tensor(decay[:, h % 2, :], decay[:, h % 2, :], cbm[:, (h // 4) % 2, :], ALU.mult).then_inc(m_sb, 1)
            dve.wait_ge(y_ps, SH)
            settle()
            for t in range(TT):
                for half in range(2):
                    cols = slice(512 + 512 * half, 1024 + 512 * half)
                    mine(dve.tensor_tensor(mix_e[:, t, cols], ps[:, 2 * t + half, :], xs[:, t, 512 * half:512 * half + 512], ALU.add))
            settle()
            for t in range(TT):
                mine(dve.tensor_tensor(mix_e[:, t, 512:1536], mix_e[:, t, 512:1536], zs[:, t, :], ALU.mult))
            settle()
            gw = D // SG
            for t in range(TT):
                mine(dve.tensor_tensor(xs[:, t, :], mix_e[:, t, 512:1536], mix_e[:, t, 512:1536], ALU.mult))
            settle()
            mine(dve.tensor_reduce(gss[:, 2, :], xs.rearrange("p t (g c) -> p (t g) c", g=SG), AX_X, ALU.add))
            settle()
            dve.tensor_scalar(gss[:, 0, :], gss[:, 2, :], 1.0 / gw, EPS, ALU.mult, ALU.add).then_inc(dt_dve, 2)
            dve.wait_ge(dt_act, 4)
            mine(dve.reciprocal(gss[:, 2, :], gss[:, 1, :]))
            settle()
            for t in range(TT):
                y = mix_e[:, t, 512:1536].rearrange("p (g c) -> p g c", g=SG)
                mine(dve.tensor_tensor(y, y, gss[:, 2, SG * t:SG * t + SG].rearrange("p (g o) -> p g o", o=1).to_broadcast([P, SG, gw]), ALU.mult))
            settle()
            dve.wait_ge(par_in, 16)
            mine(dve.tensor_tensor(mix_e[:, 0, 512:1536], mix_e[:, 0, 512:1536], normg, ALU.mult))
            mine(dve.tensor_tensor(mix_e[:, 1, 512:1536], mix_e[:, 1, 512:1536], normg, ALU.mult))
            settle()
            dve.tensor_copy(rtm[:, 0, :], rneg[:, 0, :]).then_inc(mix_sb, 1)
            transposed_lo(1)
            for _ in range(3):
                lo()
            dve.wait_ge(wout_ps, 1)
            layer_norm(0, lambda t, half: ps[:, OUT_BANKS[0] + 2 * t + half, :])
            lo()
            transposed_lo(2)

            dve.wait_ge(con_in, 144)
            small_parts(rout[:, :, :].rearrange("p k e -> p (k e)"), r_hi, r_lo, rout_cut)
            h_c, s_c, t_c = Tally(), Tally(), Tally()

            def ffn_gate():
                dve.wait_ge(s_act, s_c.up())
                dve.wait_ge(h_ps, h_c.up())
                dve.tensor_tensor(a_sb, s_sb, ps[:, 5, :], ALU.mult).then_inc(a_dve, 1)

            def act_lo(src):
                dve.wait_ge(aT_h, t_c.up())
                dve.tensor_tensor(aT_lo[:, :], src, aT_hi[:, :].bitcast(F32), ALU.subtract).then_inc(aT_l, 1)

            lo()
            ffn_gate()
            lo()
            act_lo(a_sb)
            with rounds(dve, (FFN_STEPS - 1) // 2, {unit: 6, s_c: 2, h_c: 2, t_c: 2}):
                for _ in range(2):
                    lo()
                    lo()
                    ffn_gate()
                    lo()
                    act_lo(a_sb)
            dve.wait_ge(wout_ps, 2)
            layer_norm(1, lambda t, half: ps[:, OUT_BANKS[1] + 2 * t + half, :])
            lo()
            lo()
            transposed_lo(3)

            for n in range(1, len(ODD)):
                lo()
                lo()
            attention(OH, work_o, len(groups(EH)), 4)
            for _ in range(2):
                lo()
            transposed_lo(4)
            lo()
            lo()
            dve.wait_ge(wout_ps, 3)
            layer_norm(2, lambda t, half: ps[:, OUT_BANKS[2] + 2 * t + half, :])
            transposed_lo(5)

            idx = con[:, C_IDX:C_IDX + NE].rearrange("p (o e) -> p o e", o=1).to_broadcast([P, TT, NE])
            idx8 = con[:, C_IDX8:C_IDX8 + NE].rearrange("p (o e) -> p o e", o=1).to_broadcast([P, TT, NE])

            def L(n):
                return lg[:, n, :].rearrange("p (t e) -> p t e", t=TT)

            def wide(n):
                return l1[:, n, :].rearrange("p (t o) -> p t o", o=1).to_broadcast([P, TT, NE])

            dve.wait_ge(rt_ps, 1)
            mine(dve.tensor_copy(lg[:, 0, :], ps[:, 4, 0:TT * NE]))
            settle()
            for k in range(2):
                mine(dve.tensor_reduce(l1[:, k, :], L(k), AX_X, ALU.max))
                settle()
                mine(dve.tensor_tensor(L(4), L(k), wide(k), ALU.is_equal))
                settle()
                mine(dve.scalar_tensor_tensor(out=L(5), in0=L(4), scalar=-float(NE), in1=idx8, op0=ALU.mult, op1=ALU.add))
                settle()
                mine(dve.tensor_reduce(l1[:, 2 + k, :], L(5), AX_X, ALU.min))
                settle()
                mine(dve.tensor_tensor(L(2 + k), idx, wide(2 + k), ALU.is_equal))
                settle()
                if k == 0:
                    mine(dve.scalar_tensor_tensor(out=L(1), in0=L(2), scalar=-3.0e38, in1=L(0), op0=ALU.mult, op1=ALU.add))
                    settle()
            dve.tensor_tensor(l1[:, 4, :], l1[:, 1, :], l1[:, 0, :], ALU.subtract).then_inc(rt_dve, 1)
            mine(dve.tensor_tensor(L(6), L(2), L(3), ALU.add))
            settle()
            dve.tensor_copy(L(7), L(6)).then_inc(rt_dve, 1)
            dve.wait_ge(rt_act, 1)
            mine(dve.tensor_scalar(l1[:, 6, :], l1[:, 5, :], 1.0, None, ALU.add))
            settle()
            mine(dve.reciprocal(l1[:, 7, :], l1[:, 6, :]))
            settle()
            mine(dve.tensor_tensor(l1[:, 6, :], l1[:, 7, :], l1[:, 5, :], ALU.mult))
            settle()
            mine(dve.tensor_tensor(L(8), L(2), wide(7), ALU.mult))
            mine(dve.tensor_tensor(L(9), L(3), wide(6), ALU.mult))
            settle()
            mine(dve.tensor_tensor(rot[:, :, 2:4].rearrange("p e t -> p t e"), L(8), L(9), ALU.add))
            dve.wait_ge(rt_ps, 2)
            mine(dve.scalar_tensor_tensor(out=lg[:, 1, :], in0=ps[:, 5, 0:TT * NE], scalar=1000.0, in1=lg[:, 7, :], op0=ALU.add, op1=ALU.mult))
            settle()
            mine(dve.tensor_scalar(rot[:, :, 0:2].rearrange("p e t -> p t e"), L(1), 1000.0, None, ALU.subtract))
            settle()
            mine(dve.tensor_reduce(l1[:, 0, 0:1], ps[:, 5, 2 * NE:3 * NE], AX_X, ALU.max))
            settle()
            mine(dve.tensor_scalar(l1[:, 0, 1:2], l1[:, 0, 0:1], P + 0.5, float(NE), ALU.is_gt, ALU.mult))
            settle()
            dve.tensor_copy(rtm[:, 0, 0:2], rot[:, 0, 0:2]).then_inc(rt_dve, 1)
            dve.tensor_scalar(runs[:, :], l1[0:1, 0, 1:2], float(NE), None, ALU.add).then_inc(rt_dve, 1)
            dve.wait_ge(rt_dve, 4)

            def select():
                for t in range(TT):
                    dve.tensor_scalar(Pm[:, t, :], jrow, rot[:, 0, t:t + 1], None, ALU.is_equal).then_inc(pm_sb, 1)

            def turn_round():
                mine(dve.tensor_copy(rtm[:, 0:NE - 1, :], rot[:, 1:NE, :]))
                mine(dve.tensor_scalar(rtm[:, NE - 1, 0:2], rot[:, 0, 0:2], float(P), None, ALU.subtract))
                mine(dve.tensor_copy(rtm[:, NE - 1, 2:4], rot[:, 0, 2:4]))
                settle()
                mine(dve.tensor_copy(rot[:, :, :], rtm[:, :, :]))
                settle()

            ga_c, y_c, sc_c, mt_c, sa_c = Tally(), Tally(), Tally(), Tally(), Tally()

            def gathered():
                for b in range(2):
                    dve.wait_ge(xg_h, ga_c.up())
                    dve.tensor_tensor(xg_lo[:, 4 * b:4 * b + 4, :].rearrange("p c j -> p (c j)"), ps[:, 6 + b, :],
                                      xg_hi[:, 4 * b:4 * b + 4, :].rearrange("p c j -> p (c j)").bitcast(F32), ALU.subtract).then_inc(xg_l, 1)

            def out_parts():
                dve.wait_ge(yh, y_c.up(2))
                for b in range(2):
                    dve.scalar_tensor_tensor(out=y_lo[:, 512 * b:512 * b + 512], in0=ps[:, 4 + b, :], scalar=cj[:, 0:1],
                                             in1=y_hi[:, 512 * b:512 * b + 512].bitcast(F32), op0=ALU.mult, op1=ALU.subtract).then_inc(yl, 1)

            def add_back():
                for t in range(TT):
                    for half in range(2):
                        dve.wait_ge(sc_ps, sc_c.up())
                        a = acc[:, t, 512 * half:512 * half + 512]
                        dve.tensor_tensor(a, a, ps[:, SC_BANKS[2 * t + half], :], ALU.add).then_inc(sc_add, 1)

            def gate():
                dve.wait_ge(s_act, s_c.up())
                dve.wait_ge(h_ps, h_c.up(2))
                dve.tensor_tensor(a_sb, s_sb, ps[:, 1, :], ALU.mult).then_inc(a_dve, 1)

            dve.memset(cj[:, :], 0.0).then_inc(zeroed, 1)
            dve.memset(PmT.bitcast(F32), 0.0).then_inc(zeroed, 1)
            mine(dve.memset(acc, 0.0))
            settle()
            select()
            gathered()
            n_runs = dve.value_load(runs[0:1, 0:1], min_val=NE, max_val=NE * ROUNDS)
            with rounds(dve, n_runs, {unit: 42, s_c: FE_STEPS, h_c: 2 * FE_STEPS, t_c: FE_STEPS, ga_c: 2, y_c: 2, sc_c: 4, mt_c: 1, own: 4}):
                lo()
                lo()
                out_parts()
                lo()
                lo()
                add_back()
                lo()
                gate()
                lo()
                act_lo(ps[:, 2, :])
                dve.wait_ge(pmT_ps, mt_c.up())
                dve.tensor_copy(PmT, ps[:, 3, 0:SEQ]).then_inc(pmT_sb, 1)
                dve.tensor_copy(cj[:, :], ps[:, 3, SEQ:SEQ + 1]).then_inc(pmT_sb, 1)
                turn_round()
                select()
                with rounds(dve, FE_STEPS - 1, {unit: 6, s_c: 1, h_c: 2, t_c: 1}):
                    lo()
                    lo()
                    lo()
                    gate()
                    lo()
                    lo()
                    lo()
                    act_lo(ps[:, 2, :])
                gathered()
            dve.wait_ge(pmT_sb, n_runs * 2)
            out_parts()
            add_back()
            dve.wait_ge(sc_add, n_runs * 4 + 4)
            layer_norm(3, lambda t, half: acc[:, t, 512 * half:512 * half + 512])

        @block.tensor
        def _(pe):
            unit = Tally()

            def arrive():
                slot = unit.n % CUT
                unit.up()
                pe.wait_ge(lo_done, unit.at())
                return slot

            def mm(o, a, b, start=False):
                return pe.matmul(o, a, b, start=start, stop=True, skip_group_check=True)

            def mm3(o, a_hi, a_lo, b_hi, b_lo, start=False):
                mm(o, a_hi, b_hi, start)
                mm(o, a_hi, b_lo)
                return mm(o, a_lo, b_hi)

            def turn_parts(n, src):
                for j, b in enumerate(TR_BANKS[n]):
                    if j >= 4:
                        pe.wait_ge(tr_lo, TR_BEFORE[n] + j - 3)
                    for c in range(2):
                        for t in range(TT):
                            col = (2 * j + c) * P
                            ins = pe.transpose(ps[:, b, c * SEQ + t * P:c * SEQ + t * P + P], src[:, t, col:col + P], ident)
                    ins.then_inc(tr_ps, 1)

            def project(n):
                kind = (EVEN + ODD)[n][0]
                if n >= 2:
                    pe.wait_ge(proj_sb, pieces_by[n - 2])
                b0 = 2 * (n % 2)
                for half in range(2):
                    slot = arrive()
                    w = [a[:, slot, :].rearrange("p (k n) -> p k n", k=4) for a in (w_hi, w_lo)]
                    for j in range(4 if kind in TRANSPOSED else 2):
                        for k in range(4):
                            kc = 4 * half + k
                            if kind in TRANSPOSED:
                                o = ps[:, b0 + j // 2, (j % 2) * SEQ:(j % 2) * SEQ + SEQ]
                                cols = slice(j * P, j * P + P)
                                ins = mm3(o, w[0][:, k, cols], w[1][:, k, cols], xT_hi[:, kc, :], xT_lo[:, kc, :],
                                          start=(kc == 0 and j % 2 == 0))
                            else:
                                toks = slice(j * P, j * P + P)
                                ins = mm3(ps[:, b0 + j, :], xT_hi[:, kc, toks], xT_lo[:, kc, toks], w[0][:, k, :], w[1][:, k, :], start=(kc == 0))
                    ins.then_inc(w_used, 1)
                mm(ps[:, b0, 0:2], zt[:, 0:P], zt[:, 0:2]).then_inc(proj_ps, 1)

            def attention(heads, first, work, banks):
                F = F_e if heads == EH else F_o
                q = qz_e if heads == EH else qz_o
                k = kT_e if heads == EH else kT_o
                v = v_e if heads == EH else v_o
                p = work[:, 0:1024].rearrange("p (b s) -> p b s", b=2)
                pT = work[:, 1024:2048].rearrange("p (b s) -> p b s", b=2)
                gs = groups(heads)
                exps, n = [], 0 if heads == EH else sum(len(hs) for _, hs in groups(EH))
                for t, hs in gs:
                    n += len(hs)
                    exps.append(n)

                def logits(g):
                    t, hs = gs[g]
                    if g >= 2:
                        pe.wait_ge(p_sb, exps[g - 2])
                    w = 512 // len(hs)
                    o = ps[:, g % 2, :]
                    mm(o.rearrange("p (h s) -> p h s", h=len(hs)), rev, F[:, hs[0]:hs[0] + len(hs), SEQ - w:SEQ], start=True)
                    for m, h in enumerate(hs):
                        ins = mm(o[:, m * w:(m + 1) * w], q[:, h, t * P:t * P + P], k[:, h // 2, 0:w])
                    ins.then_inc(s_ps, 1)

                def turn(g):
                    pe.wait_ge(p_sb, exps[g])
                    if g >= 2:
                        pe.wait_ge(pT_sb, first + g - 1)
                    for j in range(4):
                        ins = pe.transpose(ps[:, 2 + g % 2, j * P:j * P + P], p[:, g % 2, j * P:j * P + P], ident)
                    ins.then_inc(pT_ps, 1)

                def values(g):
                    t, hs = gs[g]
                    pe.wait_ge(pT_sb, first + g + 1)
                    for m, h in enumerate(hs):
                        b = banks + t * (heads // 8) + h // 8
                        for kc in range(t + 1):
                            j = m * (t + 1) + kc
                            ins = mm(ps[:, b, (h % 8) * HD:(h % 8) * HD + HD], pT[:, g % 2, j * P:j * P + P],
                                     v[:, kc, h * HD:h * HD + HD], start=(h % 8 == 0 and kc == 0))
                    ins.then_inc(pv_ps, 1)

                logits(0)
                for g in range(len(gs)):
                    if g + 1 < len(gs):
                        logits(g + 1)
                    turn(g)
                    if g:
                        values(g - 1)
                values(len(gs) - 1)

            def project_out(n, chunks, banks):
                for _ in range(chunks // 2):
                    slot = arrive()
                    w = [a[:, slot, :].rearrange("p (k n) -> p k n", k=2) for a in (w_hi, w_lo)]
                    for k in range(2):
                        kc = project_out.kc
                        project_out.kc += 1
                        for t in range(TT):
                            for half in range(2):
                                cols = slice(512 * half, 512 * half + 512)
                                toks = slice(t * P, t * P + P)
                                ins = mm3(ps[:, banks + 2 * t + half, :], mT_hi[:, kc, toks], mT_lo[:, kc, toks], w[0][:, k, cols], w[1][:, k, cols],
                                          start=(kc == 0))
                    ins.then_inc(w_used, 1)
                mm(ps[:, banks, 0:2], zt[:, 0:P], zt[:, 0:2]).then_inc(wout_ps, 1)

            def tables():
                pe.wait_ge(con_in, 128)
                pe.wait_ge(set_up, 2)
                for l in range(2):
                    mm(ps[0:OH, 6 + l, :], rel33[:, :], hot[:, l, :], start=True)
                pe.transpose(ps[:, 5, 0:80], crow, ident[0:80, 0:80]).then_inc(tab_ps, 1)
                pe.wait_ge(wdt_cut, 2)
                w = [a[:, 0:KC * SH].rearrange("p (k h) -> p k h", k=KC) for a in (aT_hi, aT_lo)]
                for t in range(TT):
                    for kc in range(KC):
                        toks = slice(t * P, t * P + P)
                        ins = mm3(ps[:, 4, t * SH:t * SH + SH], xT_hi[:, kc, toks], xT_lo[:, kc, toks], w[0][:, kc, :], w[1][:, kc, :],
                                  start=(t == 0 and kc == 0))
                ins.then_inc(dt_ps, 1)

            def running_sums():
                pe.wait_ge(dt_dve, 3)
                mm(ps[:, 5, 0:SH], upper, dts[:, 1, 0:SH], start=True)
                mm(ps[:, 5, SH:2 * SH], ones, dts[:, 1, 0:SH])
                mm(ps[:, 5, SH:2 * SH], upper, dts[:, 1, SH:2 * SH]).then_inc(acs_ps, 1)

            pe.wait_ge(set_up, 1)
            pe.wait_ge(x_in, 32)
            turn_parts(0, xn)
            pe.wait_ge(tr_lo, TR_BEFORE[1])
            for n in range(len(EVEN)):
                project(n)
                if n == 1:
                    tables()
                if n == 6:
                    running_sums()
            pe.wait_ge(tab_sb, 2)
            pe.wait_ge(set_up, 4)
            pe.wait_ge(proj_sb, pieces_by[len(EVEN) - 1])
            pe.wait_ge(F_in, 16)
            attention(EH, 0, work_e, 6)

            pe.wait_ge(conv_act, 4)
            pe.wait_ge(pT_sb, len(groups(EH)))
            for b in range(4):
                for c in range(4):
                    ins = pe.transpose(ps[:, b, c * P:c * P + P], cv[:, 4 * (b % 2) + c, (b // 2) * P:(b // 2) * P + P], ident)
                ins.then_inc(xs_ps, 1)
            pe.wait_ge(acs_sb, 1)
            pe.wait_ge(att_sb, 2)

            def sums(h):
                if h >= 2:
                    pe.wait_ge(seg_sb, 2 * h - 2)
                b = 4 + h % 2
                mm(ps[:, b, 0:256], dts[:, 1, h:h + 1].to_broadcast([P, P]), upper_ones, start=True)
                mm(ps[:, b, 128:256], dts[:, 1, SH + h:SH + h + 1].to_broadcast([P, P]), upper).then_inc(seg_ps, 1)

            def group_cb(g):
                if g >= 2:
                    pe.wait_ge(cb_sb, 3 * (g - 1))
                B, C = cv[:, 8 + g, :], cv[:, 12 + g, :]
                mm(ps[:, 6 + g % 2, 0:256], B[:, 0:P], C, start=True)
                mm(ps[:, 6 + g % 2, 256:384], B[:, P:SEQ], C[:, P:SEQ]).then_inc(cb_ps, 1)

            group_cb(0)
            sums(0)
            sums(1)
            for h in range(SH):
                if h % 4 == 1 and h // 4 + 1 < SG:
                    group_cb(h // 4 + 1)
                pe.wait_ge(m_sb, h + 1)
                if h == 0:
                    pe.wait_ge(xs_sb, 4)
                    pe.wait_ge(xdt_sb, 2)
                col = (h % 8) * HD
                M = decay[:, h % 2, :]
                xh = [xdt[:, t, h * HD:h * HD + HD] for t in range(TT)]
                mm(ps[:, h // 8, col:col + HD], M[:, 0:P], xh[0], start=(h % 8 == 0))
                mm(ps[:, 2 + h // 8, col:col + HD], M[:, P:2 * P], xh[0], start=(h % 8 == 0))
                mm(ps[:, 2 + h // 8, col:col + HD], M[:, 2 * P:3 * P], xh[1]).then_inc(y_ps, 1)
                if h + 2 < SH:
                    sums(h + 2)

            pe.wait_ge(mix_sb, 1)
            turn_parts(1, mix_e)
            pe.wait_ge(tr_lo, TR_BEFORE[2])
            project_out.kc = 0
            project_out(0, 12, 0)
            pe.wait_ge(x_new, TT)
            turn_parts(2, xn)

            s_c, t_c, a_c = Tally(), Tally(), Tally()
            for b in range(4):
                mm(ps[:, b, :], zt[:, 0:P], zt[:, :], start=True)
            pe.wait_ge(tr_lo, TR_BEFORE[3])

            def ffn_up():
                if a_c.started():
                    pe.wait_ge(a_dve, a_c.at())
                a_c.up()
                for bank in (4, 5):
                    slot = arrive()
                    w = [a[:, slot, :].rearrange("p (k n) -> p k n", k=KC) for a in (w_hi, w_lo)]
                    for j in range(2):
                        cols = slice(j * P, j * P + P)
                        for kc in range(KC):
                            ins = mm3(ps[:, bank, j * SEQ:j * SEQ + SEQ], w[0][:, kc, cols], w[1][:, kc, cols], xT_hi[:, kc, :], xT_lo[:, kc, :],
                                      start=(j == 0 and kc == 0))
                    ins.then_inc(w_used, 1)
                mm(ps[:, 4, 0:2], zt[:, 0:P], zt[:, 0:2]).then_inc(h_ps, 1)

            def ffn_down():
                pe.wait_ge(aT_l, t_c.up())
                slot = arrive()
                w = [a[:, slot, :].rearrange("p (k n) -> p k n", k=2) for a in (w_hi, w_lo)]
                for k in range(2):
                    for t in range(TT):
                        toks = slice(k * SEQ + t * P, k * SEQ + t * P + P)
                        for half in range(2):
                            cols = slice(512 * half, 512 * half + 512)
                            ins = mm3(ps[:, 2 * t + half, :], aT_hi[:, toks], aT_lo[:, toks], w[0][:, k, cols], w[1][:, k, cols])
                ins.then_inc(w_used, 1)

            ffn_up()
            with rounds(pe, (FFN_STEPS - 1) // 2, {unit: 6, t_c: 2, a_c: 2}):
                for _ in range(2):
                    ffn_up()
                    ffn_down()
            ffn_down()
            mm(ps[:, 0, 0:2], zt[:, 0:P], zt[:, 0:2]).then_inc(wout_ps, 1)
            pe.wait_ge(x_new, 2 * TT)
            turn_parts(3, xn)
            pe.wait_ge(tr_lo, TR_BEFORE[4])

            for n in range(len(EVEN), len(EVEN) + len(ODD)):
                project(n)
            pe.wait_ge(proj_sb, pieces_by[-1])
            pe.wait_ge(F_in, 32)
            attention(OH, len(groups(EH)), work_o, 4)
            pe.wait_ge(att_sb, 2 + 4)
            turn_parts(4, mix_o)
            pe.wait_ge(tr_lo, TR_BEFORE[5])
            project_out.kc = 0
            project_out(2, 8, 4)
            pe.wait_ge(x_new, 3 * TT)
            turn_parts(5, xn)
            pe.wait_ge(tr_lo, TR_BEFORE[6])

            pe.wait_ge(rout_cut, 2)
            for t in range(TT):
                for kc in range(KC):
                    toks = slice(t * P, t * P + P)
                    cols = slice(kc * NE, kc * NE + NE)
                    ins = mm3(ps[:, 4, t * NE:t * NE + NE], xT_hi[:, kc, toks], xT_lo[:, kc, toks], r_hi[:, cols], r_lo[:, cols],
                              start=(t == 0 and kc == 0))
            ins.then_inc(rt_ps, 1)
            pe.wait_ge(rt_dve, 2)
            mm(ps[:, 5, 0:NE], strict, lg[:, 7, 0:NE], start=True)
            mm(ps[:, 5, NE:2 * NE], ones, lg[:, 7, 0:NE])
            mm(ps[:, 5, NE:2 * NE], strict, lg[:, 7, NE:2 * NE])
            mm(ps[:, 5, 2 * NE:3 * NE], ones, lg[:, 7, 0:NE])
            mm(ps[:, 5, 2 * NE:3 * NE], ones, lg[:, 7, NE:2 * NE]).then_inc(rt_ps, 1)

            pm_c, xg_c, y_c, pt_c, sa_c, se_c = Tally(), Tally(), Tally(), Tally(), Tally(), Tally()

            def gather():
                pe.wait_ge(pm_sb, pm_c.up(2))
                for b in range(2):
                    for c in range(4):
                        kc = 4 * b + c
                        for t in range(TT):
                            ins = mm(ps[:, 6 + b, c * P:c * P + P], xn[:, t, kc * P:kc * P + P], Pm[:, t, :], start=(t == 0))
                    ins.then_inc(ga_ps, 1)

            def up(bank):
                for half in range(2):
                    slot = arrive()
                    w = [a[:, slot, :].rearrange("p (k n) -> p k n", k=4) for a in (w_hi, w_lo)]
                    for k in range(4):
                        kc = 4 * half + k
                        ins = mm3(ps[:, bank, :], xg_hi[:, kc, :], xg_lo[:, kc, :], w[0][:, k, :], w[1][:, k, :], start=(kc == 0))
                    ins.then_inc(w_used, 1)
                mm(ps[:, bank, 0:2], zt[:, 0:P], zt[:, 0:2]).then_inc(h_ps, 1)

            def turn():
                pe.wait_ge(a_dve, a_c.at())
                for c in range(4):
                    ins = pe.transpose(ps[:, 2, c * P:c * P + P], a_sb[:, c * P:c * P + P], ident)
                ins.then_inc(aT_ps, 1)

            def down():
                pe.wait_ge(aT_l, t_c.up())
                for u in range(2):
                    slot = arrive()
                    w = [a[:, slot, :].rearrange("p (k n) -> p k n", k=2) for a in (w_hi, w_lo)]
                    for k in range(2):
                        rows = slice((2 * u + k) * P, (2 * u + k) * P + P)
                        for half in range(2):
                            cols = slice(512 * half, 512 * half + 512)
                            ins = mm3(ps[:, 4 + half, :], aT_hi[:, rows], aT_lo[:, rows], w[0][:, k, cols], w[1][:, k, cols])
                    ins.then_inc(w_used, 1)

            def scatter():
                pe.wait_ge(yl, y_c.up(2))
                for t in range(TT):
                    for half in range(2):
                        n = 2 * t + half
                        cols = slice(512 * half, 512 * half + 512)
                        mm(ps[:, SC_BANKS[n], :], PmT[:, t * P:t * P + P], y_hi[:, cols], start=True)
                        mm(ps[:, SC_BANKS[n], :], PmT[:, t * P:t * P + P], y_lo[:, cols]).then_inc(sc_ps, 1)
                sa_c.up(4)

            def gate_up(first=False):
                pe.wait_ge(a_dve, a_c.at())
                a_c.up()
                up(0)
                if first:
                    scatter()
                    for b in range(2):
                        mm(ps[:, 4 + b, :], zt[:, 0:P], zt[:, :], start=True)
                up(1)

            pe.wait_ge(rt_dve, 4)
            mm(ps[:, 4, :], zt[:, 0:P], zt[:, :], start=True)
            mm(ps[:, 5, :], zt[:, 0:P], zt[:, :], start=True).then_inc(down_ps, 1)
            gather()
            n_runs = pe.value_load(runs[0:1, 0:1], min_val=NE, max_val=NE * ROUNDS)
            with rounds(pe, n_runs, {unit: 42, pm_c: 2, xg_c: 2, y_c: 2, sa_c: 4, t_c: FE_STEPS, a_c: FE_STEPS, pt_c: 2}):
                pe.wait_ge(xg_l, xg_c.up(2))
                gate_up(first=True)
                pe.wait_ge(sc_add, sa_c.at())
                for t in range(TT):
                    pe.transpose(ps[:, 3, t * P:t * P + P], Pm[:, t, :], ident)
                for t in range(TT):
                    ins = mm(ps[:, 3, SEQ:SEQ + 1], Pm[:, t, :], rot[:, 0, 2 + t:3 + t], start=(t == 0))
                ins.then_inc(pmT_ps, 1)
                turn()
                with rounds(pe, FE_STEPS - 1, {unit: 6, t_c: 1, a_c: 1}):
                    gate_up()
                    down()
                    turn()
                pe.wait_ge(pmT_sb, pt_c.up(2))
                gather()
                down()
                mm(ps[:, 4, 0:2], zt[:, 0:P], zt[:, 0:2]).then_inc(down_ps, 1)
            scatter()


SC_BANKS = [6, 7, 3, 2]

_INS = ["x", "rel_bias", "ln_mix_g", "ln_mix_b", "ln_ffn_g", "ln_ffn_b", "even_w_in", "even_conv_w",
        "even_conv_b", "even_dt_bias", "even_A_log", "even_D", "even_norm_g", "even_w_out",
        "ffn_w_in", "ffn_w_down", "odd_w_qkv", "odd_w_out", "moe_router", "moe_w_in", "moe_w_down"]
_OUTS = [((1, SEQ, D), "float32")]


def kernel(**inputs):
    import numpy as _np
    import concourse.bacc as _bacc
    from concourse import mybir as _mybir
    from concourse.bass_utils import run_bass_kernel_spmd as _run

    nc = _bacc.Bacc("TRN2", target_bir_lowering=False, num_devices=1)
    arrays, args = {}, []
    named = [(n, _np.ascontiguousarray(inputs[n])) for n in _INS]
    named += list(zip(("const", "hot"), shape_constants()))
    for name, a in named:
        arrays[f"in_{name}_dram"] = a
        args.append(nc.dram_tensor(f"in_{name}_dram", a.shape, _mybir.dt.from_np(a.dtype), kind="ExternalInput").ap())
    for i, (shape, dtype) in enumerate(_OUTS):
        args.append(nc.dram_tensor(f"out_{i}_dram", shape, _mybir.dt.from_np(_np.dtype(dtype)), kind="ExternalOutput").ap())
    trunk(nc, *args)
    r = _run(nc, [arrays], core_ids=[0])
    return r.results[0]["out_0_dram"]
```

```python
import math
from contextlib import ExitStack, contextmanager

import numpy as np

import concourse.bass as bass
from concourse import mybir

F32 = mybir.dt.float32
F32R = mybir.dt.float32r
BF16 = mybir.dt.bfloat16
ALU = mybir.AluOpType
ACT = mybir.ActivationFunctionType
AX_X = mybir.AxisListType.X

P = 128
SEQ = 256
D = 1024
TT = SEQ // P
KC = D // P
HD = 64
EH = 8
OH = 16
SH = 16
SG = 4
CONV = 4
XBC_T = 16
FFN = 2816
NE = 8
FE = 3584
BUCKETS = 32
ALPHA = (2.0 * 2) ** 0.25
EPS = 1e-5
QSCALE = HD ** -0.5
MASKED = -1.0e30

RAW = 6
CUT = 3
UNIT = 2048
FFN_STEPS = FFN // 256
FE_STEPS = FE // 512
ROUNDS = SEQ // P

C_ID, C_UP, C_ONE, C_SU, C_JROW, C_REV, C_IDX, C_IDX8 = 0, 128, 256, 384, 512, 640, 768, 776
C_W = 784


def shape_constants():
    c = np.zeros((P, C_W), np.float32)
    i = np.arange(P)
    c[:, C_ID:C_ID + P] = np.eye(P)
    c[:, C_UP:C_UP + P] = i[:, None] <= i[None, :]
    c[:, C_ONE:C_ONE + P] = 1.0
    c[:, C_SU:C_SU + P] = i[:, None] < i[None, :]
    c[:, C_JROW:C_JROW + P] = i[None, :]
    c[:, C_REV:C_REV + P] = i[:, None] + i[None, :] == P - 1
    c[:, C_IDX:C_IDX + NE] = np.arange(NE)
    c[:, C_IDX8:C_IDX8 + NE] = np.arange(NE) + NE
    hot = np.zeros((BUCKETS + 1, 2, 512), np.float32)
    for col in range(2 * SEQ - 1):
        d = SEQ - 1 - col
        if d < 0:
            hot[BUCKETS, :, col] = MASKED
            continue
        half = BUCKETS // 2
        b = d if d < half else min(BUCKETS - 1, half + int(math.log(d / half) / math.log(2048 / half) * half))
        hot[b, :, col] = 1.0 / QSCALE
        seen = (d <= 128) + (d % 4 == 0) + (d % 16 == 0)
        hot[BUCKETS, 1, col] = math.log(seen) / QSCALE if seen else MASKED
    return c, hot


class Tally:

    def __init__(self, n=0):
        self.n = n
        self.loops = []

    def at(self, back=0):
        v = self.n - back
        for i, k in self.loops:
            v = i * k + v
        return v

    def up(self, k=1):
        self.n += k
        return self.at()

    def started(self, back=0):
        return bool(self.loops) or self.n - back > 0


@contextmanager
def rounds(eng, count, steps):
    first = {t: t.n for t in steps}
    with eng.Fori(0, count) as i:
        for t, k in steps.items():
            t.loops.append((i, k))
        yield i
    for t, k in steps.items():
        assert t.n - first[t] == k, (t.n - first[t], k)
        t.loops.pop()
        if isinstance(count, int):
            t.n = first[t] + k * count
        else:
            t.n = first[t]
            t.loops.append((count, k))


def trunk(nc, x, rel_bias, ln_mix_g, ln_mix_b, ln_ffn_g, ln_ffn_b, even_w_in, even_conv_w,
          even_conv_b, even_dt_bias, even_A_log, even_D, even_norm_g, even_w_out,
          ffn_w_in, ffn_w_down, odd_w_qkv, odd_w_out, moe_router, moe_w_in, moe_w_down,
          const_in, hot_in, out):
    with ExitStack() as ctx:
        def sb(name, shape, dt=F32):
            return ctx.enter_context(nc.sbuf_tensor(name, shape, dt))

        def sem(name):
            return ctx.enter_context(nc.semaphore(name))

        raw = sb("raw", [P, RAW, UNIT])
        w_hi = sb("w_hi", [P, CUT, UNIT], F32R)
        w_lo = sb("w_lo", [P, CUT, UNIT], F32R)
        t_hi = sb("t_hi", [P, 12 * SEQ], F32R)
        t_lo = sb("t_lo", [P, 12 * SEQ], F32R)
        aT_hi = sb("aT_hi", [P, 512], F32R)
        aT_lo = sb("aT_lo", [P, 512], F32R)
        xn = sb("xn", [P, TT, D])
        con = sb("con", [P, C_W])
        zt = sb("zt", [P, 512], BF16)
        arena = sb("arena", [P, 17200])
        rel33 = sb("rel33", [BUCKETS + 1, OH])
        pcol = sb("pcol", [P, 80])
        w_dt = sb("w_dt", [P, KC, SH])
        hpar = sb("hpar", [P, 3, SH])
        dts = sb("dts", [P, 8, TT * SH])
        acs = sb("acs", [P, TT, SH])
        rmx = sb("rmx", [P, 2, 4])
        rneg = sb("rneg", [P, 2, 4])
        rsum = sb("rsum", [P, TT, OH])
        rinv = sb("rinv", [P, TT, OH])
        stat = sb("stat", [P, TT, 2, 6])
        mv = sb("mv", [P, TT, 2])
        rstd = sb("rstd", [P, TT, 3])
        gss = sb("gss", [P, 3, TT * SG])
        rout = sb("rout", [P, KC, NE])
        lg = sb("lg", [P, 10, TT * NE])
        l1 = sb("l1", [P, 8, TT])
        rot = sb("rot", [P, NE, 4])
        rtm = sb("rtm", [P, NE, 4])
        cj = sb("cj", [P, 1])
        runs = sb("runs", [1, 1], mybir.dt.int32)

        def area(at, n, **kw):
            return arena[:, at:at + n]

        ident = con[:, C_ID:C_ID + P]
        upper = con[:, C_UP:C_UP + P]
        upper_ones = con[:, C_UP:C_UP + 2 * P]
        ones = con[:, C_ONE:C_ONE + P]
        strict = con[:, C_SU:C_SU + P]
        jrow = con[:, C_JROW:C_JROW + P]
        rev = con[:, C_REV:C_REV + P]

        PADW = SEQ + CONV - 1
        xp = area(0, XBC_T * PADW).rearrange("p (c s) -> p c s", c=XBC_T)
        cv = area(4144, XBC_T * SEQ).rearrange("p (c s) -> p c s", c=XBC_T)
        zs = area(8240, TT * D).rearrange("p (t c) -> p t c", t=TT)
        v_e = area(10288, TT * 512).rearrange("p (t c) -> p t c", t=TT)
        kT_e = area(11312, 4 * SEQ).rearrange("p (c s) -> p c s", c=4)
        F_e = area(12336, EH * SEQ).rearrange("p (h s) -> p h s", h=EH)
        mix_e = area(12336, TT * 1536).rearrange("p (t c) -> p t c", t=TT)
        hot = arena[0:BUCKETS + 1, 12336:12336 + 1024].rearrange("p (l s) -> p l s", l=2)
        crow = arena[0:80, 16432:16560]
        tbs = arena[0:OH, 13360:14384].rearrange("p (l s) -> p l s", l=2)
        qz_e = area(14384, EH * SEQ).rearrange("p (h s) -> p h s", h=EH)
        normg = area(15408, D)
        work_e = area(8240, 2048)
        XP_HALF = 4 * PADW
        xs = [area(XP_HALF * h, TT * 512).rearrange("p (t c) -> p t c", t=TT) for h in range(2)]
        xdt = area(2 * XP_HALF, TT * D).rearrange("p (t c) -> p t c", t=TT)
        decay = area(10288, 4 * 384).rearrange("p (b h s) -> p b h s", b=2, h=2)
        cbm = area(16432, 768).rearrange("p (b s) -> p b s", b=2)
        gb = area(12288, 2 * D).rearrange("p (g c) -> p g c", g=2)
        F_o = area(0, OH * SEQ).rearrange("p (h s) -> p h s", h=OH)
        qz_o = area(4096, OH * SEQ).rearrange("p (h s) -> p h s", h=OH)
        kT_o = area(8192, 8 * SEQ).rearrange("p (c s) -> p c s", c=8)
        v_o = area(10240, TT * D).rearrange("p (t c) -> p t c", t=TT)
        work_o = area(14336, 2048)
        mix_o = area(4096, TT * D).rearrange("p (t c) -> p t c", t=TT)
        a_sb = area(14336, 512)
        s_sb = area(14848, 512)
        acc = area(0, TT * D).rearrange("p (t c) -> p t c", t=TT)
        Pm = area(2048, TT * P).rearrange("p (t j) -> p t j", t=TT)
        y_hi = t_hi[:, 1024:2048]
        y_lo = t_lo[:, 1024:2048]
        PmT = t_hi[:, 2048:2048 + SEQ]
        r_hi = t_hi[:, 2304:2304 + KC * NE]
        r_lo = t_lo[:, 2304:2304 + KC * NE]
        xT_hi = t_hi[:, 0:KC * SEQ].rearrange("p (c s) -> p c s", c=KC)
        xT_lo = t_lo[:, 0:KC * SEQ].rearrange("p (c s) -> p c s", c=KC)
        mT_hi = t_hi[:, :].rearrange("p (c s) -> p c s", c=12)
        mT_lo = t_lo[:, :].rearrange("p (c s) -> p c s", c=12)
        xg_hi = t_hi[:, 0:D].rearrange("p (c j) -> p c j", c=KC)
        xg_lo = t_lo[:, 0:D].rearrange("p (c j) -> p c j", c=KC)

        ps = ctx.enter_context(nc.psum_tensor("ps", [P, 8, 512], F32))
        table = nc.dram_tensor("bias_by_distance", [2, OH, 512], F32, kind="Internal").ap()

        raw_in = [sem(f"raw_in{i}") for i in range(RAW)]
        hi_done = sem("hi_done")
        lo_done = sem("lo_done")
        w_used = sem("w_used")
        con_in = sem("con_in")
        x_in = sem("x_in")
        par_in = sem("par_in")
        set_up = sem("set_up")
        tab_ps = sem("tab_ps")
        tab_sb = sem("tab_sb")
        tab_out = sem("tab_out")
        F_in = sem("F_in")
        tr_ps = sem("tr_ps")
        tr_hi = sem("tr_hi")
        tr_lo = sem("tr_lo")
        proj_ps = sem("proj_ps")
        proj_sb = sem("proj_sb")
        conv_raw = sem("conv_raw")
        conv_act = sem("conv_act")
        wdt_cut = sem("wdt_cut")
        rout_cut = sem("rout_cut")
        dt_ps = sem("dt_ps")
        dt_dve = sem("dt_dve")
        sq_act = sem("sq_act")
        dt_act = sem("dt_act")
        acs_ps = sem("acs_ps")
        acs_sb = sem("acs_sb")
        s_ps = sem("s_ps")
        neg_max = sem("neg_max")
        p_sb = sem("p_sb")
        pT_ps = sem("pT_ps")
        pT_sb = sem("pT_sb")
        pv_ps = sem("pv_ps")
        att_sb = sem("att_sb")
        xs_ps = sem("xs_ps")
        xs_sb = sem("xs_sb")
        xdt_sb = sem("xdt_sb")
        gate_sb = sem("gate_sb")
        cb_ps = sem("cb_ps")
        cb_sb = sem("cb_sb")
        seg_ps = sem("seg_ps")
        seg_sb = sem("seg_sb")
        dec_sb = sem("dec_sb")
        m_sb = sem("m_sb")
        y_ps = sem("y_ps")
        mix_sb = sem("mix_sb")
        wout_ps = sem("wout_ps")
        ln_var = sem("ln_var")
        ln_sd = sem("ln_sd")
        x_new = sem("x_new")
        dve_seq = sem("dve_seq")
        ln_seq = sem("ln_seq")
        h_ps = sem("h_ps")
        s_act = sem("s_act")
        a_dve = sem("a_dve")
        aT_ps = sem("aT_ps")
        aT_h = sem("aT_h")
        aT_l = sem("aT_l")
        rt_ps = sem("rt_ps")
        rt_dve = sem("rt_dve")
        rt_act = sem("rt_act")
        pm_sb = sem("pm_sb")
        ga_ps = sem("ga_ps")
        xg_h = sem("xg_h")
        xg_l = sem("xg_l")
        pmT_ps = sem("pmT_ps")
        pmT_sb = sem("pmT_sb")
        down_ps = sem("down_ps")
        yh = sem("yh")
        yl = sem("yl")
        sc_ps = sem("sc_ps")
        sc_add = sem("sc_add")
        zeroed = sem("zeroed")
        done = sem("done")

        EVEN = [("v", 1024), ("k", 512), ("q", 0), ("x", 3584), ("x", 4096),
                ("x", 2560), ("x", 3072), ("z", 1536), ("z", 2048)]
        CONV_BLOCKS = [2, 3, 0, 1]
        ODD = [("k", 1024), ("k", 1536), ("q", 0), ("q", 512), ("v", 2048), ("v", 2560)]
        PIECES = {"v": 2, "z": 2, "k": 2, "q": 4, "x": 2}
        pieces = [PIECES[k] for k, _ in EVEN + ODD]
        pieces_by = [sum(pieces[:n + 1]) for n in range(len(pieces))]
        TRANSPOSED = "kqx"

        def groups(heads):
            return ([(0, list(range(h, h + 4))) for h in range(0, heads, 4)]
                    + [(1, list(range(h, h + 2))) for h in range(0, heads, 2)])

        TR_BANKS = [[4, 5, 6, 7], [4, 5], [0, 1, 4, 5], [4, 5, 0, 1], [4, 5, 6, 7], [0, 1, 2, 3], [0, 1, 2, 3]]
        TR_BEFORE = [sum(len(b) for b in TR_BANKS[:n]) for n in range(8)]
        TR_CHUNK = [0, 8, 0, 0, 0, 0, 0]
        OUT_BANKS = [[2, 3, 6, 7], [0, 1, 2, 3], [4, 5, 6, 7]]
        Y_BANKS = [[4, 5], [0, 1]]
        SSD_STEPS = {14: [0, 1], 15: [2], 16: [3, 4], 17: [5, 6], 18: [7]}
        UNITS_EVEN = 2 * len(EVEN)
        ATT_FROM = 6
        SSD_FROM = 14

        def bank_of(n):
            return 2 if n in (len(EVEN) - 2, len(EVEN) - 1) else 2 * (n % 2)

        block = ctx.enter_context(nc.Block())

        @block.sync
        def _(sp):
            unit = Tally()

            def load(src, chunks):
                slot = unit.n % RAW
                if unit.started(RAW - 1) and (unit.loops or unit.n >= RAW):
                    sp.wait_ge(lo_done, unit.at(RAW - 1))
                dst = raw[:, slot, :].rearrange("p (k n) -> p k n", k=chunks)
                sp.dma_start(dst, src).then_inc(raw_in[slot], 16)
                unit.up()

            sp.dma_start(con[:, :], const_in[:, :]).then_inc(x_in, 16)
            sp.dma_start(xn[:, :, :], x[0].rearrange("(t p) c -> p t c", p=P)).then_inc(x_in, 16)
            w_in = even_w_in[0].rearrange("(k p) n -> p k n", p=P)
            for _, c0 in EVEN:
                for half in range(2):
                    load(w_in[:, 4 * half:4 * half + 4, c0:c0 + 512], 4)
            w_o = even_w_out[0].rearrange("(k p) n -> p k n", p=P)
            for u in range(6):
                load(w_o[:, 2 * u:2 * u + 2, :], 2)

            f_in = ffn_w_in[0].rearrange("(k p) n -> p k n", p=P)
            f_dn = ffn_w_down[0].rearrange("(k p) n -> p k n", p=P)

            def ffn_in(c):
                load(f_in[:, :, bass.ds(c, 256)], KC)
                load(f_in[:, :, bass.ds(c + FFN, 256)], KC)

            ffn_in(0)
            with rounds(sp, (FFN_STEPS - 1) // 2, {unit: 6}) as i:
                for j in range(2):
                    ffn_in(i * 512 + (j + 1) * 256)
                    load(f_dn[:, bass.ds(i * 4 + j * 2, 2), :], 2)
            load(f_dn[:, 2 * (FFN_STEPS - 1):2 * FFN_STEPS, :], 2)

            w_qkv = odd_w_qkv[0].rearrange("(k p) n -> p k n", p=P)
            for _, c0 in ODD:
                for half in range(2):
                    load(w_qkv[:, 4 * half:4 * half + 4, c0:c0 + 512], 4)
            w_o = odd_w_out[0].rearrange("(k p) n -> p k n", p=P)
            for u in range(4):
                load(w_o[:, 2 * u:2 * u + 2, :], 2)

            e_in = moe_w_in[0].rearrange("e (k p) n -> p e k n", p=P)
            e_dn = moe_w_down[0].rearrange("e (k p) n -> p e k n", p=P)

            def up_block(e, c):
                for half in range(2):
                    load(e_in[:, bass.ds(e, 1), 4 * half:4 * half + 4, bass.ds(c, 512)]
                         .rearrange("p e k n -> p (e k) n"), 4)

            def down_block(e, k):
                for half in range(2):
                    load(e_dn[:, bass.ds(e, 1), bass.ds(k + 2 * half, 2), :]
                         .rearrange("p e k n -> p (e k) n"), 2)

            def all_experts():
                with rounds(sp, NE, {unit: 42}) as e:
                    up_block(e, 0)
                    up_block(e, FE)
                    with rounds(sp, FE_STEPS - 1, {unit: 6}) as f:
                        up_block(e, f * 512 + 512)
                        up_block(e, f * 512 + 512 + FE)
                        down_block(e, f * 4)
                    down_block(e, 4 * (FE_STEPS - 1))

            all_experts()
            sp.wait_ge(rt_dve, 4)
            with sp.If(sp.value_load(runs[0:1, 0:1], min_val=NE, max_val=NE * ROUNDS) > NE):
                all_experts()

            for t in range(TT):
                sp.wait_ge(x_new, 3 * TT + t + 1)
                sp.dma_start(out[0, t * P:t * P + P, :], xn[:, t, :]).then_inc(done, 16)
            sp.wait_ge(done, 16 * TT)

        @block.gpsimd
        def _(pool):
            def everywhere(src, n):
                return bass.AP(src.tensor, src.offset, [[0, P], [1, n]])

            pool.memset(zt[:, :], 0.0).then_inc(set_up, 1)
            pool.memset(rel33[:, :], 1.0).then_inc(set_up, 1)
            pool.wait_ge(set_up, 2)
            pool.dma_start(rel33[0:BUCKETS, :], rel_bias[:, :]).then_inc(con_in, 16)
            pool.dma_start(hot, hot_in[:, :, :]).then_inc(con_in, 16)
            pool.dma_start(crow[0:64, :], even_conv_w[0].rearrange("k (c p) -> (k c) p", p=P)).then_inc(con_in, 16)
            pool.dma_start(crow[64:80, :], even_conv_b[0].rearrange("(c p) -> c p", p=P)).then_inc(con_in, 16)
            pool.dma_start(w_dt[:, :, :], even_w_in[0].rearrange("(k p) n -> p k n", p=P)[:, :, 4608:4624]).then_inc(con_in, 16)
            for n, src in enumerate((even_dt_bias, even_A_log, even_D)):
                pool.dma_start(hpar[:, n, :], everywhere(src[0], SH)).then_inc(con_in, 16)
            pool.memset(qz_e, 0.0).then_inc(set_up, 1)
            pool.memset(xp, 0.0).then_inc(set_up, 1)

            pool.wait_ge(tab_sb, 2)
            pool.dma_start(table.rearrange("l h s -> h l s"), tbs).then_inc(tab_out, 16)
            pool.wait_ge(tab_out, 16)
            pool.dma_start(F_e, bass.AP(table.tensor, table.offset, [[1, P], [512, EH], [1, SEQ]])).then_inc(F_in, 16)
            pool.wait_ge(att_sb, 2)
            pool.dma_start(normg, everywhere(even_norm_g[0], D)).then_inc(par_in, 16)
            pool.wait_ge(mix_sb, 2)
            pool.dma_start(F_o, bass.AP(table.tensor, table.offset + OH * 512, [[1, P], [512, OH], [1, SEQ]])).then_inc(F_in, 16)
            pool.memset(qz_o, 0.0).then_inc(set_up, 1)
            pool.wait_ge(tr_hi, TR_BEFORE[3])
            pool.dma_start(gb[:, 0, :], everywhere(ln_mix_g[0], D)).then_inc(par_in, 16)
            pool.dma_start(gb[:, 1, :], everywhere(ln_mix_b[0], D)).then_inc(par_in, 16)
            pool.dma_start(rout[:, :, :], moe_router[0].rearrange("(k p) e -> p k e", p=P)).then_inc(con_in, 16)
            for n, (g, b) in enumerate(((ln_ffn_g[0], ln_ffn_b[0]), (ln_mix_g[1], ln_mix_b[1]), (ln_ffn_g[1], ln_ffn_b[1]))):
                pool.wait_ge(x_new, TT * (n + 1))
                pool.dma_start(gb[:, 0, :], everywhere(g, D)).then_inc(par_in, 16)
                pool.dma_start(gb[:, 1, :], everywhere(b, D)).then_inc(par_in, 16)

        @block.scalar
        def _(act):
            unit = Tally()

            def hi():
                n = unit.n
                turn = 16 * (n // RAW + 1)
                for i, k in unit.loops:
                    turn = i * (16 * k // RAW) + turn
                act.wait_ge(raw_in[n % RAW], turn)
                if unit.loops or n >= CUT:
                    act.wait_ge(w_used, unit.at(CUT - 1))
                act.activation(w_hi[:, n % CUT, :], raw[:, n % RAW, :], ACT.Copy).then_inc(hi_done, 1)
                unit.up()

            def transposed_hi(n):
                for j, b in enumerate(TR_BANKS[n]):
                    c = TR_CHUNK[n] + 2 * j
                    act.wait_ge(tr_ps, TR_BEFORE[n] + j + 1)
                    act.activation(mT_hi[:, c:c + 2, :].rearrange("p c s -> p (c s)"), ps[:, b, :], ACT.Copy).then_inc(tr_hi, 1)

            def project_evac(n):
                kind, c0 = (EVEN + ODD)[n]
                even = n < len(EVEN)
                act.wait_ge(proj_ps, n + 1)
                for b in range(2):
                    src = ps[:, bank_of(n) + b, :]
                    if kind == "z":
                        act.activation(zs[:, b, c0 - 1536:c0 - 1024], src, ACT.Silu).then_inc(proj_sb, 1)
                    elif kind == "v":
                        at = c0 - (1024 if even else 2048)
                        act.activation((v_e if even else v_o)[:, b, at:at + 512], src, ACT.Copy).then_inc(proj_sb, 1)
                    elif kind == "k":
                        at = (c0 - (512 if even else 1024)) // P + 2 * b
                        act.activation((kT_e if even else kT_o)[:, at:at + 2, :], src.rearrange("p (c s) -> p c s", c=2), ACT.Copy).then_inc(proj_sb, 1)
                    elif kind == "x":
                        at = (c0 - 2560) // P + 2 * b
                        act.activation(xp[:, at:at + 2, CONV - 1:], src.rearrange("p (c s) -> p c s", c=2), ACT.Copy).then_inc(proj_sb, 1)
                    else:
                        if b == 0:
                            act.wait_ge(set_up, 4 if even else 5)
                        h0 = 2 * (c0 // P + 2 * b)
                        q = qz_e if even else qz_o
                        for s in range(2):
                            rows = slice(HD * s, HD * s + HD)
                            act.activation(q[rows, h0 + s:h0 + s + 3:2, :], src[rows, :].rearrange("p (c s) -> p c s", c=2), ACT.Copy).then_inc(proj_sb, 1)

            def silu_conv(i):
                c = 4 * CONV_BLOCKS[i // 2] + 2 * (i % 2)
                act.wait_ge(conv_raw, i + 1)
                act.activation(cv[:, c:c + 2, :], cv[:, c:c + 2, :], ACT.Silu).then_inc(conv_act, 1)

            def attention(heads, work, first, s_banks):
                p = work[:, 0:1024].rearrange("p (b s) -> p b s", b=2)
                gs = groups(heads)

                def exps(g):
                    t, hs = gs[g]
                    act.wait_ge(neg_max, first + g + 1)
                    if g >= 2:
                        act.wait_ge(pT_ps, first + g - 1)
                    w = 512 // len(hs)
                    for m, h in enumerate(hs):
                        act.activation(p[:, g % 2, m * w:(m + 1) * w], ps[:, s_banks[g % len(s_banks)], m * w:(m + 1) * w], ACT.Exp,
                                       bias=rneg[:, g % 2, m:m + 1], scale=QSCALE,
                                       accum_out=rsum[:, t, h:h + 1]).then_inc(p_sb, 1)

                return exps

            def norm_root(n, t):
                act.wait_ge(ln_var, TT * n + t + 1)
                act.activation(rstd[:, t, 1:2], rstd[:, t, 0:1], ACT.Sqrt).then_inc(ln_sd, 1)

            def decays(q):
                act.wait_ge(seg_sb, q + 1)
                act.activation(decay[:, q % 2, :, :], decay[:, q % 2, :, :], ACT.Exp).then_inc(dec_sb, 1)

            transposed_hi(0)
            hi()
            hi()
            exps = attention(EH, work_e, 0, [4])
            for u in range(UNITS_EVEN + 1):
                if u == 16:
                    project_evac(7)
                hi()
                if u % 2 == 0 and 2 <= u and u != 16:
                    if u == 8:
                        act.wait_ge(set_up, 4)
                    project_evac(u // 2 - 1)
                if u == 5:
                    act.wait_ge(dt_dve, 1)
                    act.activation(dts[:, 2, :], dts[:, 1, :], ACT.Exp).then_inc(dt_act, 1)
                    act.activation(hpar[:, 1, :], hpar[:, 1, :], ACT.Exp).then_inc(dt_act, 1)
                if 0 <= u - ATT_FROM < len(groups(EH)):
                    exps(u - ATT_FROM)
                if u == 6:
                    act.wait_ge(dt_dve, 2)
                    act.activation(dts[:, 4, :], dts[:, 3, :], ACT.Ln).then_inc(dt_act, 1)
                if u == SSD_FROM:
                    transposed_hi(1)
                if 9 <= u < 17:
                    silu_conv(u - 9)
                for q in SSD_STEPS.get(u, ()):
                    decays(q)
            for t in range(TT):
                act.wait_ge(gate_sb, t + 1)
                for g in range(SG):
                    act.activation(cv[:, 0, :], mix_e[:, t, 512 + 256 * g:768 + 256 * g], ACT.Square,
                                   accum_out=gss[:, 2, SG * t + g:SG * t + g + 1]).then_inc(sq_act, 1)
                    if (t, g) != (TT - 1, SG - 1):
                        act.wait_ge(sq_act, SG * t + g + 1)
            act.wait_ge(dt_dve, 5)
            act.activation(gss[:, 1, :], gss[:, 0, :], ACT.Sqrt).then_inc(dt_act, 1)
            transposed_hi(2)
            for _ in range(3):
                hi()
            norm_root(0, 0)
            hi()
            hi()
            norm_root(0, 1)
            transposed_hi(3)

            h_c, a_c, t_c = Tally(), Tally(), Tally()

            def ffn_silu():
                act.wait_ge(h_ps, h_c.up())
                if a_c.started():
                    act.wait_ge(a_dve, a_c.at())
                a_c.up()
                act.activation(s_sb, ps[:, 4, :], ACT.Silu).then_inc(s_act, 1)

            def ffn_hi(first=False):
                act.wait_ge(a_dve, a_c.at())
                if not first:
                    act.wait_ge(w_used, unit.at(1))
                act.activation(aT_hi[:, :], a_sb, ACT.Copy).then_inc(aT_h, 1)

            def turned():
                act.wait_ge(aT_ps, t_c.up())
                act.activation(aT_hi[:, :], ps[:, 2, :], ACT.Copy).then_inc(aT_h, 1)

            ffn_silu()
            hi()
            ffn_hi(first=True)
            with rounds(act, (FFN_STEPS - 1) // 2, {unit: 6, h_c: 2, a_c: 2}):
                for _ in range(2):
                    hi()
                    hi()
                    ffn_silu()
                    hi()
                    ffn_hi()
            norm_root(1, 0)
            hi()
            norm_root(1, 1)
            hi()
            transposed_hi(4)

            for n in range(len(ODD)):
                if n:
                    hi()
                    hi()
                    project_evac(len(EVEN) + n - 1)
            project_evac(len(EVEN) + len(ODD) - 1)
            exps = attention(OH, work_o, len(groups(EH)), [0, 1])
            for g in range(len(groups(OH))):
                exps(g)
            for _ in range(2):
                hi()
            transposed_hi(5)
            hi()
            hi()
            norm_root(2, 0)
            norm_root(2, 1)
            transposed_hi(6)

            act.wait_ge(rt_dve, 1)
            act.activation(l1[:, 5, :], l1[:, 4, :], ACT.Exp).then_inc(rt_act, 1)

            ga_c, yd_c = Tally(), Tally()

            def gathered():
                for b in range(2):
                    act.wait_ge(ga_ps, ga_c.up())
                    act.activation(xg_hi[:, 4 * b:4 * b + 4, :].rearrange("p c j -> p (c j)"), ps[:, 6 + b, :], ACT.Copy).then_inc(xg_h, 1)

            def out_parts():
                act.wait_ge(down_ps, yd_c.up())
                for b in range(2):
                    act.activation(y_hi[:, 512 * b:512 * b + 512], ps[:, 4 + b, :], ACT.Copy, scale=cj[:, 0:1]).then_inc(yh, 1)

            def silu():
                act.wait_ge(h_ps, h_c.up())
                act.wait_ge(a_dve, a_c.at())
                a_c.up()
                h_c.up()
                act.activation(s_sb, ps[:, 0, :], ACT.Silu).then_inc(s_act, 1)

            act.wait_ge(zeroed, 2)
            gathered()
            act.wait_ge(rt_dve, 4)
            n_runs = act.value_load(runs[0:1, 0:1], min_val=NE, max_val=NE * ROUNDS)
            with rounds(act, n_runs, {unit: 42, h_c: 2 * FE_STEPS, a_c: FE_STEPS, t_c: FE_STEPS, ga_c: 2, yd_c: 1}):
                hi()
                hi()
                out_parts()
                hi()
                hi()
                silu()
                hi()
                hi()
                turned()
                with rounds(act, FE_STEPS - 1, {unit: 6, h_c: 2, a_c: 1, t_c: 1}):
                    hi()
                    hi()
                    silu()
                    for _ in range(4):
                        hi()
                    turned()
                gathered()
            out_parts()
            norm_root(3, 0)
            norm_root(3, 1)

        @block.vector
        def _(dve):
            unit = Tally()
            own = Tally()
            own_sem = [dve_seq]

            def mine(ins):
                ins.then_inc(own_sem[0], 1)
                own.up()

            def settle():
                dve.wait_ge(own_sem[0], own.at())

            def lo():
                n = unit.n
                unit.up()
                dve.wait_ge(hi_done, unit.at())
                dve.tensor_tensor(w_lo[:, n % CUT, :], raw[:, n % RAW, :], w_hi[:, n % CUT, :].bitcast(F32), ALU.subtract).then_inc(lo_done, 1)

            def transposed_lo(n):
                for j, b in enumerate(TR_BANKS[n]):
                    c = TR_CHUNK[n] + 2 * j
                    dve.wait_ge(tr_hi, TR_BEFORE[n] + j + 1)
                    dve.tensor_tensor(mT_lo[:, c:c + 2, :].rearrange("p c s -> p (c s)"), ps[:, b, :],
                                      mT_hi[:, c:c + 2, :].rearrange("p c s -> p (c s)").bitcast(F32),
                                      ALU.subtract).then_inc(tr_lo, 1)

            def conv(i):
                tiles = [4 * CONV_BLOCKS[i // 2] + 2 * (i % 2) + c for c in range(2)]
                dve.wait_ge(proj_sb, pieces_by[3 + i // 2])
                for c in tiles:
                    mine(dve.tensor_scalar(cv[:, c, :], xp[:, c, 0:SEQ], pcol[:, c:c + 1], pcol[:, 64 + c:65 + c], ALU.mult, ALU.add))
                for k in range(1, CONV):
                    settle()
                    for c in tiles:
                        ins = dve.scalar_tensor_tensor(out=cv[:, c, :], in0=xp[:, c, k:k + SEQ], scalar=pcol[:, 16 * k + c:16 * k + c + 1],
                                                       in1=cv[:, c, :], op0=ALU.mult, op1=ALU.add)
                        if k == CONV - 1 and c == tiles[-1]:
                            ins.then_inc(conv_raw, 1)
                        else:
                            mine(ins)

            def attention(heads, work, first, s_banks, t_banks, banks):
                pT = work[:, 1024:2048].rearrange("p (b s) -> p b s", b=2)
                gs = groups(heads)

                def maxima(g):
                    t, hs = gs[g]
                    dve.wait_ge(s_ps, first + g + 1)
                    if g >= 2:
                        dve.wait_ge(p_sb, exps[g - 2])
                    mine(dve.tensor_reduce(rmx[:, g % 2, 0:len(hs)], ps[:, s_banks[g % len(s_banks)], :].rearrange("p (h s) -> p h s", h=len(hs)), AX_X, ALU.max))
                    settle()
                    dve.tensor_scalar(rneg[:, g % 2, 0:len(hs)], rmx[:, g % 2, 0:len(hs)], -QSCALE, None, ALU.mult).then_inc(neg_max, 1)

                def turned(g):
                    dve.wait_ge(pT_ps, first + g + 1)
                    if g >= 2:
                        dve.wait_ge(pv_ps, first + g - 1)
                    dve.tensor_copy(pT[:, g % 2, :], ps[:, t_banks[g % len(t_banks)], :]).then_inc(pT_sb, 1)

                base = 0 if heads == EH else EXPS_EVEN
                exps, n = [], base
                for t, hs in gs:
                    n += len(hs)
                    exps.append(n)

                def finish():
                    dve.wait_ge(p_sb, exps[-1])
                    mine(dve.reciprocal(rinv[:, :, 0:heads], rsum[:, :, 0:heads]))
                    settle()
                    dve.wait_ge(pv_ps, first + len(gs))
                    mix = mix_e if heads == EH else mix_o
                    for t in range(TT):
                        for half in range(heads // 8):
                            dve.tensor_tensor(mix[:, t, 512 * half:512 * half + 512].rearrange("p (h c) -> p h c", h=8),
                                              ps[:, banks + t * (heads // 8) + half, :].rearrange("p (h c) -> p h c", h=8),
                                              rinv[:, t, 8 * half:8 * half + 8].rearrange("p (h o) -> p h o", o=1).to_broadcast([P, 8, HD]),
                                              ALU.mult).then_inc(att_sb, 1)

                return maxima, turned, finish

            def layer_norm(n, parts, ready, between=None):
                if n == 3:
                    own_sem[0] = ln_seq
                    own.n, own.loops = 0, []
                for t in range(TT):
                    ready(t)
                    for half in range(2):
                        cols = slice(512 * half, 512 * half + 512)
                        mine(dve.scalar_tensor_tensor(out=xn[:, t, cols], in0=xn[:, t, cols], scalar=ALPHA, in1=parts(t, half),
                                                      op0=ALU.mult, op1=ALU.add))
                    settle()
                    for half in range(2):
                        mine(dve.bn_stats(stat[:, t, half, :], xn[:, t, 512 * half:512 * half + 512]))
                    settle()
                    mine(dve.bn_aggr(mv[:, t, :], stat[:, t, :, :].rearrange("p a b -> p (a b)")))
                    settle()
                    dve.tensor_scalar(rstd[:, t, 0:1], mv[:, t, 1:2], EPS, None, ALU.add).then_inc(ln_var, 1)
                    if t == 0:
                        dve.wait_ge(par_in, 16 * (3 + 2 * n))
                    mine(dve.scalar_tensor_tensor(out=xn[:, t, :], in0=xn[:, t, :], scalar=mv[:, t, 0:1], in1=gb[:, 0, :],
                                                  op0=ALU.subtract, op1=ALU.mult))
                    dve.wait_ge(ln_sd, TT * n + t + 1)
                    mine(dve.reciprocal(rstd[:, t, 2:3], rstd[:, t, 1:2]))
                    settle()
                    dve.scalar_tensor_tensor(out=xn[:, t, :], in0=xn[:, t, :], scalar=rstd[:, t, 2:3], in1=gb[:, 1, :],
                                             op0=ALU.mult, op1=ALU.add).then_inc(x_new, 1)
                    if t == 0 and between:
                        between()

            def from_psum(n):
                return (lambda t, half: ps[:, OUT_BANKS[n][2 * t + half], :],
                        lambda t: dve.wait_ge(wout_ps, TT * n + t + 1))

            EXPS_EVEN = sum(len(hs) for _, hs in groups(EH))

            def softplus_a():
                dve.wait_ge(dt_ps, 1)
                mine(dve.tensor_tensor(dts[:, 0, :].rearrange("p (t h) -> p t h", t=TT), ps[:, 4, 0:TT * SH].rearrange("p (t h) -> p t h", t=TT),
                                       hpar[:, 0:1, :].to_broadcast([P, TT, SH]), ALU.add))
                settle()
                mine(dve.tensor_scalar(dts[:, 1, :], dts[:, 0, :], -1.0, None, ALU.mult))
                settle()
                dve.tensor_tensor(dts[:, 1, :], dts[:, 0, :], dts[:, 1, :], ALU.min).then_inc(dt_dve, 1)

            def softplus_b():
                dve.wait_ge(dt_act, 2)
                dve.tensor_scalar(dts[:, 3, :], dts[:, 2, :], 1.0, None, ALU.add).then_inc(dt_dve, 1)

            def softplus_c():
                dve.wait_ge(dt_dve, 2)
                mine(dve.tensor_scalar(dts[:, 5, :], dts[:, 3, :], 1.0, None, ALU.subtract))
                settle()
                mine(dve.tensor_scalar(dts[:, 6, :], dts[:, 5, :], 0.0, None, ALU.is_equal))
                mine(dve.tensor_scalar(dts[:, 5, :], dts[:, 5, :], 1e-30, None, ALU.max))
                settle()
                mine(dve.reciprocal(dts[:, 7, :], dts[:, 5, :]))
                mine(dve.tensor_tensor(dts[:, 6, :], dts[:, 6, :], dts[:, 2, :], ALU.mult))
                settle()
                mine(dve.tensor_tensor(dts[:, 7, :], dts[:, 7, :], dts[:, 2, :], ALU.mult))
                settle()
                dve.wait_ge(dt_act, 3)
                mine(dve.tensor_tensor(dts[:, 7, :], dts[:, 7, :], dts[:, 4, :], ALU.mult))
                settle()
                mine(dve.tensor_tensor(dts[:, 7, :], dts[:, 7, :], dts[:, 6, :], ALU.add))
                settle()
                mine(dve.tensor_scalar(dts[:, 0, :], dts[:, 0, :], 0.0, None, ALU.max))
                settle()
                mine(dve.tensor_tensor(dts[:, 0, :], dts[:, 0, :], dts[:, 7, :], ALU.add))
                settle()
                mine(dve.tensor_tensor(dts[:, 1, :].rearrange("p (t h) -> p t h", t=TT), dts[:, 0, :].rearrange("p (t h) -> p t h", t=TT),
                                       hpar[:, 1:2, :].to_broadcast([P, TT, SH]), ALU.mult))
                settle()
                dve.tensor_scalar(dts[:, 1, :], dts[:, 1, :], -1.0, None, ALU.mult).then_inc(dt_dve, 1)


            def small_parts(src, at_hi, at_lo, done):
                dve.tensor_copy(at_hi, src).then_inc(done, 1)
                dve.wait_ge(done, 1)
                dve.tensor_tensor(at_lo, src, at_hi.bitcast(F32), ALU.subtract).then_inc(done, 1)

            def half_heads(a):
                return a.rearrange("p (h o) -> p h o", o=1).to_broadcast([P, SH // 2, HD])

            def x_rows(half):
                dve.wait_ge(xs_ps, half + 1)
                for t in range(TT):
                    src = ps[:, Y_BANKS[half][t], :].rearrange("p (h c) -> p h c", h=SH // 2)
                    h0 = SH * t + SH // 2 * half
                    dve.tensor_tensor(xdt[:, t, 512 * half:512 * half + 512].rearrange("p (h c) -> p h c", h=SH // 2), src,
                                      half_heads(dts[:, 0, h0:h0 + SH // 2]), ALU.mult).then_inc(xdt_sb, 1)
                    dve.tensor_tensor(xs[half][:, t, :].rearrange("p (h c) -> p h c", h=SH // 2), src,
                                      half_heads(hpar[:, 2, SH // 2 * half:SH // 2 * half + SH // 2]), ALU.mult).then_inc(xs_sb, 1)

            def differences(q):
                dve.wait_ge(seg_ps, q + 1)
                if q >= 2:
                    dve.wait_ge(y_ps, q - 1)
                for m in range(2):
                    h = 2 * q + m
                    mine(dve.tensor_scalar(decay[:, q % 2, m, 0:256], ps[:, 6, 256 * m:256 * m + 256], acs[:, 0, h:h + 1], 0.0, ALU.subtract, ALU.min))
                    ins = dve.tensor_scalar(decay[:, q % 2, m, 256:384], ps[:, 6, 256 * m + 128:256 * m + 256], acs[:, 1, h:h + 1], 0.0, ALU.subtract, ALU.min)
                    if m == 1:
                        ins.then_inc(seg_sb, 1)
                    else:
                        mine(ins)

            def masked_cb(g):
                dve.wait_ge(cb_ps, g + 1)
                if g >= 2:
                    dve.wait_ge(m_sb, 2 * g - 2)
                dve.tensor_tensor(cbm[:, g % 2, 0:128], ps[:, 7, 0:128], upper, ALU.mult).then_inc(cb_sb, 1)
                dve.tensor_copy(cbm[:, g % 2, 128:256], ps[:, 7, 128:256]).then_inc(cb_sb, 1)
                dve.tensor_tensor(cbm[:, g % 2, 256:384], ps[:, 7, 256:384], upper, ALU.mult).then_inc(cb_sb, 1)

            def times_cb(q):
                dve.wait_ge(dec_sb, q + 1)
                dve.wait_ge(cb_sb, 3 * (q // 2) + 3)
                dve.tensor_tensor(decay[:, q % 2, :, :], decay[:, q % 2, :, :], cbm[:, (q // 2) % 2:(q // 2) % 2 + 1, :].to_broadcast([P, 2, 384]),
                                  ALU.mult).then_inc(m_sb, 1)

            transposed_lo(0)
            lo()
            lo()
            maxima, turned, finish = attention(EH, work_e, 0, [4], [5], 6)
            n_groups = len(groups(EH))
            for u in range(UNITS_EVEN + 1):
                s = u - ATT_FROM
                if u == 4:
                    dve.wait_ge(tab_ps, 1)
                    dve.tensor_copy(tbs, ps[0:OH, 6:8, :]).then_inc(tab_sb, 1)
                    dve.tensor_copy(pcol[:, :], ps[:, 5, 0:80]).then_inc(tab_sb, 1)
                if u == SSD_FROM - 1:
                    dve.wait_ge(acs_ps, 1)
                    dve.tensor_copy(acs[:, :, :].rearrange("p t h -> p (t h)"), ps[:, 5, 0:TT * SH]).then_inc(acs_sb, 1)
                    finish()
                if 0 <= s < n_groups:
                    maxima(s)
                if 1 <= s <= n_groups:
                    turned(s - 1)
                if u == 14:
                    dve.wait_ge(acs_sb, 1)
                    differences(0)
                    masked_cb(0)
                    transposed_lo(1)
                    lo()
                    times_cb(0)
                    differences(1)
                elif u == 15:
                    times_cb(1)
                    x_rows(0)
                    lo()
                elif u == 16:
                    times_cb(2)
                    differences(3)
                    lo()
                    times_cb(3)
                    differences(4)
                    masked_cb(2)
                    x_rows(1)
                elif u == 17:
                    times_cb(4)
                    differences(5)
                    lo()
                    times_cb(5)
                    masked_cb(3)
                    differences(6)
                elif u == 18:
                    times_cb(6)
                    differences(7)
                    lo()
                    times_cb(7)
                else:
                    lo()
                if 8 <= u < 16:
                    if u == 8:
                        dve.wait_ge(tab_sb, 2)
                    conv(u - 8)
                if u == 15:
                    differences(2)
                    masked_cb(1)
                if u == 0:
                    dve.wait_ge(con_in, 128)
                    small_parts(w_dt[:, :, :].rearrange("p k h -> p (k h)"), aT_hi[:, 0:KC * SH], aT_lo[:, 0:KC * SH], wdt_cut)
                if u == 5:
                    softplus_a()
                if u == 6:
                    softplus_b()
                if u == 7:
                    softplus_c()

            dve.wait_ge(xs_sb, 4)
            dve.wait_ge(y_ps, SH // 2)
            dve.wait_ge(proj_sb, pieces_by[len(EVEN) - 1])
            for t in range(TT):
                for half in range(2):
                    mine(dve.tensor_tensor(mix_e[:, t, 512 + 512 * half:1024 + 512 * half], ps[:, Y_BANKS[half][t], :], xs[half][:, t, :], ALU.add))
                settle()
                dve.tensor_tensor(mix_e[:, t, 512:1536], mix_e[:, t, 512:1536], zs[:, t, :], ALU.mult).then_inc(gate_sb, 1)
            gw = D // SG
            dve.wait_ge(sq_act, TT * SG)
            dve.tensor_scalar(gss[:, 0, :], gss[:, 2, :], 1.0 / gw, EPS, ALU.mult, ALU.add).then_inc(dt_dve, 2)
            dve.wait_ge(dt_act, 4)
            mine(dve.reciprocal(gss[:, 2, :], gss[:, 1, :]))
            settle()
            dve.wait_ge(par_in, 16)
            dve.wait_ge(gate_sb, TT)
            for t in range(TT):
                for g in range(SG):
                    y = mix_e[:, t, 512 + gw * g:512 + gw * g + gw]
                    ins = dve.scalar_tensor_tensor(out=y, in0=y, scalar=gss[:, 2, SG * t + g:SG * t + g + 1], in1=normg[:, gw * g:gw * g + gw],
                                                   op0=ALU.mult, op1=ALU.mult)
                    if g == SG - 1:
                        ins.then_inc(mix_sb, 1)
                    else:
                        mine(ins)
            transposed_lo(2)
            for _ in range(3):
                lo()
            layer_norm(0, *from_psum(0), between=lo)
            transposed_lo(3)

            dve.wait_ge(con_in, 144)
            small_parts(rout[:, :, :].rearrange("p k e -> p (k e)"), r_hi, r_lo, rout_cut)
            h_c, s_c, t_c = Tally(), Tally(), Tally()

            def ffn_gate():
                dve.wait_ge(s_act, s_c.up())
                dve.wait_ge(h_ps, h_c.up())
                dve.tensor_tensor(a_sb, s_sb, ps[:, 5, :], ALU.mult).then_inc(a_dve, 1)

            def act_lo(src):
                dve.wait_ge(aT_h, t_c.up())
                dve.tensor_tensor(aT_lo[:, :], src, aT_hi[:, :].bitcast(F32), ALU.subtract).then_inc(aT_l, 1)

            lo()
            ffn_gate()
            lo()
            act_lo(a_sb)
            with rounds(dve, (FFN_STEPS - 1) // 2, {unit: 6, s_c: 2, h_c: 2, t_c: 2}):
                for _ in range(2):
                    lo()
                    lo()
                    ffn_gate()
                    lo()
                    act_lo(a_sb)
            layer_norm(1, *from_psum(1), between=lo)
            transposed_lo(4)

            for n in range(len(ODD)):
                if n:
                    lo()
                lo()
            maxima, turned, finish = attention(OH, work_o, len(groups(EH)), [0, 1], [2, 3], 4)
            maxima(0)
            for g in range(len(groups(OH))):
                if g + 1 < len(groups(OH)):
                    maxima(g + 1)
                turned(g)
            finish()
            for _ in range(2):
                lo()
            transposed_lo(5)
            lo()
            lo()
            layer_norm(2, *from_psum(2))
            transposed_lo(6)

            idx = con[:, C_IDX:C_IDX + NE].rearrange("p (o e) -> p o e", o=1).to_broadcast([P, TT, NE])
            idx8 = con[:, C_IDX8:C_IDX8 + NE].rearrange("p (o e) -> p o e", o=1).to_broadcast([P, TT, NE])

            def L(n):
                return lg[:, n, :].rearrange("p (t e) -> p t e", t=TT)

            def wide(n):
                return l1[:, n, :].rearrange("p (t o) -> p t o", o=1).to_broadcast([P, TT, NE])

            dve.wait_ge(rt_ps, 1)
            mine(dve.tensor_copy(lg[:, 0, :], ps[:, 4, 0:TT * NE]))
            settle()
            for k in range(2):
                mine(dve.tensor_reduce(l1[:, k, :], L(k), AX_X, ALU.max))
                settle()
                mine(dve.tensor_tensor(L(4), L(k), wide(k), ALU.is_equal))
                settle()
                mine(dve.scalar_tensor_tensor(out=L(5), in0=L(4), scalar=-float(NE), in1=idx8, op0=ALU.mult, op1=ALU.add))
                settle()
                mine(dve.tensor_reduce(l1[:, 2 + k, :], L(5), AX_X, ALU.min))
                settle()
                mine(dve.tensor_tensor(L(2 + k), idx, wide(2 + k), ALU.is_equal))
                settle()
                if k == 0:
                    mine(dve.scalar_tensor_tensor(out=L(1), in0=L(2), scalar=-3.0e38, in1=L(0), op0=ALU.mult, op1=ALU.add))
                    settle()
            dve.tensor_tensor(l1[:, 4, :], l1[:, 1, :], l1[:, 0, :], ALU.subtract).then_inc(rt_dve, 1)
            mine(dve.tensor_tensor(L(6), L(2), L(3), ALU.add))
            settle()
            dve.tensor_copy(L(7), L(6)).then_inc(rt_dve, 1)
            dve.wait_ge(rt_act, 1)
            mine(dve.tensor_scalar(l1[:, 6, :], l1[:, 5, :], 1.0, None, ALU.add))
            settle()
            mine(dve.reciprocal(l1[:, 7, :], l1[:, 6, :]))
            settle()
            mine(dve.tensor_tensor(l1[:, 6, :], l1[:, 7, :], l1[:, 5, :], ALU.mult))
            settle()
            mine(dve.tensor_tensor(L(8), L(2), wide(7), ALU.mult))
            mine(dve.tensor_tensor(L(9), L(3), wide(6), ALU.mult))
            settle()
            mine(dve.tensor_tensor(rot[:, :, 2:4].rearrange("p e t -> p t e"), L(8), L(9), ALU.add))
            dve.wait_ge(rt_ps, 2)
            mine(dve.scalar_tensor_tensor(out=lg[:, 1, :], in0=ps[:, 5, 0:TT * NE], scalar=1000.0, in1=lg[:, 7, :], op0=ALU.add, op1=ALU.mult))
            settle()
            mine(dve.tensor_scalar(rot[:, :, 0:2].rearrange("p e t -> p t e"), L(1), 1000.0, None, ALU.subtract))
            settle()
            mine(dve.tensor_reduce(l1[:, 0, 0:1], ps[:, 5, 2 * NE:3 * NE], AX_X, ALU.max))
            settle()
            mine(dve.tensor_scalar(l1[:, 0, 1:2], l1[:, 0, 0:1], P + 0.5, float(NE), ALU.is_gt, ALU.mult))
            settle()
            dve.tensor_copy(rtm[:, 0, 0:2], rot[:, 0, 0:2]).then_inc(rt_dve, 1)
            dve.tensor_scalar(runs[:, :], l1[0:1, 0, 1:2], float(NE), None, ALU.add).then_inc(rt_dve, 1)
            dve.wait_ge(rt_dve, 4)

            def select():
                for t in range(TT):
                    dve.tensor_scalar(Pm[:, t, :], jrow, rot[:, 0, t:t + 1], None, ALU.is_equal).then_inc(pm_sb, 1)

            def turn_round():
                mine(dve.tensor_copy(rtm[:, 0:NE - 1, :], rot[:, 1:NE, :]))
                mine(dve.tensor_scalar(rtm[:, NE - 1, 0:2], rot[:, 0, 0:2], float(P), None, ALU.subtract))
                mine(dve.tensor_copy(rtm[:, NE - 1, 2:4], rot[:, 0, 2:4]))
                settle()
                mine(dve.tensor_copy(rot[:, :, :], rtm[:, :, :]))
                settle()

            ga_c, y_c, sc_c, mt_c, sa_c = Tally(), Tally(), Tally(), Tally(), Tally()

            def gathered():
                for b in range(2):
                    dve.wait_ge(xg_h, ga_c.up())
                    dve.tensor_tensor(xg_lo[:, 4 * b:4 * b + 4, :].rearrange("p c j -> p (c j)"), ps[:, 6 + b, :],
                                      xg_hi[:, 4 * b:4 * b + 4, :].rearrange("p c j -> p (c j)").bitcast(F32), ALU.subtract).then_inc(xg_l, 1)

            def out_parts():
                dve.wait_ge(yh, y_c.up(2))
                for b in range(2):
                    dve.scalar_tensor_tensor(out=y_lo[:, 512 * b:512 * b + 512], in0=ps[:, 4 + b, :], scalar=cj[:, 0:1],
                                             in1=y_hi[:, 512 * b:512 * b + 512].bitcast(F32), op0=ALU.mult, op1=ALU.subtract).then_inc(yl, 1)

            def add_back(tiles=range(TT)):
                for t in tiles:
                    for half in range(2):
                        dve.wait_ge(sc_ps, sc_c.up())
                        a = acc[:, t, 512 * half:512 * half + 512]
                        dve.tensor_tensor(a, a, ps[:, SC_BANKS[2 * t + half], :], ALU.add).then_inc(sc_add, 1)

            def gate():
                dve.wait_ge(s_act, s_c.up())
                dve.wait_ge(h_ps, h_c.up(2))
                dve.tensor_tensor(a_sb, s_sb, ps[:, 1, :], ALU.mult).then_inc(a_dve, 1)

            dve.memset(cj[:, :], 0.0).then_inc(zeroed, 1)
            dve.memset(PmT.bitcast(F32), 0.0).then_inc(zeroed, 1)
            mine(dve.memset(acc, 0.0))
            settle()
            select()
            gathered()
            n_runs = dve.value_load(runs[0:1, 0:1], min_val=NE, max_val=NE * ROUNDS)
            with rounds(dve, n_runs, {unit: 42, s_c: FE_STEPS, h_c: 2 * FE_STEPS, t_c: FE_STEPS, ga_c: 2, y_c: 2, sc_c: 4, mt_c: 1, own: 4}):
                lo()
                lo()
                out_parts()
                lo()
                lo()
                add_back()
                lo()
                gate()
                lo()
                act_lo(ps[:, 2, :])
                dve.wait_ge(pmT_ps, mt_c.up())
                dve.tensor_copy(PmT, ps[:, 3, 0:SEQ]).then_inc(pmT_sb, 1)
                dve.tensor_copy(cj[:, :], ps[:, 3, SEQ:SEQ + 1]).then_inc(pmT_sb, 1)
                turn_round()
                select()
                with rounds(dve, FE_STEPS - 1, {unit: 6, s_c: 1, h_c: 2, t_c: 1}):
                    lo()
                    lo()
                    lo()
                    gate()
                    lo()
                    lo()
                    lo()
                    act_lo(ps[:, 2, :])
                gathered()
            dve.wait_ge(pmT_sb, n_runs * 2)
            out_parts()

            def last_ready(t):
                add_back([t])
                dve.wait_ge(sc_add, n_runs * 4 + 2 * t + 2)

            layer_norm(3, lambda t, half: acc[:, t, 512 * half:512 * half + 512], last_ready)

        @block.tensor
        def _(pe):
            unit = Tally()

            def arrive():
                slot = unit.n % CUT
                unit.up()
                pe.wait_ge(lo_done, unit.at())
                return slot

            def mm(o, a, b, start=False):
                return pe.matmul(o, a, b, start=start, stop=True, skip_group_check=True)

            def mm3(o, a_hi, a_lo, b_hi, b_lo, start=False):
                mm(o, a_hi, b_hi, start)
                mm(o, a_hi, b_lo)
                return mm(o, a_lo, b_hi)

            def turn_x(n, after):
                turn_parts(n, xn, ready=lambda t: pe.wait_ge(x_new, after + t + 1))

            def parts_ready(n, kc):
                if kc % 2 == 0:
                    pe.wait_ge(tr_lo, TR_BEFORE[n] + kc // 2 + 1)

            def turn_parts(n, src, col0=0, ready=None):
                for t in range(TT):
                    if ready:
                        ready(t)
                    for j, b in enumerate(TR_BANKS[n]):
                        for c in range(2):
                            col = col0 + (2 * j + c) * P
                            ins = pe.transpose(ps[:, b, c * SEQ + t * P:c * SEQ + t * P + P], src[:, t, col:col + P], ident)
                        if t == TT - 1:
                            ins.then_inc(tr_ps, 1)

            def project(n, fresh=None, before=None):
                kind = (EVEN + ODD)[n][0]
                b0 = bank_of(n)
                for half in range(2):
                    for j in range(4 if kind in TRANSPOSED else 2):
                        if before:
                            before(2 * n + half, j)
                        if j == 0:
                            if half == 0 and n >= 2:
                                pe.wait_ge(proj_sb, pieces_by[n - 1 if bank_of(n - 1) == b0 else n - 2])
                            slot = arrive()
                            w = [a[:, slot, :].rearrange("p (k n) -> p k n", k=4) for a in (w_hi, w_lo)]
                        for k in range(4):
                            kc = 4 * half + k
                            if fresh is not None and j == 0:
                                parts_ready(fresh, kc)
                            if kind in TRANSPOSED:
                                o = ps[:, b0 + j // 2, (j % 2) * SEQ:(j % 2) * SEQ + SEQ]
                                cols = slice(j * P, j * P + P)
                                ins = mm3(o, w[0][:, k, cols], w[1][:, k, cols], xT_hi[:, kc, :], xT_lo[:, kc, :],
                                          start=(kc == 0 and j % 2 == 0))
                            else:
                                toks = slice(j * P, j * P + P)
                                ins = mm3(ps[:, b0 + j, :], xT_hi[:, kc, toks], xT_lo[:, kc, toks], w[0][:, k, :], w[1][:, k, :], start=(kc == 0))
                    ins.then_inc(w_used, 1)
                mm(ps[:, b0, 0:2], zt[:, 0:P], zt[:, 0:2]).then_inc(proj_ps, 1)

            def attention(heads, first, work, s_banks, t_banks, banks):
                F = F_e if heads == EH else F_o
                q = qz_e if heads == EH else qz_o
                k = kT_e if heads == EH else kT_o
                v = v_e if heads == EH else v_o
                p = work[:, 0:1024].rearrange("p (b s) -> p b s", b=2)
                pT = work[:, 1024:2048].rearrange("p (b s) -> p b s", b=2)
                gs = groups(heads)
                exps, n = [], 0 if heads == EH else sum(len(hs) for _, hs in groups(EH))
                for t, hs in gs:
                    n += len(hs)
                    exps.append(n)

                def logits(g):
                    t, hs = gs[g]
                    if g >= len(s_banks):
                        pe.wait_ge(p_sb, exps[g - len(s_banks)])
                    w = 512 // len(hs)
                    o = ps[:, s_banks[g % len(s_banks)], :]
                    mm(o.rearrange("p (h s) -> p h s", h=len(hs)), rev, F[:, hs[0]:hs[0] + len(hs), SEQ - w:SEQ], start=True)
                    for m, h in enumerate(hs):
                        ins = mm(o[:, m * w:(m + 1) * w], q[:, h, t * P:t * P + P], k[:, h // 2, 0:w])
                    ins.then_inc(s_ps, 1)

                def turn(g):
                    pe.wait_ge(p_sb, exps[g])
                    if g >= len(t_banks):
                        pe.wait_ge(pT_sb, first + g - len(t_banks) + 1)
                    for j in range(4):
                        ins = pe.transpose(ps[:, t_banks[g % len(t_banks)], j * P:j * P + P], p[:, g % 2, j * P:j * P + P], ident)
                    ins.then_inc(pT_ps, 1)

                def values(g):
                    t, hs = gs[g]
                    pe.wait_ge(pT_sb, first + g + 1)
                    for m, h in enumerate(hs):
                        b = banks + t * (heads // 8) + h // 8
                        for kc in range(t + 1):
                            j = m * (t + 1) + kc
                            ins = mm(ps[:, b, (h % 8) * HD:(h % 8) * HD + HD], pT[:, g % 2, j * P:j * P + P],
                                     v[:, kc, h * HD:h * HD + HD], start=(h % 8 == 0 and kc == 0))
                    ins.then_inc(pv_ps, 1)

                return logits, turn, values

            def out_products(m, n, slot, u, t, before=0):
                w = [a[:, slot, :].rearrange("p (k n) -> p k n", k=2) for a in (w_hi, w_lo)]
                toks = slice(t * P, t * P + P)
                for k in range(2):
                    kc = 2 * u + k
                    if t == 0:
                        parts_ready(n, kc - before)
                    c = TR_CHUNK[n] + kc - before
                    for half in range(2):
                        cols = slice(512 * half, 512 * half + 512)
                        ins = mm3(ps[:, OUT_BANKS[m][2 * t + half], :], mT_hi[:, c, toks], mT_lo[:, c, toks], w[0][:, k, cols], w[1][:, k, cols],
                                  start=(kc == 0))
                return ins

            def project_out(m, n, units, before=0):
                for u in units[:-CUT]:
                    slot = arrive()
                    for t in range(TT):
                        ins = out_products(m, n, slot, u, t, before)
                    ins.then_inc(w_used, 1)
                held = []
                for u in units[-CUT:]:
                    held.append(arrive())
                    ins = out_products(m, n, held[-1], u, 0, before)
                ins.then_inc(wout_ps, 1)
                for slot, u in zip(held, units[-CUT:]):
                    out_products(m, n, slot, u, 1, before).then_inc(w_used, 1)
                mm(ps[:, OUT_BANKS[m][2], 0:2], zt[:, 0:P], zt[:, 0:2]).then_inc(wout_ps, 1)

            def tables():
                pe.wait_ge(con_in, 128)
                pe.wait_ge(set_up, 2)
                for l in range(2):
                    mm(ps[0:OH, 6 + l, :], rel33[:, :], hot[:, l, :], start=True)
                pe.transpose(ps[:, 5, 0:80], crow, ident[0:80, 0:80]).then_inc(tab_ps, 1)
                pe.wait_ge(wdt_cut, 2)
                w = [a[:, 0:KC * SH].rearrange("p (k h) -> p k h", k=KC) for a in (aT_hi, aT_lo)]
                for t in range(TT):
                    for kc in range(KC):
                        toks = slice(t * P, t * P + P)
                        ins = mm3(ps[:, 4, t * SH:t * SH + SH], xT_hi[:, kc, toks], xT_lo[:, kc, toks], w[0][:, kc, :], w[1][:, kc, :],
                                  start=(t == 0 and kc == 0))
                ins.then_inc(dt_ps, 1)

            def running_sums():
                pe.wait_ge(dt_dve, 3)
                mm(ps[:, 5, 0:SH], upper, dts[:, 1, 0:SH], start=True)
                mm(ps[:, 5, SH:2 * SH], ones, dts[:, 1, 0:SH])
                mm(ps[:, 5, SH:2 * SH], upper, dts[:, 1, SH:2 * SH]).then_inc(acs_ps, 1)

            pe.wait_ge(set_up, 1)
            pe.wait_ge(x_in, 32)
            turn_parts(0, xn)
            logits, turn, values = attention(EH, 0, work_e, [4], [5], 6)
            n_groups = len(groups(EH))

            def attention_step(u):
                s = u - ATT_FROM
                if s == 0:
                    pe.wait_ge(tab_sb, 2)
                    pe.wait_ge(dt_dve, 1)
                    pe.wait_ge(set_up, 3)
                    pe.wait_ge(proj_sb, pieces_by[2])
                    pe.wait_ge(F_in, 16)
                if s < n_groups:
                    logits(s)
                if 1 <= s <= n_groups:
                    turn(s - 1)
                if s >= 2:
                    values(s - 2)

            def x_rows(half):
                pe.wait_ge(conv_act, 6 + 2 * half)
                if half == 0:
                    pe.wait_ge(tr_lo, TR_BEFORE[2])
                else:
                    pe.wait_ge(proj_sb, pieces_by[6])
                for t in range(TT):
                    for c in range(4):
                        ins = pe.transpose(ps[:, Y_BANKS[half][t], c * P:c * P + P], cv[:, 4 * half + c, t * P:t * P + P], ident)
                ins.then_inc(xs_ps, 1)

            def sums(q):
                if q:
                    pe.wait_ge(seg_sb, q)
                for m in range(2):
                    h = 2 * q + m
                    mm(ps[:, 6, 256 * m:256 * m + 256], dts[:, 1, h:h + 1].to_broadcast([P, P]), upper_ones, start=(m == 0))
                    ins = mm(ps[:, 6, 256 * m + 128:256 * m + 256], dts[:, 1, SH + h:SH + h + 1].to_broadcast([P, P]), upper)
                ins.then_inc(seg_ps, 1)

            def group_cb(g):
                if g:
                    pe.wait_ge(cb_sb, 3 * g)
                B, C = cv[:, 8 + g, :], cv[:, 12 + g, :]
                mm(ps[:, 7, 0:256], B[:, 0:P], C, start=True)
                mm(ps[:, 7, 256:384], B[:, P:SEQ], C[:, P:SEQ]).then_inc(cb_ps, 1)

            def heads_out(q):
                pe.wait_ge(m_sb, q + 1)
                if q % 4 == 0:
                    pe.wait_ge(xdt_sb, q // 2 + 2)
                    pe.wait_ge(xs_sb, q // 2 + 2)
                for m in range(2):
                    h = 2 * q + m
                    col = (h % 8) * HD
                    M = decay[:, q % 2, m, :]
                    y = [ps[:, b, col:col + HD] for b in Y_BANKS[h // 8]]
                    xh = [xdt[:, t, h * HD:h * HD + HD] for t in range(TT)]
                    mm(y[0], M[:, 0:P], xh[0], start=(h % 8 == 0))
                    mm(y[1], M[:, P:2 * P], xh[0], start=(h % 8 == 0))
                    ins = mm(y[1], M[:, 2 * P:3 * P], xh[1])
                ins.then_inc(y_ps, 1)

            def ssd_step(u, part):
                step = 2 * (u - SSD_FROM) + part
                if step == 0:
                    pe.wait_ge(att_sb, 2)
                    pe.wait_ge(acs_sb, 1)
                    pe.wait_ge(conv_act, 4)
                    turn_parts(1, mix_e)
                    sums(0)
                    group_cb(0)
                elif step == 1:
                    sums(1)
                elif step == 2:
                    x_rows(0)
                else:
                    heads_out(step - 3)
                    sums(step - 1)
                    if step % 2:
                        group_cb((step - 1) // 2)
                    if step == 5:
                        x_rows(1)

            for n in range(len(EVEN)):
                before = None
                if ATT_FROM <= 2 * n < SSD_FROM:
                    def before(u, part):
                        if part == 0:
                            if u == SSD_FROM - 1:
                                pe.wait_ge(pT_sb, n_groups)
                                running_sums()
                            attention_step(u)
                if 2 * n >= SSD_FROM:
                    before = ssd_step
                project(n, fresh=0 if n == 0 else None, before=before)
                if n == 1:
                    tables()
            heads_out(5)
            sums(7)
            pe.wait_ge(proj_sb, pieces_by[len(EVEN) - 1])
            held = [arrive()]
            out_products(0, 1, held[0], 0, 0)
            heads_out(6)
            held.append(arrive())
            out_products(0, 1, held[1], 1, 0)
            heads_out(7)
            pe.wait_ge(seg_sb, 8)
            pe.wait_ge(cb_sb, 12)
            for u in range(2):
                out_products(0, 1, held[u], u, 1).then_inc(w_used, 1)
            turn_parts(2, mix_e, col0=512, ready=lambda t: pe.wait_ge(mix_sb, t + 1))
            project_out(0, 2, range(2, 6), before=4)
            turn_x(3, 0)

            s_c, t_c, a_c = Tally(), Tally(), Tally()

            def ffn_up(fresh=None):
                if a_c.started():
                    pe.wait_ge(a_dve, a_c.at())
                a_c.up()
                for bank in (4, 5):
                    slot = arrive()
                    w = [a[:, slot, :].rearrange("p (k n) -> p k n", k=KC) for a in (w_hi, w_lo)]
                    for j in range(2):
                        cols = slice(j * P, j * P + P)
                        for kc in range(KC):
                            if fresh is not None and bank == 4 and j == 0:
                                parts_ready(fresh, kc)
                            ins = mm3(ps[:, bank, j * SEQ:j * SEQ + SEQ], w[0][:, kc, cols], w[1][:, kc, cols], xT_hi[:, kc, :], xT_lo[:, kc, :],
                                      start=(j == 0 and kc == 0))
                    ins.then_inc(w_used, 1)
                mm(ps[:, 4, 0:2], zt[:, 0:P], zt[:, 0:2]).then_inc(h_ps, 1)

            def ffn_down(last=False):
                pe.wait_ge(aT_l, t_c.up())
                slot = arrive()
                w = [a[:, slot, :].rearrange("p (k n) -> p k n", k=2) for a in (w_hi, w_lo)]
                for t in range(TT):
                    for k in range(2):
                        toks = slice(k * SEQ + t * P, k * SEQ + t * P + P)
                        for half in range(2):
                            cols = slice(512 * half, 512 * half + 512)
                            ins = mm3(ps[:, 2 * t + half, :], aT_hi[:, toks], aT_lo[:, toks], w[0][:, k, cols], w[1][:, k, cols])
                    if last and t == 0:
                        ins.then_inc(wout_ps, 1)
                ins.then_inc(w_used, 1)

            ffn_up(fresh=3)
            for b in range(4):
                mm(ps[:, b, :], zt[:, 0:P], zt[:, :], start=True)
            with rounds(pe, (FFN_STEPS - 1) // 2, {unit: 6, t_c: 2, a_c: 2}):
                for _ in range(2):
                    ffn_up()
                    ffn_down()
            ffn_down(last=True)
            mm(ps[:, 2, 0:2], zt[:, 0:P], zt[:, 0:2]).then_inc(wout_ps, 1)
            turn_x(4, TT)

            for n in range(len(EVEN), len(EVEN) + len(ODD)):
                project(n, fresh=4 if n == len(EVEN) else None)
            pe.wait_ge(proj_sb, pieces_by[-1])
            pe.wait_ge(F_in, 32)
            logits, turn, values = attention(OH, len(groups(EH)), work_o, [0, 1], [2, 3], 4)
            logits(0)
            for g in range(len(groups(OH))):
                if g + 1 < len(groups(OH)):
                    logits(g + 1)
                turn(g)
                if g:
                    values(g - 1)
            values(len(groups(OH)) - 1)
            pe.wait_ge(att_sb, 2 + 4)
            turn_parts(5, mix_o)
            project_out(2, 5, range(4))
            turn_x(6, 2 * TT)

            pe.wait_ge(rout_cut, 2)
            for kc in range(KC):
                parts_ready(6, kc)
                for t in range(TT):
                    toks = slice(t * P, t * P + P)
                    cols = slice(kc * NE, kc * NE + NE)
                    ins = mm3(ps[:, 4, t * NE:t * NE + NE], xT_hi[:, kc, toks], xT_lo[:, kc, toks], r_hi[:, cols], r_lo[:, cols],
                              start=(t == 0 and kc == 0))
            ins.then_inc(rt_ps, 1)
            pe.wait_ge(rt_dve, 2)
            mm(ps[:, 5, 0:NE], strict, lg[:, 7, 0:NE], start=True)
            mm(ps[:, 5, NE:2 * NE], ones, lg[:, 7, 0:NE])
            mm(ps[:, 5, NE:2 * NE], strict, lg[:, 7, NE:2 * NE])
            mm(ps[:, 5, 2 * NE:3 * NE], ones, lg[:, 7, 0:NE])
            mm(ps[:, 5, 2 * NE:3 * NE], ones, lg[:, 7, NE:2 * NE]).then_inc(rt_ps, 1)

            pm_c, xg_c, y_c, pt_c, sa_c, se_c = Tally(), Tally(), Tally(), Tally(), Tally(), Tally()

            def gather():
                pe.wait_ge(pm_sb, pm_c.up(2))
                for b in range(2):
                    for c in range(4):
                        kc = 4 * b + c
                        for t in range(TT):
                            ins = mm(ps[:, 6 + b, c * P:c * P + P], xn[:, t, kc * P:kc * P + P], Pm[:, t, :], start=(t == 0))
                    ins.then_inc(ga_ps, 1)

            def up(bank):
                for half in range(2):
                    slot = arrive()
                    w = [a[:, slot, :].rearrange("p (k n) -> p k n", k=4) for a in (w_hi, w_lo)]
                    for k in range(4):
                        kc = 4 * half + k
                        ins = mm3(ps[:, bank, :], xg_hi[:, kc, :], xg_lo[:, kc, :], w[0][:, k, :], w[1][:, k, :], start=(kc == 0))
                    ins.then_inc(w_used, 1)
                mm(ps[:, bank, 0:2], zt[:, 0:P], zt[:, 0:2]).then_inc(h_ps, 1)

            def turn():
                pe.wait_ge(a_dve, a_c.at())
                for c in range(4):
                    ins = pe.transpose(ps[:, 2, c * P:c * P + P], a_sb[:, c * P:c * P + P], ident)
                ins.then_inc(aT_ps, 1)

            def down():
                pe.wait_ge(aT_l, t_c.up())
                for u in range(2):
                    slot = arrive()
                    w = [a[:, slot, :].rearrange("p (k n) -> p k n", k=2) for a in (w_hi, w_lo)]
                    for k in range(2):
                        rows = slice((2 * u + k) * P, (2 * u + k) * P + P)
                        for half in range(2):
                            cols = slice(512 * half, 512 * half + 512)
                            ins = mm3(ps[:, 4 + half, :], aT_hi[:, rows], aT_lo[:, rows], w[0][:, k, cols], w[1][:, k, cols])
                    ins.then_inc(w_used, 1)

            def scatter():
                pe.wait_ge(yl, y_c.up(2))
                for t in range(TT):
                    for half in range(2):
                        n = 2 * t + half
                        cols = slice(512 * half, 512 * half + 512)
                        mm(ps[:, SC_BANKS[n], :], PmT[:, t * P:t * P + P], y_hi[:, cols], start=True)
                        mm(ps[:, SC_BANKS[n], :], PmT[:, t * P:t * P + P], y_lo[:, cols]).then_inc(sc_ps, 1)
                sa_c.up(4)

            def gate_up(first=False):
                pe.wait_ge(a_dve, a_c.at())
                a_c.up()
                up(0)
                if first:
                    scatter()
                    for b in range(2):
                        mm(ps[:, 4 + b, :], zt[:, 0:P], zt[:, :], start=True)
                up(1)

            pe.wait_ge(rt_dve, 4)
            mm(ps[:, 4, :], zt[:, 0:P], zt[:, :], start=True)
            mm(ps[:, 5, :], zt[:, 0:P], zt[:, :], start=True).then_inc(down_ps, 1)
            gather()
            n_runs = pe.value_load(runs[0:1, 0:1], min_val=NE, max_val=NE * ROUNDS)
            with rounds(pe, n_runs, {unit: 42, pm_c: 2, xg_c: 2, y_c: 2, sa_c: 4, t_c: FE_STEPS, a_c: FE_STEPS, pt_c: 2}):
                pe.wait_ge(xg_l, xg_c.up(2))
                gate_up(first=True)
                pe.wait_ge(sc_add, sa_c.at())
                for t in range(TT):
                    pe.transpose(ps[:, 3, t * P:t * P + P], Pm[:, t, :], ident)
                for t in range(TT):
                    ins = mm(ps[:, 3, SEQ:SEQ + 1], Pm[:, t, :], rot[:, 0, 2 + t:3 + t], start=(t == 0))
                ins.then_inc(pmT_ps, 1)
                turn()
                with rounds(pe, FE_STEPS - 1, {unit: 6, t_c: 1, a_c: 1}):
                    gate_up()
                    down()
                    turn()
                pe.wait_ge(pmT_sb, pt_c.up(2))
                gather()
                down()
                mm(ps[:, 4, 0:2], zt[:, 0:P], zt[:, 0:2]).then_inc(down_ps, 1)
            scatter()


SC_BANKS = [6, 7, 3, 2]

_INS = ["x", "rel_bias", "ln_mix_g", "ln_mix_b", "ln_ffn_g", "ln_ffn_b", "even_w_in", "even_conv_w",
        "even_conv_b", "even_dt_bias", "even_A_log", "even_D", "even_norm_g", "even_w_out",
        "ffn_w_in", "ffn_w_down", "odd_w_qkv", "odd_w_out", "moe_router", "moe_w_in", "moe_w_down"]
_OUTS = [((1, SEQ, D), "float32")]


def kernel(**inputs):
    import numpy as _np
    import concourse.bacc as _bacc
    from concourse import mybir as _mybir
    from concourse.bass_utils import run_bass_kernel_spmd as _run

    nc = _bacc.Bacc("TRN2", target_bir_lowering=False, num_devices=1)
    arrays, args = {}, []
    named = [(n, _np.ascontiguousarray(inputs[n])) for n in _INS]
    named += list(zip(("const", "hot"), shape_constants()))
    for name, a in named:
        arrays[f"in_{name}_dram"] = a
        args.append(nc.dram_tensor(f"in_{name}_dram", a.shape, _mybir.dt.from_np(a.dtype), kind="ExternalInput").ap())
    for i, (shape, dtype) in enumerate(_OUTS):
        args.append(nc.dram_tensor(f"out_{i}_dram", shape, _mybir.dt.from_np(_np.dtype(dtype)), kind="ExternalOutput").ap())
    trunk(nc, *args)
    r = _run(nc, [arrays], core_ids=[0])
    return r.results[0]["out_0_dram"]
```

```python
import math
from contextlib import ExitStack, contextmanager

import numpy as np

import concourse.bass as bass
from concourse import mybir

F32 = mybir.dt.float32
F32R = mybir.dt.float32r
BF16 = mybir.dt.bfloat16
ALU = mybir.AluOpType
ACT = mybir.ActivationFunctionType
AX_X = mybir.AxisListType.X

P = 128
SEQ = 256
D = 1024
TT = SEQ // P
KC = D // P
HD = 64
EH = 8
OH = 16
SH = 16
SG = 4
CONV = 4
XBC_T = 16
FFN = 2816
NE = 8
FE = 3584
BUCKETS = 32
ALPHA = (2.0 * 2) ** 0.25
EPS = 1e-5
QSCALE = HD ** -0.5
MASKED = -1.0e30

RAW = 6
CUT = 3
UNIT = 2048
FFN_STEPS = FFN // 256
FE_STEPS = FE // 512
ROUNDS = SEQ // P

C_ID, C_UP, C_ONE, C_SU, C_JROW, C_REV, C_IDX, C_IDX8 = 0, 128, 256, 384, 512, 640, 768, 776
C_W = 784


def shape_constants():
    c = np.zeros((P, C_W), np.float32)
    i = np.arange(P)
    c[:, C_ID:C_ID + P] = np.eye(P)
    c[:, C_UP:C_UP + P] = i[:, None] <= i[None, :]
    c[:, C_ONE:C_ONE + P] = 1.0
    c[:, C_SU:C_SU + P] = i[:, None] < i[None, :]
    c[:, C_JROW:C_JROW + P] = i[None, :]
    c[:, C_REV:C_REV + P] = i[:, None] + i[None, :] == P - 1
    c[:, C_IDX:C_IDX + NE] = np.arange(NE)
    c[:, C_IDX8:C_IDX8 + NE] = np.arange(NE) + NE
    hot = np.zeros((BUCKETS + 1, 2, 512), np.float32)
    for col in range(2 * SEQ - 1):
        d = SEQ - 1 - col
        if d < 0:
            hot[BUCKETS, :, col] = MASKED
            continue
        half = BUCKETS // 2
        b = d if d < half else min(BUCKETS - 1, half + int(math.log(d / half) / math.log(2048 / half) * half))
        hot[b, :, col] = 1.0 / QSCALE
        seen = (d <= 128) + (d % 4 == 0) + (d % 16 == 0)
        hot[BUCKETS, 1, col] = math.log(seen) / QSCALE if seen else MASKED
    return c, hot


class Tally:

    def __init__(self, n=0):
        self.n = n
        self.loops = []

    def at(self, back=0):
        v = self.n - back
        for i, k in self.loops:
            v = i * k + v
        return v

    def up(self, k=1):
        self.n += k
        return self.at()

    def started(self, back=0):
        return bool(self.loops) or self.n - back > 0


@contextmanager
def rounds(eng, count, steps):
    first = {t: t.n for t in steps}
    with eng.Fori(0, count) as i:
        for t, k in steps.items():
            t.loops.append((i, k))
        yield i
    for t, k in steps.items():
        assert t.n - first[t] == k, (t.n - first[t], k)
        t.loops.pop()
        if isinstance(count, int):
            t.n = first[t] + k * count
        else:
            t.n = first[t]
            t.loops.append((count, k))


def trunk(nc, x, rel_bias, ln_mix_g, ln_mix_b, ln_ffn_g, ln_ffn_b, even_w_in, even_conv_w,
          even_conv_b, even_dt_bias, even_A_log, even_D, even_norm_g, even_w_out,
          ffn_w_in, ffn_w_down, odd_w_qkv, odd_w_out, moe_router, moe_w_in, moe_w_down,
          const_in, hot_in, out):
    with ExitStack() as ctx:
        def sb(name, shape, dt=F32):
            return ctx.enter_context(nc.sbuf_tensor(name, shape, dt))

        def sem(name):
            return ctx.enter_context(nc.semaphore(name))

        raw = sb("raw", [P, RAW, UNIT])
        w_hi = sb("w_hi", [P, CUT, UNIT], F32R)
        w_lo = sb("w_lo", [P, CUT, UNIT], F32R)
        t_hi = sb("t_hi", [P, 12 * SEQ], F32R)
        t_lo = sb("t_lo", [P, 12 * SEQ], F32R)
        aT_hi = sb("aT_hi", [P, 512], F32R)
        aT_lo = sb("aT_lo", [P, 512], F32R)
        xn = sb("xn", [P, TT, D])
        con = sb("con", [P, C_W])
        zt = sb("zt", [P, 512], BF16)
        arena = sb("arena", [P, 17200])
        rel33 = sb("rel33", [BUCKETS + 1, OH])
        pcol = sb("pcol", [P, 80])
        w_dt = sb("w_dt", [P, KC, SH])
        hpar = sb("hpar", [P, 3, SH])
        dts = sb("dts", [P, 8, TT * SH])
        heads_first = dts[:, :, :].rearrange("p a b -> p (a b)")
        acs = sb("acs", [P, TT, SH])
        rmx = sb("rmx", [P, 2, 4])
        rneg = sb("rneg", [P, 2, 4])
        rsum = sb("rsum", [P, TT, OH])
        rinv = sb("rinv", [P, TT, OH])
        stat = sb("stat", [P, TT, 2, 6])
        mv = sb("mv", [P, TT, 2])
        rstd = sb("rstd", [P, TT, 3])
        gss = sb("gss", [P, 3, TT * SG])
        rout = sb("rout", [P, KC, NE])
        lg = sb("lg", [P, 10, TT * NE])
        l1 = sb("l1", [P, 8, TT])
        rot = sb("rot", [P, NE, 4])
        rtm = sb("rtm", [P, NE, 4])
        cj = sb("cj", [P, 1])
        warm = sb("warm", [P, 2])
        runs = sb("runs", [1, 2], mybir.dt.int32)

        def area(at, n):
            return arena[:, at:at + n]

        ident = con[:, C_ID:C_ID + P]
        upper = con[:, C_UP:C_UP + P]
        upper_ones = con[:, C_UP:C_UP + 2 * P]
        ones = con[:, C_ONE:C_ONE + P]
        strict = con[:, C_SU:C_SU + P]
        jrow = con[:, C_JROW:C_JROW + P]
        rev = con[:, C_REV:C_REV + P]

        PADW = SEQ + CONV - 1
        xp = area(0, XBC_T * PADW).rearrange("p (c s) -> p c s", c=XBC_T)
        cv = area(4144, XBC_T * SEQ).rearrange("p (c s) -> p c s", c=XBC_T)
        zs = area(8240, TT * D).rearrange("p (t c) -> p t c", t=TT)
        v_e = area(10288, TT * 512).rearrange("p (t c) -> p t c", t=TT)
        kT_e = area(11312, 4 * SEQ).rearrange("p (c s) -> p c s", c=4)
        F_e = area(12336, EH * SEQ).rearrange("p (h s) -> p h s", h=EH)
        mix_e = area(12336, TT * 1536).rearrange("p (t c) -> p t c", t=TT)
        hot = arena[0:BUCKETS + 1, 12336:12336 + 1024].rearrange("p (l s) -> p l s", l=2)
        crow = arena[0:80, 16432:16560]
        tbs = arena[0:OH, 13360:14384].rearrange("p (l s) -> p l s", l=2)
        qz_e = area(14384, EH * SEQ).rearrange("p (h s) -> p h s", h=EH)
        normg = area(15408, D)
        work_e = area(8240, 2048)
        XP_HALF = 4 * PADW
        xs = [area(XP_HALF * h, TT * 512).rearrange("p (t c) -> p t c", t=TT) for h in range(2)]
        xdt = area(2 * XP_HALF, TT * D).rearrange("p (t c) -> p t c", t=TT)
        decay = area(10288, 4 * 384).rearrange("p (b h s) -> p b h s", b=2, h=2)
        cbm = area(16432, 768).rearrange("p (b s) -> p b s", b=2)
        gb = area(12288, 2 * D).rearrange("p (g c) -> p g c", g=2)
        F_o = area(0, OH * SEQ).rearrange("p (h s) -> p h s", h=OH)
        qz_o = area(4096, OH * SEQ).rearrange("p (h s) -> p h s", h=OH)
        kT_o = area(8192, 8 * SEQ).rearrange("p (c s) -> p c s", c=8)
        v_o = area(10240, TT * D).rearrange("p (t c) -> p t c", t=TT)
        work_o = area(14336, 2048)
        mix_o = area(4096, TT * D).rearrange("p (t c) -> p t c", t=TT)
        a_sb = area(14336, 512)
        s_sb = area(14848, 512)
        acc = area(0, TT * D).rearrange("p (t c) -> p t c", t=TT)
        Pm = area(2048, TT * P).rearrange("p (t j) -> p t j", t=TT)
        y_hi = t_hi[:, 1024:2048]
        y_lo = t_lo[:, 1024:2048]
        PmT = t_hi[:, 2048:2048 + SEQ]
        r_hi = t_hi[:, 2304:2304 + KC * NE]
        r_lo = t_lo[:, 2304:2304 + KC * NE]
        fT_hi = [aT_hi[:, :], t_hi[:, 2560:3072]]
        fT_lo = [aT_lo[:, :], t_lo[:, 2560:3072]]
        xT_hi = t_hi[:, 0:KC * SEQ].rearrange("p (c s) -> p c s", c=KC)
        xT_lo = t_lo[:, 0:KC * SEQ].rearrange("p (c s) -> p c s", c=KC)
        mT_hi = t_hi[:, :].rearrange("p (c s) -> p c s", c=12)
        mT_lo = t_lo[:, :].rearrange("p (c s) -> p c s", c=12)
        xg_hi = t_hi[:, 0:D].rearrange("p (c j) -> p c j", c=KC)
        xg_lo = t_lo[:, 0:D].rearrange("p (c j) -> p c j", c=KC)

        ps = ctx.enter_context(nc.psum_tensor("ps", [P, 8, 512], F32))
        table = nc.dram_tensor("bias_by_distance", [2, OH, 512], F32, kind="Internal").ap()

        raw_in = [sem(f"raw_in{i}") for i in range(RAW)]
        first_in = sem("first_in")
        first_hi = sem("first_hi")
        first_lo = sem("first_lo")
        hi_done = sem("hi_done")
        lo_done = sem("lo_done")
        w_used = sem("w_used")
        con_in = sem("con_in")
        x_in = [sem(f"x_in{t}") for t in range(TT)]
        par_in = sem("par_in")
        set_up = sem("set_up")
        tab_ps = sem("tab_ps")
        tab_sb = sem("tab_sb")
        tab_out = sem("tab_out")
        F_in = sem("F_in")
        tr_ps = sem("tr_ps")
        tr_hi = sem("tr_hi")
        tr_lo = sem("tr_lo")
        proj_ps = sem("proj_ps")
        proj_sb = sem("proj_sb")
        conv_raw = sem("conv_raw")
        conv_act = sem("conv_act")
        wdt_cut = sem("wdt_cut")
        rout_cut = sem("rout_cut")
        dt_ps = sem("dt_ps")
        turned_sb = sem("turned_sb")
        dt_dve = sem("dt_dve")
        sq_act = sem("sq_act")
        dt_act = sem("dt_act")
        acs_ps = sem("acs_ps")
        acs_sb = sem("acs_sb")
        s_ps = sem("s_ps")
        neg_max = sem("neg_max")
        p_sb = sem("p_sb")
        pT_ps = sem("pT_ps")
        pT_sb = sem("pT_sb")
        pv_ps = sem("pv_ps")
        att_sb = sem("att_sb")
        xs_ps = sem("xs_ps")
        xs_sb = sem("xs_sb")
        xdt_sb = sem("xdt_sb")
        gate_sb = sem("gate_sb")
        cb_ps = sem("cb_ps")
        cb_sb = sem("cb_sb")
        seg_ps = sem("seg_ps")
        seg_sb = sem("seg_sb")
        dec_sb = sem("dec_sb")
        m_sb = sem("m_sb")
        y_ps = sem("y_ps")
        mix_sb = sem("mix_sb")
        wout_ps = sem("wout_ps")
        ln_var = sem("ln_var")
        ln_sd = sem("ln_sd")
        x_new = sem("x_new")
        dve_seq = sem("dve_seq")
        ln_seq = sem("ln_seq")
        h_ps = sem("h_ps")
        s_act = sem("s_act")
        a_dve = sem("a_dve")
        aT_ps = sem("aT_ps")
        aT_h = sem("aT_h")
        aT_l = sem("aT_l")
        rt_ps = sem("rt_ps")
        rt_dve = sem("rt_dve")
        rt_act = sem("rt_act")
        pm_sb = sem("pm_sb")
        ga_ps = sem("ga_ps")
        xg_h = sem("xg_h")
        xg_l = sem("xg_l")
        pmT_ps = sem("pmT_ps")
        pmT_sb = sem("pmT_sb")
        down_ps = sem("down_ps")
        yh = sem("yh")
        yl = sem("yl")
        sc_ps = sem("sc_ps")
        sc_add = sem("sc_add")
        zeroed = sem("zeroed")
        done = sem("done")

        G8 = 6
        EVEN = [("k", 512), ("q", 0), ("v", 1024), ("x", 3584), ("x", 4096),
                ("x", 2560), ("x", 3072), ("z", 1536), ("z", 2048)]
        CONV_BLOCKS = [2, 3, 0, 1]
        ODD = [("k", 1024), ("q", 0), ("v", 2048), ("k", 1536), ("q", 512), ("v", 2560)]
        PIECES = {"v": 2, "z": 2, "k": 2, "q": 4, "x": 2}
        pieces = [PIECES[k] for k, _ in EVEN + ODD]
        pieces_by = [sum(pieces[:n + 1]) for n in range(len(pieces))]
        TRANSPOSED = "kqx"

        def groups(heads):
            return [g for r in range(0, heads, 8)
                    for g in [(0, list(range(r + h, r + h + 4))) for h in range(0, 8, 4)]
                    + [(1, list(range(r + h, r + h + 2))) for h in range(0, 8, 2)]]

        TR_BANKS = [[4, 5, 6, 7], [4, 5], [0, 1, 4, 5], [4, 5, 0, 1], [4, 5, 6, 7], [2, 3], [4, 5], [4, 5, 6, 7]]
        TR_BEFORE = [sum(len(b) for b in TR_BANKS[:n]) for n in range(9)]
        TR_CHUNK = [0, 8, 0, 0, 0, 0, 4, 0]
        OUT_BANKS = [[2, 3, 6, 7], [0, 1, 2, 3], [0, 1, 2, 3]]
        Y_BANKS = [[4, 5], [0, 1]]
        SSD_STEPS = {14: [0, 1], 15: [2], 16: [3, 4], 17: [5, 6], 18: [7]}
        ODD_FROM = 4
        UNITS_EVEN = 2 * len(EVEN)
        ATT_FROM = 6
        SSD_FROM = 14

        def bank_of(n):
            return 2 if n in (len(EVEN) - 2, len(EVEN) - 1) else 2 * (n % 2)

        block = ctx.enter_context(nc.Block())

        @block.sync
        def _(sp):
            unit = Tally()

            def load(src, chunks):
                slot = unit.n % RAW
                if unit.started(RAW - 1) and (unit.loops or unit.n >= RAW):
                    sp.wait_ge(lo_done, unit.at(RAW - 1))
                dst = raw[:, slot, :].rearrange("p (k n) -> p k n", k=chunks)
                sp.dma_start(dst, src).then_inc(raw_in[slot], 16)
                unit.up()

            sp.dma_start(con[:, :], const_in[:, :]).then_inc(x_in[0], 16)
            for t in range(TT):
                sp.dma_start(xn[:, t, :], x[0, t * P:t * P + P, :]).then_inc(x_in[t], 16)
            w_in = even_w_in[0].rearrange("(k p) n -> p k n", p=P)
            c0 = EVEN[0][1]
            for part, done_in in enumerate((first_in, raw_in[0])):
                sp.dma_start(raw[:, 0, 1024 * part:1024 * part + 1024].rearrange("p (k n) -> p k n", k=2),
                             w_in[:, 2 * part:2 * part + 2, c0:c0 + 512]).then_inc(done_in, 16)
            unit.up()
            for n, (_, c0) in enumerate(EVEN):
                for half in range(0 if n else 1, 2):
                    load(w_in[:, 4 * half:4 * half + 4, c0:c0 + 512], 4)
            w_o = even_w_out[0].rearrange("(k p) n -> p k n", p=P)
            for u in range(6):
                load(w_o[:, 2 * u:2 * u + 2, :], 2)

            f_in = ffn_w_in[0].rearrange("(k p) n -> p k n", p=P)
            f_dn = ffn_w_down[0].rearrange("(k p) n -> p k n", p=P)

            def ffn_in(c):
                load(f_in[:, :, bass.ds(c, 256)], KC)
                load(f_in[:, :, bass.ds(c + FFN, 256)], KC)

            ffn_in(0)
            with rounds(sp, (FFN_STEPS - 1) // 2, {unit: 6}) as i:
                for j in range(2):
                    ffn_in(i * 512 + (j + 1) * 256)
                    load(f_dn[:, bass.ds(i * 4 + j * 2, 2), :], 2)
            load(f_dn[:, 2 * (FFN_STEPS - 1):2 * FFN_STEPS, :], 2)

            w_qkv = odd_w_qkv[0].rearrange("(k p) n -> p k n", p=P)
            for _, c0 in ODD:
                for half in range(2):
                    load(w_qkv[:, 4 * half:4 * half + 4, c0:c0 + 512], 4)
            w_o = odd_w_out[0].rearrange("(k p) n -> p k n", p=P)
            for u in range(4):
                load(w_o[:, 2 * u:2 * u + 2, :], 2)

            e_in = moe_w_in[0].rearrange("e (k p) n -> p e k n", p=P)
            e_dn = moe_w_down[0].rearrange("e (k p) n -> p e k n", p=P)

            def up_block(e, c):
                for half in range(2):
                    load(e_in[:, bass.ds(e, 1), 4 * half:4 * half + 4, bass.ds(c, 512)]
                         .rearrange("p e k n -> p (e k) n"), 4)

            def down_block(e, k):
                for half in range(2):
                    load(e_dn[:, bass.ds(e, 1), bass.ds(k + 2 * half, 2), :]
                         .rearrange("p e k n -> p (e k) n"), 2)

            def all_experts():
                with rounds(sp, NE, {unit: 42}) as e:
                    up_block(e, 0)
                    up_block(e, FE)
                    with rounds(sp, FE_STEPS - 1, {unit: 6}) as f:
                        up_block(e, f * 512 + 512)
                        up_block(e, f * 512 + 512 + FE)
                        down_block(e, f * 4)
                    down_block(e, 4 * (FE_STEPS - 1))

            all_experts()
            sp.wait_ge(rt_dve, 5)
            with sp.If(sp.value_load(runs[0:1, 0:1], min_val=NE, max_val=NE * ROUNDS) > NE):
                all_experts()

            for t in range(TT):
                sp.wait_ge(x_new, 3 * 2 * TT + 2 * t + 2)
                sp.dma_start(out[0, t * P:t * P + P, :], xn[:, t, :]).then_inc(done, 16)
            sp.wait_ge(done, 16 * TT)

        @block.gpsimd
        def _(pool):
            def everywhere(src, n):
                return bass.AP(src.tensor, src.offset, [[0, P], [1, n]])

            pool.memset(zt[:, :], 0.0).then_inc(set_up, 1)
            pool.memset(rel33[:, :], 1.0).then_inc(set_up, 1)
            pool.wait_ge(set_up, 2)
            pool.dma_start(rel33[0:BUCKETS, :], rel_bias[:, :]).then_inc(con_in, 16)
            pool.dma_start(hot, hot_in[:, :, :]).then_inc(con_in, 16)
            pool.dma_start(crow[0:64, :], even_conv_w[0].rearrange("k (c p) -> (k c) p", p=P)).then_inc(con_in, 16)
            pool.dma_start(crow[64:80, :], even_conv_b[0].rearrange("(c p) -> c p", p=P)).then_inc(con_in, 16)
            pool.dma_start(w_dt[:, :, :], even_w_in[0].rearrange("(k p) n -> p k n", p=P)[:, :, 4608:4624]).then_inc(con_in, 16)
            for n, src in enumerate((even_dt_bias, even_A_log, even_D)):
                pool.dma_start(hpar[:, n, :], everywhere(src[0], SH)).then_inc(con_in, 16)
            pool.memset(qz_e, 0.0).then_inc(set_up, 1)
            pool.memset(xp, 0.0).then_inc(set_up, 1)

            pool.wait_ge(tab_sb, 2)
            pool.dma_start(table.rearrange("l h s -> h l s"), tbs).then_inc(tab_out, 16)
            pool.wait_ge(tab_out, 16)
            pool.dma_start(F_e, bass.AP(table.tensor, table.offset, [[1, P], [512, EH], [1, SEQ]])).then_inc(F_in, 16)
            pool.wait_ge(att_sb, 2)
            pool.dma_start(normg, everywhere(even_norm_g[0], D)).then_inc(par_in, 16)
            pool.wait_ge(mix_sb, 4)
            pool.dma_start(F_o, bass.AP(table.tensor, table.offset + OH * 512, [[1, P], [512, OH], [1, SEQ]])).then_inc(F_in, 16)
            pool.memset(qz_o, 0.0).then_inc(set_up, 1)
            pool.wait_ge(tr_hi, TR_BEFORE[3])
            pool.dma_start(gb[:, 0, :], everywhere(ln_mix_g[0], D)).then_inc(par_in, 16)
            pool.dma_start(gb[:, 1, :], everywhere(ln_mix_b[0], D)).then_inc(par_in, 16)
            pool.dma_start(rout[:, :, :], moe_router[0].rearrange("(k p) e -> p k e", p=P)).then_inc(con_in, 16)
            for n, (g, b) in enumerate(((ln_ffn_g[0], ln_ffn_b[0]), (ln_mix_g[1], ln_mix_b[1]), (ln_ffn_g[1], ln_ffn_b[1]))):
                pool.wait_ge(x_new, 2 * TT * (n + 1))
                pool.dma_start(gb[:, 0, :], everywhere(g, D)).then_inc(par_in, 16)
                pool.dma_start(gb[:, 1, :], everywhere(b, D)).then_inc(par_in, 16)

        @block.scalar
        def _(act):
            unit = Tally()

            def hi():
                n = unit.n
                turn = 16 * (n // RAW + 1)
                for i, k in unit.loops:
                    turn = i * (16 * k // RAW) + turn
                act.wait_ge(raw_in[n % RAW], turn)
                if unit.loops or n >= CUT:
                    act.wait_ge(w_used, unit.at(CUT - 1))
                act.activation(w_hi[:, n % CUT, :], raw[:, n % RAW, :], ACT.Copy).then_inc(hi_done, 1)
                unit.up()

            def transposed_hi(n):
                for j, b in enumerate(TR_BANKS[n]):
                    c = TR_CHUNK[n] + 2 * j
                    act.wait_ge(tr_ps, TR_BEFORE[n] + j + 1)
                    act.activation(mT_hi[:, c:c + 2, :].rearrange("p c s -> p (c s)"), ps[:, b, :], ACT.Copy).then_inc(tr_hi, 1)

            def project_evac(n):
                kind, c0 = (EVEN + ODD)[n]
                even = n < len(EVEN)
                act.wait_ge(proj_ps, n + 1)
                for b in range(2):
                    src = ps[:, bank_of(n) + b, :]
                    if kind == "z":
                        act.activation(zs[:, b, c0 - 1536:c0 - 1024], src, ACT.Silu).then_inc(proj_sb, 1)
                    elif kind == "v":
                        at = c0 - (1024 if even else 2048)
                        act.activation((v_e if even else v_o)[:, b, at:at + 512], src, ACT.Copy).then_inc(proj_sb, 1)
                    elif kind == "k":
                        at = (c0 - (512 if even else 1024)) // P + 2 * b
                        act.activation((kT_e if even else kT_o)[:, at:at + 2, :], src.rearrange("p (c s) -> p c s", c=2), ACT.Copy).then_inc(proj_sb, 1)
                    elif kind == "x":
                        at = (c0 - 2560) // P + 2 * b
                        act.activation(xp[:, at:at + 2, CONV - 1:], src.rearrange("p (c s) -> p c s", c=2), ACT.Copy).then_inc(proj_sb, 1)
                    else:
                        if b == 0:
                            act.wait_ge(set_up, 4 if even else 5)
                        h0 = 2 * (c0 // P + 2 * b)
                        q = qz_e if even else qz_o
                        for s in range(2):
                            rows = slice(HD * s, HD * s + HD)
                            act.activation(q[rows, h0 + s:h0 + s + 3:2, :], src[rows, :].rearrange("p (c s) -> p c s", c=2), ACT.Copy).then_inc(proj_sb, 1)

            def silu_conv(i):
                c = 4 * CONV_BLOCKS[i // 2] + 2 * (i % 2)
                act.wait_ge(conv_raw, i + 1)
                act.activation(cv[:, c:c + 2, :], cv[:, c:c + 2, :], ACT.Silu).then_inc(conv_act, 1)

            def attention(heads, work, first, s_banks, t_banks):
                pT = work[:, 1024:2048].rearrange("p (b s) -> p b s", b=2)
                p = work[:, 0:1024].rearrange("p (b s) -> p b s", b=2)
                gs = groups(heads)

                def exps(g):
                    t, hs = gs[g]
                    act.wait_ge(neg_max, first + g + 1)
                    if g >= 2:
                        act.wait_ge(pT_ps, first + g - 1)
                    w = 512 // len(hs)
                    for m, h in enumerate(hs):
                        act.activation(p[:, g % 2, m * w:(m + 1) * w], ps[:, s_banks[g % len(s_banks)], m * w:(m + 1) * w], ACT.Exp,
                                       bias=rneg[:, g % 2, m:m + 1], scale=QSCALE,
                                       accum_out=rsum[:, t, h:h + 1]).then_inc(p_sb, 1)

                def turned(g):
                    act.wait_ge(pT_ps, first + g + 1)
                    if g >= 2:
                        act.wait_ge(pv_ps, first + g - 1)
                    act.activation(pT[:, g % 2, :], ps[:, t_banks[g % len(t_banks)], :], ACT.Copy).then_inc(pT_sb, 1)

                return exps, turned

            def root_table(n):
                act.activation(warm[:, n:n + 1], con[:, C_ONE:C_ONE + 1], ACT.Sqrt)

            def norm_root(n, t):
                act.wait_ge(ln_var, TT * n + t + 1)
                act.activation(rstd[:, t, 1:2], rstd[:, t, 0:1], ACT.Sqrt).then_inc(ln_sd, 1)

            def decays(q):
                act.wait_ge(seg_sb, q + 1)
                act.activation(decay[:, q % 2, :, :], decay[:, q % 2, :, :], ACT.Exp).then_inc(dec_sb, 1)

            transposed_hi(0)
            act.wait_ge(first_in, 16)
            act.activation(w_hi[:, 0, 0:1024], raw[:, 0, 0:1024], ACT.Copy).then_inc(first_hi, 1)
            act.wait_ge(raw_in[0], 16)
            act.activation(w_hi[:, 0, 1024:2048], raw[:, 0, 1024:2048], ACT.Copy).then_inc(hi_done, 1)
            unit.up()
            hi()
            exps, turned = attention(EH, work_e, 0, [4], [5])
            for u in range(UNITS_EVEN + 1):
                if u == 16:
                    project_evac(7)
                hi()
                if u % 2 == 0 and 2 <= u and u != 16:
                    if u == 8:
                        act.wait_ge(set_up, 4)
                    project_evac(u // 2 - 1)
                if u == 5:
                    act.wait_ge(dt_dve, 1)
                    act.activation(dts[:, 2, :], dts[:, 1, :], ACT.Exp).then_inc(dt_act, 1)
                    act.activation(hpar[:, 1, :], hpar[:, 1, :], ACT.Exp).then_inc(dt_act, 1)
                if 1 <= u - ATT_FROM <= len(groups(EH)):
                    turned(u - ATT_FROM - 1)
                if 0 <= u - ATT_FROM < len(groups(EH)):
                    exps(u - ATT_FROM)
                if u == 6:
                    act.wait_ge(dt_dve, 2)
                    act.activation(dts[:, 4, :], dts[:, 3, :], ACT.Ln).then_inc(dt_act, 1)
                if u == SSD_FROM:
                    transposed_hi(1)
                if 9 <= u < 15:
                    silu_conv(u - 9)
                for q in SSD_STEPS.get(u, ()):
                    decays(q)
                    if q == 2:
                        silu_conv(6)
                    if q == 3:
                        silu_conv(7)
            root_table(0)
            n_sq = 0
            for half in range(2):
                for t in range(TT):
                    act.wait_ge(gate_sb, 2 * half + t + 1)
                    for g in range(2 * half, 2 * half + 2):
                        if n_sq:
                            act.wait_ge(sq_act, n_sq)
                        act.activation(cv[:, 0, :], mix_e[:, t, 512 + 256 * g:768 + 256 * g], ACT.Square,
                                       accum_out=gss[:, 2, SG * t + g:SG * t + g + 1]).then_inc(sq_act, 1)
                        n_sq += 1
            act.wait_ge(dt_dve, 5)
            act.activation(gss[:, 1, :], gss[:, 0, :], ACT.Sqrt).then_inc(dt_act, 1)
            transposed_hi(2)
            for _ in range(3):
                hi()
            norm_root(0, 0)
            hi()
            hi()
            norm_root(0, 1)
            transposed_hi(3)

            h_c, a_c, t_c = Tally(), Tally(), Tally()

            def ffn_silu():
                act.wait_ge(h_ps, h_c.up())
                if a_c.started():
                    act.wait_ge(a_dve, a_c.at())
                a_c.up()
                act.activation(s_sb, ps[:, 4, :], ACT.Silu).then_inc(s_act, 1)

            def ffn_hi(buf, first=False):
                act.wait_ge(a_dve, a_c.at())
                if not first:
                    act.wait_ge(w_used, unit.at(4))
                act.activation(fT_hi[buf], a_sb, ACT.Copy).then_inc(aT_h, 1)

            def act_turned():
                act.wait_ge(aT_ps, t_c.up())
                act.activation(aT_hi[:, :], ps[:, 2, :], ACT.Copy).then_inc(aT_h, 1)

            hi()
            ffn_silu()
            ffn_hi(0, first=True)
            with rounds(act, (FFN_STEPS - 1) // 2, {unit: 6, h_c: 2, a_c: 2}):
                for buf in (1, 0):
                    hi()
                    hi()
                    ffn_silu()
                    hi()
                    ffn_hi(buf)
            hi()
            hi()
            norm_root(1, 0)
            norm_root(1, 1)
            transposed_hi(4)

            exps, turned = attention(OH, work_o, G8, [4], [5])
            for u in range(2 * len(ODD)):
                hi()
                if u >= 2 and u % 2 == 0:
                    project_evac(len(EVEN) + u // 2 - 1)
                if u > ODD_FROM:
                    turned(u - ODD_FROM - 1)
                if u >= ODD_FROM:
                    exps(u - ODD_FROM)
            project_evac(len(EVEN) + len(ODD) - 1)
            turned(7)
            exps(8)
            transposed_hi(5)
            hi()
            turned(8)
            exps(9)
            turned(9)
            exps(10)
            turned(10)
            exps(11)
            hi()
            turned(11)
            transposed_hi(6)
            hi()
            root_table(1)
            norm_root(2, 0)
            hi()
            norm_root(2, 1)
            transposed_hi(7)

            act.wait_ge(rt_dve, 1)
            act.activation(l1[:, 5, :], l1[:, 4, :], ACT.Exp).then_inc(rt_act, 1)

            ga_c, yd_c = Tally(), Tally()

            def gathered():
                for b in range(2):
                    act.wait_ge(ga_ps, ga_c.up())
                    act.activation(xg_hi[:, 4 * b:4 * b + 4, :].rearrange("p c j -> p (c j)"), ps[:, 6 + b, :], ACT.Copy).then_inc(xg_h, 1)

            def out_parts():
                act.wait_ge(down_ps, yd_c.up())
                for b in range(2):
                    act.activation(y_hi[:, 512 * b:512 * b + 512], ps[:, 4 + b, :], ACT.Copy, scale=cj[:, 0:1]).then_inc(yh, 1)

            def silu():
                act.wait_ge(h_ps, h_c.up())
                act.wait_ge(a_dve, a_c.at())
                a_c.up()
                h_c.up()
                act.activation(s_sb, ps[:, 0, :], ACT.Silu).then_inc(s_act, 1)

            def expert(last=False):
                out_parts()
                hi()
                hi()
                silu()
                hi()
                hi()
                act_turned()
                with rounds(act, FE_STEPS - 1, {unit: 6, h_c: 2, a_c: 1, t_c: 1}):
                    hi()
                    hi()
                    silu()
                    for _ in range(4):
                        hi()
                    act_turned()
                gathered()
                if not last:
                    hi()
                    hi()

            act.wait_ge(zeroed, 2)
            gathered()
            act.wait_ge(rt_dve, 5)
            all_but_last = act.value_load(runs[0:1, 1:2], min_val=NE - 1, max_val=NE * ROUNDS - 1)
            with rounds(act, all_but_last, {unit: 42, h_c: 2 * FE_STEPS, a_c: FE_STEPS, t_c: FE_STEPS, ga_c: 2, yd_c: 1}):
                expert()
            expert(last=True)
            out_parts()
            norm_root(3, 0)
            norm_root(3, 1)

        @block.vector
        def _(dve):
            unit = Tally()
            own = Tally()
            own_sem = [dve_seq]

            def mine(ins):
                ins.then_inc(own_sem[0], 1)
                own.up()

            def settle():
                dve.wait_ge(own_sem[0], own.at())

            def lo():
                n = unit.n
                unit.up()
                dve.wait_ge(hi_done, unit.at())
                dve.tensor_tensor(w_lo[:, n % CUT, :], raw[:, n % RAW, :], w_hi[:, n % CUT, :].bitcast(F32), ALU.subtract).then_inc(lo_done, 1)

            def transposed_lo(n):
                for j, b in enumerate(TR_BANKS[n]):
                    c = TR_CHUNK[n] + 2 * j
                    dve.wait_ge(tr_hi, TR_BEFORE[n] + j + 1)
                    dve.tensor_tensor(mT_lo[:, c:c + 2, :].rearrange("p c s -> p (c s)"), ps[:, b, :],
                                      mT_hi[:, c:c + 2, :].rearrange("p c s -> p (c s)").bitcast(F32),
                                      ALU.subtract).then_inc(tr_lo, 1)

            def conv(i):
                tiles = [4 * CONV_BLOCKS[i // 2] + 2 * (i % 2) + c for c in range(2)]
                dve.wait_ge(proj_sb, pieces_by[3 + i // 2])
                for c in tiles:
                    mine(dve.tensor_scalar(cv[:, c, :], xp[:, c, 0:SEQ], pcol[:, c:c + 1], pcol[:, 64 + c:65 + c], ALU.mult, ALU.add))
                for k in range(1, CONV):
                    settle()
                    for c in tiles:
                        ins = dve.scalar_tensor_tensor(out=cv[:, c, :], in0=xp[:, c, k:k + SEQ], scalar=pcol[:, 16 * k + c:16 * k + c + 1],
                                                       in1=cv[:, c, :], op0=ALU.mult, op1=ALU.add)
                        if k == CONV - 1 and c == tiles[-1]:
                            ins.then_inc(conv_raw, 1)
                        else:
                            mine(ins)

            def attention(heads, work, first, s_banks, banks):
                gs = groups(heads)

                def maxima(g):
                    t, hs = gs[g]
                    dve.wait_ge(s_ps, first + g + 1)
                    if g >= 2:
                        dve.wait_ge(p_sb, exps[g - 2])
                    mine(dve.tensor_reduce(rmx[:, g % 2, 0:len(hs)], ps[:, s_banks[g % len(s_banks)], :].rearrange("p (h s) -> p h s", h=len(hs)), AX_X, ALU.max))
                    settle()
                    dve.tensor_scalar(rneg[:, g % 2, 0:len(hs)], rmx[:, g % 2, 0:len(hs)], -QSCALE, None, ALU.mult).then_inc(neg_max, 1)

                base = 0 if heads == EH else EXPS_EVEN
                exps, n = [], base
                for t, hs in gs:
                    n += len(hs)
                    exps.append(n)

                def finish(r=0):
                    dve.wait_ge(p_sb, exps[G8 * r + G8 - 1])
                    mine(dve.reciprocal(rinv[:, :, 8 * r:8 * r + 8], rsum[:, :, 8 * r:8 * r + 8]))
                    settle()
                    dve.wait_ge(pv_ps, first + G8 * r + G8)
                    mix = mix_e if heads == EH else mix_o
                    for t in range(TT):
                        dve.tensor_tensor(mix[:, t, 512 * r:512 * r + 512].rearrange("p (h c) -> p h c", h=8),
                                          ps[:, banks + t, :].rearrange("p (h c) -> p h c", h=8),
                                          rinv[:, t, 8 * r:8 * r + 8].rearrange("p (h o) -> p h o", o=1).to_broadcast([P, 8, HD]),
                                          ALU.mult).then_inc(att_sb, 1)

                return maxima, finish

            def layer_norm(n, add, between=None):
                if n == 3:
                    own_sem[0] = ln_seq
                    own.n, own.loops = 0, []
                for t in range(TT):
                    for half in range(2):
                        mine(add(t, half))
                        settle()
                        mine(dve.bn_stats(stat[:, t, half, :], xn[:, t, 512 * half:512 * half + 512]))
                    settle()
                    mine(dve.bn_aggr(mv[:, t, :], stat[:, t, :, :].rearrange("p a b -> p (a b)")))
                    settle()
                    dve.tensor_scalar(rstd[:, t, 0:1], mv[:, t, 1:2], EPS, None, ALU.add).then_inc(ln_var, 1)
                    if t == 0:
                        dve.wait_ge(par_in, 16 * (3 + 2 * n))
                    mine(dve.scalar_tensor_tensor(out=xn[:, t, :], in0=xn[:, t, :], scalar=mv[:, t, 0:1], in1=gb[:, 0, :],
                                                  op0=ALU.subtract, op1=ALU.mult))
                    dve.wait_ge(ln_sd, TT * n + t + 1)
                    mine(dve.reciprocal(rstd[:, t, 2:3], rstd[:, t, 1:2]))
                    settle()
                    for half in range(2):
                        cols = slice(512 * half, 512 * half + 512)
                        dve.scalar_tensor_tensor(out=xn[:, t, cols], in0=xn[:, t, cols], scalar=rstd[:, t, 2:3], in1=gb[:, 1, cols],
                                                 op0=ALU.mult, op1=ALU.add).then_inc(x_new, 1)
                    if t == 0 and between:
                        between()

            def residual(n):
                def add(t, half):
                    cols = slice(512 * half, 512 * half + 512)
                    dve.wait_ge(wout_ps, 2 * TT * n + 2 * t + half + 1)
                    return dve.scalar_tensor_tensor(out=xn[:, t, cols], in0=xn[:, t, cols], scalar=ALPHA, in1=ps[:, OUT_BANKS[n][2 * t + half], :],
                                                    op0=ALU.mult, op1=ALU.add)
                return add

            EXPS_EVEN = sum(len(hs) for _, hs in groups(EH))

            def softplus_a():
                dve.wait_ge(dt_ps, 2)
                mine(dve.tensor_tensor(dts[:, 0, :].rearrange("p (t h) -> p t h", t=TT), ps[:, 4, SEQ:SEQ + TT * SH].rearrange("p (t h) -> p t h", t=TT),
                                       hpar[:, 0:1, :].to_broadcast([P, TT, SH]), ALU.add))
                settle()
                mine(dve.tensor_scalar(dts[:, 1, :], dts[:, 0, :], -1.0, None, ALU.mult))
                settle()
                dve.tensor_tensor(dts[:, 1, :], dts[:, 0, :], dts[:, 1, :], ALU.min).then_inc(dt_dve, 1)

            def softplus_b():
                dve.wait_ge(dt_act, 2)
                dve.tensor_scalar(dts[:, 3, :], dts[:, 2, :], 1.0, None, ALU.add).then_inc(dt_dve, 1)

            def softplus_c():
                dve.wait_ge(dt_dve, 2)
                mine(dve.tensor_scalar(dts[:, 5, :], dts[:, 3, :], 1.0, None, ALU.subtract))
                settle()
                mine(dve.tensor_scalar(dts[:, 6, :], dts[:, 5, :], 0.0, None, ALU.is_equal))
                mine(dve.tensor_scalar(dts[:, 5, :], dts[:, 5, :], 1e-30, None, ALU.max))
                settle()
                mine(dve.reciprocal(dts[:, 7, :], dts[:, 5, :]))
                mine(dve.tensor_tensor(dts[:, 6, :], dts[:, 6, :], dts[:, 2, :], ALU.mult))
                settle()
                mine(dve.tensor_tensor(dts[:, 7, :], dts[:, 7, :], dts[:, 2, :], ALU.mult))
                settle()
                dve.wait_ge(dt_act, 3)
                mine(dve.tensor_tensor(dts[:, 7, :], dts[:, 7, :], dts[:, 4, :], ALU.mult))
                settle()
                mine(dve.tensor_tensor(dts[:, 7, :], dts[:, 7, :], dts[:, 6, :], ALU.add))
                settle()
                mine(dve.tensor_scalar(dts[:, 0, :], dts[:, 0, :], 0.0, None, ALU.max))
                settle()
                mine(dve.tensor_tensor(dts[:, 0, :], dts[:, 0, :], dts[:, 7, :], ALU.add))
                settle()
                mine(dve.tensor_tensor(dts[:, 1, :].rearrange("p (t h) -> p t h", t=TT), dts[:, 0, :].rearrange("p (t h) -> p t h", t=TT),
                                       hpar[:, 1:2, :].to_broadcast([P, TT, SH]), ALU.mult))
                settle()
                dve.tensor_scalar(dts[:, 1, :], dts[:, 1, :], -1.0, None, ALU.mult).then_inc(dt_dve, 1)

            def small_parts(src, at_hi, at_lo, done):
                dve.tensor_copy(at_hi, src).then_inc(done, 1)
                dve.wait_ge(done, 1)
                dve.tensor_tensor(at_lo, src, at_hi.bitcast(F32), ALU.subtract).then_inc(done, 1)

            def half_heads(a):
                return a.rearrange("p (h o) -> p h o", o=1).to_broadcast([P, SH // 2, HD])

            def x_rows(half):
                dve.wait_ge(xs_ps, half + 1)
                for t in range(TT):
                    src = ps[:, Y_BANKS[half][t], :].rearrange("p (h c) -> p h c", h=SH // 2)
                    h0 = SH * t + SH // 2 * half
                    dve.tensor_tensor(xdt[:, t, 512 * half:512 * half + 512].rearrange("p (h c) -> p h c", h=SH // 2), src,
                                      half_heads(dts[:, 0, h0:h0 + SH // 2]), ALU.mult).then_inc(xdt_sb, 1)
                    dve.tensor_tensor(xs[half][:, t, :].rearrange("p (h c) -> p h c", h=SH // 2), src,
                                      half_heads(hpar[:, 2, SH // 2 * half:SH // 2 * half + SH // 2]), ALU.mult).then_inc(xs_sb, 1)

            def differences(q):
                dve.wait_ge(seg_ps, q + 1)
                if q >= 2:
                    dve.wait_ge(y_ps, q - 1)
                for m in range(2):
                    h = 2 * q + m
                    mine(dve.tensor_scalar(decay[:, q % 2, m, 0:256], ps[:, 6, 256 * m:256 * m + 256], acs[:, 0, h:h + 1], 0.0, ALU.subtract, ALU.min))
                    ins = dve.tensor_scalar(decay[:, q % 2, m, 256:384], ps[:, 6, 256 * m + 128:256 * m + 256], acs[:, 1, h:h + 1], 0.0, ALU.subtract, ALU.min)
                    if m == 1:
                        ins.then_inc(seg_sb, 1)
                    else:
                        mine(ins)

            def masked_cb(g):
                dve.wait_ge(cb_ps, g + 1)
                if g >= 2:
                    dve.wait_ge(m_sb, 2 * g - 2)
                dve.tensor_tensor(cbm[:, g % 2, 0:128], ps[:, 7, 0:128], upper, ALU.mult).then_inc(cb_sb, 1)
                dve.tensor_copy(cbm[:, g % 2, 128:256], ps[:, 7, 128:256]).then_inc(cb_sb, 1)
                dve.tensor_tensor(cbm[:, g % 2, 256:384], ps[:, 7, 256:384], upper, ALU.mult).then_inc(cb_sb, 1)

            def times_cb(q):
                dve.wait_ge(dec_sb, q + 1)
                dve.wait_ge(cb_sb, 3 * (q // 2) + 3)
                dve.tensor_tensor(decay[:, q % 2, :, :], decay[:, q % 2, :, :], cbm[:, (q // 2) % 2:(q // 2) % 2 + 1, :].to_broadcast([P, 2, 384]),
                                  ALU.mult).then_inc(m_sb, 1)

            def gated(half):
                dve.wait_ge(xs_sb, 2 * half + 2)
                dve.wait_ge(y_ps, 4 * half + 4)
                dve.wait_ge(proj_sb, pieces_by[7 + half])
                for t in range(TT):
                    y = mix_e[:, t, 512 + 512 * half:1024 + 512 * half]
                    mine(dve.tensor_tensor(y, ps[:, Y_BANKS[half][t], :], xs[half][:, t, :], ALU.add))
                    settle()
                    dve.tensor_tensor(y, y, zs[:, t, 512 * half:512 * half + 512], ALU.mult).then_inc(gate_sb, 1)

            transposed_lo(0)
            dve.wait_ge(first_hi, 1)
            dve.tensor_tensor(w_lo[:, 0, 0:1024], raw[:, 0, 0:1024], w_hi[:, 0, 0:1024].bitcast(F32), ALU.subtract).then_inc(first_lo, 1)
            unit.up()
            dve.wait_ge(hi_done, 1)
            dve.tensor_tensor(w_lo[:, 0, 1024:2048], raw[:, 0, 1024:2048], w_hi[:, 0, 1024:2048].bitcast(F32), ALU.subtract).then_inc(lo_done, 1)
            lo()
            maxima, finish = attention(EH, work_e, 0, [4], 6)
            n_groups = len(groups(EH))
            for u in range(UNITS_EVEN + 1):
                s = u - ATT_FROM
                if u == 4:
                    dve.wait_ge(tab_ps, 1)
                    dve.tensor_copy(tbs, ps[0:OH, 6:8, :]).then_inc(tab_sb, 1)
                    dve.tensor_copy(pcol[:, :], ps[:, 5, 0:80]).then_inc(tab_sb, 1)
                    dve.wait_ge(dt_ps, 1)
                    dve.tensor_copy(heads_first[0:SH, :], ps[0:SH, 4, 0:SEQ]).then_inc(turned_sb, 1)
                if u == SSD_FROM - 1:
                    dve.wait_ge(acs_ps, 1)
                    dve.tensor_copy(acs[:, :, :].rearrange("p t h -> p (t h)"), ps[:, 5, 0:TT * SH]).then_inc(acs_sb, 1)
                    finish()
                if 0 <= s < n_groups:
                    maxima(s)
                if u == 14:
                    dve.wait_ge(acs_sb, 1)
                    differences(0)
                    masked_cb(0)
                    transposed_lo(1)
                    lo()
                    times_cb(0)
                    differences(1)
                elif u == 15:
                    times_cb(1)
                    x_rows(0)
                    lo()
                    differences(2)
                    masked_cb(1)
                    conv(6)
                elif u == 16:
                    times_cb(2)
                    differences(3)
                    conv(7)
                    lo()
                    times_cb(3)
                    differences(4)
                    masked_cb(2)
                    x_rows(1)
                elif u == 17:
                    times_cb(4)
                    differences(5)
                    lo()
                    times_cb(5)
                    masked_cb(3)
                    differences(6)
                elif u == 18:
                    times_cb(6)
                    differences(7)
                    gated(0)
                    times_cb(7)
                    lo()
                else:
                    lo()
                if 8 <= u < 14:
                    if u == 8:
                        dve.wait_ge(tab_sb, 2)
                    conv(u - 8)
                if u == 0:
                    dve.wait_ge(con_in, 128)
                    small_parts(w_dt[:, :, :].rearrange("p k h -> p (k h)"), aT_hi[:, 0:KC * SH], aT_lo[:, 0:KC * SH], wdt_cut)
                if u == 5:
                    softplus_a()
                if u == 6:
                    softplus_b()
                if u == 7:
                    softplus_c()

            gated(1)
            gw = D // SG
            dve.wait_ge(sq_act, TT * SG)
            dve.tensor_scalar(gss[:, 0, :], gss[:, 2, :], 1.0 / gw, EPS, ALU.mult, ALU.add).then_inc(dt_dve, 2)
            dve.wait_ge(dt_act, 4)
            mine(dve.reciprocal(gss[:, 2, :], gss[:, 1, :]))
            settle()
            dve.wait_ge(par_in, 16)
            dve.wait_ge(gate_sb, 2 * TT)
            for t in range(TT):
                for g in range(SG):
                    y = mix_e[:, t, 512 + gw * g:512 + gw * g + gw]
                    ins = dve.scalar_tensor_tensor(out=y, in0=y, scalar=gss[:, 2, SG * t + g:SG * t + g + 1], in1=normg[:, gw * g:gw * g + gw],
                                                   op0=ALU.mult, op1=ALU.mult)
                    if g % 2:
                        ins.then_inc(mix_sb, 1)
                    else:
                        mine(ins)
            transposed_lo(2)
            for _ in range(3):
                lo()
            layer_norm(0, residual(0), between=lo)
            transposed_lo(3)

            dve.wait_ge(con_in, 144)
            small_parts(rout[:, :, :].rearrange("p k e -> p (k e)"), r_hi, r_lo, rout_cut)
            h_c, s_c, t_c = Tally(), Tally(), Tally()

            def ffn_gate():
                dve.wait_ge(s_act, s_c.up())
                dve.wait_ge(h_ps, h_c.up())
                dve.tensor_tensor(a_sb, s_sb, ps[:, 5, :], ALU.mult).then_inc(a_dve, 1)

            def act_lo(src, buf=0):
                dve.wait_ge(aT_h, t_c.up())
                dve.tensor_tensor(fT_lo[buf], src, fT_hi[buf].bitcast(F32), ALU.subtract).then_inc(aT_l, 1)

            lo()
            lo()
            ffn_gate()
            act_lo(a_sb)
            with rounds(dve, (FFN_STEPS - 1) // 2, {unit: 6, s_c: 2, h_c: 2, t_c: 2}):
                for buf in (1, 0):
                    lo()
                    lo()
                    ffn_gate()
                    lo()
                    act_lo(a_sb, buf)
            lo()
            layer_norm(1, residual(1))
            transposed_lo(4)
            lo()
            maxima, finish = attention(OH, work_o, G8, [4], 6)
            for u in range(2 * len(ODD)):
                lo()
                if u >= ODD_FROM:
                    maxima(u - ODD_FROM)
            finish(0)
            maxima(8)
            transposed_lo(5)
            lo()
            for g in (9, 10, 11):
                maxima(g)
            lo()
            finish(1)
            transposed_lo(6)
            dve.memset(cj[:, :], 0.0).then_inc(zeroed, 1)
            dve.memset(PmT.bitcast(F32), 0.0).then_inc(zeroed, 1)
            mine(dve.memset(acc, 0.0))
            lo()
            layer_norm(2, residual(2))
            transposed_lo(7)
            lo()

            idx = con[:, C_IDX:C_IDX + NE].rearrange("p (o e) -> p o e", o=1).to_broadcast([P, TT, NE])
            idx8 = con[:, C_IDX8:C_IDX8 + NE].rearrange("p (o e) -> p o e", o=1).to_broadcast([P, TT, NE])

            def L(n):
                return lg[:, n, :].rearrange("p (t e) -> p t e", t=TT)

            def wide(n):
                return l1[:, n, :].rearrange("p (t o) -> p t o", o=1).to_broadcast([P, TT, NE])

            dve.wait_ge(rt_ps, 1)
            dve.tensor_copy(heads_first[0:NE, :], ps[0:NE, 4, 0:SEQ]).then_inc(turned_sb, 1)
            dve.wait_ge(rt_ps, 2)
            mine(dve.tensor_copy(lg[:, 0, :], ps[:, 4, SEQ:SEQ + TT * NE]))
            settle()
            for k in range(2):
                mine(dve.tensor_reduce(l1[:, k, :], L(k), AX_X, ALU.max))
                settle()
                mine(dve.tensor_tensor(L(4), L(k), wide(k), ALU.is_equal))
                settle()
                mine(dve.scalar_tensor_tensor(out=L(5), in0=L(4), scalar=-float(NE), in1=idx8, op0=ALU.mult, op1=ALU.add))
                settle()
                mine(dve.tensor_reduce(l1[:, 2 + k, :], L(5), AX_X, ALU.min))
                settle()
                mine(dve.tensor_tensor(L(2 + k), idx, wide(2 + k), ALU.is_equal))
                settle()
                if k == 0:
                    mine(dve.scalar_tensor_tensor(out=L(1), in0=L(2), scalar=-3.0e38, in1=L(0), op0=ALU.mult, op1=ALU.add))
                    settle()
            dve.tensor_tensor(l1[:, 4, :], l1[:, 1, :], l1[:, 0, :], ALU.subtract).then_inc(rt_dve, 1)
            mine(dve.tensor_tensor(L(6), L(2), L(3), ALU.add))
            settle()
            dve.tensor_copy(L(7), L(6)).then_inc(rt_dve, 1)
            def select():
                for t in range(TT):
                    dve.tensor_scalar(Pm[:, t, :], jrow, rot[:, 0, t:t + 1], None, ALU.is_equal).then_inc(pm_sb, 1)

            dve.wait_ge(rt_ps, 3)
            mine(dve.scalar_tensor_tensor(out=lg[:, 1, :], in0=ps[:, 5, 0:TT * NE], scalar=1000.0, in1=lg[:, 7, :], op0=ALU.add, op1=ALU.mult))
            settle()
            mine(dve.tensor_scalar(rot[:, :, 0:2].rearrange("p e t -> p t e"), L(1), 1000.0, None, ALU.subtract))
            settle()
            select()
            dve.wait_ge(rt_act, 1)
            mine(dve.tensor_scalar(l1[:, 6, :], l1[:, 5, :], 1.0, None, ALU.add))
            settle()
            mine(dve.reciprocal(l1[:, 7, :], l1[:, 6, :]))
            settle()
            mine(dve.tensor_tensor(l1[:, 6, :], l1[:, 7, :], l1[:, 5, :], ALU.mult))
            settle()
            mine(dve.tensor_tensor(L(8), L(2), wide(7), ALU.mult))
            mine(dve.tensor_tensor(L(9), L(3), wide(6), ALU.mult))
            settle()
            mine(dve.tensor_tensor(rot[:, :, 2:4].rearrange("p e t -> p t e"), L(8), L(9), ALU.add))
            mine(dve.tensor_reduce(l1[:, 0, 0:1], ps[:, 5, 2 * NE:3 * NE], AX_X, ALU.max))
            settle()
            mine(dve.tensor_scalar(l1[:, 0, 1:2], l1[:, 0, 0:1], P + 0.5, float(NE), ALU.is_gt, ALU.mult))
            settle()
            dve.tensor_copy(rtm[:, 0, 0:2], rot[:, 0, 0:2]).then_inc(rt_dve, 1)
            dve.tensor_scalar(runs[:, 0:1], l1[0:1, 0, 1:2], float(NE), None, ALU.add).then_inc(rt_dve, 1)
            dve.tensor_scalar(runs[:, 1:2], l1[0:1, 0, 1:2], float(NE - 1), None, ALU.add).then_inc(rt_dve, 1)
            dve.wait_ge(rt_dve, 5)

            def turn_round():
                mine(dve.tensor_copy(rtm[:, 0:NE - 1, :], rot[:, 1:NE, :]))
                mine(dve.tensor_scalar(rtm[:, NE - 1, 0:2], rot[:, 0, 0:2], float(P), None, ALU.subtract))
                mine(dve.tensor_copy(rtm[:, NE - 1, 2:4], rot[:, 0, 2:4]))
                settle()
                mine(dve.tensor_copy(rot[:, :, :], rtm[:, :, :]))
                settle()

            ga_c, y_c, sc_c, mt_c, sa_c = Tally(), Tally(), Tally(), Tally(), Tally()

            def gathered():
                for b in range(2):
                    dve.wait_ge(xg_h, ga_c.up())
                    dve.tensor_tensor(xg_lo[:, 4 * b:4 * b + 4, :].rearrange("p c j -> p (c j)"), ps[:, 6 + b, :],
                                      xg_hi[:, 4 * b:4 * b + 4, :].rearrange("p c j -> p (c j)").bitcast(F32), ALU.subtract).then_inc(xg_l, 1)

            def out_parts():
                dve.wait_ge(yh, y_c.up(2))
                for b in range(2):
                    dve.scalar_tensor_tensor(out=y_lo[:, 512 * b:512 * b + 512], in0=ps[:, 4 + b, :], scalar=cj[:, 0:1],
                                             in1=y_hi[:, 512 * b:512 * b + 512].bitcast(F32), op0=ALU.mult, op1=ALU.subtract).then_inc(yl, 1)

            def add_back():
                for t in range(TT):
                    for half in range(2):
                        dve.wait_ge(sc_ps, sc_c.up())
                        a = acc[:, t, 512 * half:512 * half + 512]
                        dve.tensor_tensor(a, a, ps[:, SC_BANKS[2 * t + half], :], ALU.add).then_inc(sc_add, 1)

            def gate():
                dve.wait_ge(s_act, s_c.up())
                dve.wait_ge(h_ps, h_c.up(2))
                dve.tensor_tensor(a_sb, s_sb, ps[:, 1, :], ALU.mult).then_inc(a_dve, 1)

            gathered()

            def expert(last=False):
                out_parts()
                lo()
                lo()
                add_back()
                if last:
                    dve.wait_ge(sc_add, sc_c.at())
                    for t in range(TT):
                        mine(dve.scalar_tensor_tensor(out=acc[:, t, :], in0=xn[:, t, :], scalar=ALPHA, in1=acc[:, t, :],
                                                      op0=ALU.mult, op1=ALU.add))
                lo()
                gate()
                lo()
                act_lo(ps[:, 2, :])
                dve.wait_ge(pmT_ps, mt_c.up())
                dve.tensor_copy(PmT, ps[:, 3, 0:SEQ]).then_inc(pmT_sb, 1)
                dve.tensor_copy(cj[:, :], ps[:, 3, SEQ:SEQ + 1]).then_inc(pmT_sb, 1)
                turn_round()
                select()
                with rounds(dve, FE_STEPS - 1, {unit: 6, s_c: 1, h_c: 2, t_c: 1}):
                    for _ in range(4):
                        lo()
                    gate()
                    lo()
                    lo()
                    act_lo(ps[:, 2, :])
                gathered()
                if not last:
                    lo()
                    lo()

            all_but_last = dve.value_load(runs[0:1, 1:2], min_val=NE - 1, max_val=NE * ROUNDS - 1)
            with rounds(dve, all_but_last, {unit: 42, s_c: FE_STEPS, h_c: 2 * FE_STEPS, t_c: FE_STEPS, ga_c: 2, y_c: 2, sc_c: 4, mt_c: 1, own: 4}):
                expert()
            expert(last=True)
            dve.wait_ge(pmT_sb, all_but_last * 2 + 2)
            out_parts()

            def last_add(t, half):
                cols = slice(512 * half, 512 * half + 512)
                dve.wait_ge(sc_ps, sc_c.up())
                return dve.tensor_tensor(xn[:, t, cols], acc[:, t, cols], ps[:, SC_BANKS[2 * t + half], :], ALU.add)

            layer_norm(3, last_add)

        @block.tensor
        def _(pe):
            unit = Tally()

            def arrive():
                slot = unit.n % CUT
                unit.up()
                pe.wait_ge(lo_done, unit.at())
                return slot

            def mm(o, a, b, start=False):
                return pe.matmul(o, a, b, start=start, stop=True, skip_group_check=True)

            def mm3(o, a_hi, a_lo, b_hi, b_lo, start=False):
                mm(o, a_hi, b_hi, start)
                mm(o, a_hi, b_lo)
                return mm(o, a_lo, b_hi)

            def turn_x(n, after):
                turn_parts(n, xn, ready=lambda t, half: pe.wait_ge(x_new, 2 * after + 2 * t + half + 1))

            def parts_ready(n, kc):
                if kc % 2 == 0:
                    pe.wait_ge(tr_lo, TR_BEFORE[n] + kc // 2 + 1)

            def turn_parts(n, src, col0=0, ready=None):
                for t in range(TT):
                    for j, b in enumerate(TR_BANKS[n]):
                        if ready and j % 2 == 0:
                            ready(t, j // 2)
                        for c in range(2):
                            col = col0 + (2 * j + c) * P
                            ins = pe.transpose(ps[:, b, c * SEQ + t * P:c * SEQ + t * P + P], src[:, t, col:col + P], ident)
                        if t == TT - 1:
                            ins.then_inc(tr_ps, 1)

            def project(n, fresh=None, before=None):
                kind = (EVEN + ODD)[n][0]
                b0 = bank_of(n)
                for half in range(2):
                    for j in range(4 if kind in TRANSPOSED else 2):
                        if before:
                            before(2 * n + half, j)
                        if j == 0:
                            if half == 0 and n >= 2:
                                pe.wait_ge(proj_sb, pieces_by[n - 1 if bank_of(n - 1) == b0 else n - 2])
                            if n == 0 and half == 0:
                                pe.wait_ge(first_lo, 1)
                                slot = 0
                            else:
                                slot = arrive()
                            w = [a[:, slot, :].rearrange("p (k n) -> p k n", k=4) for a in (w_hi, w_lo)]
                        for k in range(4):
                            kc = 4 * half + k
                            if (n, half, j, k) == (0, 0, 0, 2):
                                arrive()
                            if fresh is not None and j == 0:
                                parts_ready(fresh, kc)
                            if kind in TRANSPOSED:
                                o = ps[:, b0 + j // 2, (j % 2) * SEQ:(j % 2) * SEQ + SEQ]
                                cols = slice(j * P, j * P + P)
                                ins = mm3(o, w[0][:, k, cols], w[1][:, k, cols], xT_hi[:, kc, :], xT_lo[:, kc, :],
                                          start=(kc == 0 and j % 2 == 0))
                            else:
                                toks = slice(j * P, j * P + P)
                                ins = mm3(ps[:, b0 + j, :], xT_hi[:, kc, toks], xT_lo[:, kc, toks], w[0][:, k, :], w[1][:, k, :], start=(kc == 0))
                    ins.then_inc(w_used, 1)
                mm(ps[:, b0, 0:2], zt[:, 0:P], zt[:, 0:2]).then_inc(proj_ps, 1)

            def attention(heads, first, work, s_banks, t_banks, banks):
                F = F_e if heads == EH else F_o
                q = qz_e if heads == EH else qz_o
                k = kT_e if heads == EH else kT_o
                v = v_e if heads == EH else v_o
                p = work[:, 0:1024].rearrange("p (b s) -> p b s", b=2)
                pT = work[:, 1024:2048].rearrange("p (b s) -> p b s", b=2)
                gs = groups(heads)
                exps, n = [], 0 if heads == EH else sum(len(hs) for _, hs in groups(EH))
                for t, hs in gs:
                    n += len(hs)
                    exps.append(n)

                def logits(g):
                    t, hs = gs[g]
                    if g >= len(s_banks):
                        pe.wait_ge(p_sb, exps[g - len(s_banks)])
                    w = 512 // len(hs)
                    o = ps[:, s_banks[g % len(s_banks)], :]
                    mm(o.rearrange("p (h s) -> p h s", h=len(hs)), rev, F[:, hs[0]:hs[0] + len(hs), SEQ - w:SEQ], start=True)
                    for m, h in enumerate(hs):
                        ins = mm(o[:, m * w:(m + 1) * w], q[:, h, t * P:t * P + P], k[:, h // 2, 0:w])
                    ins.then_inc(s_ps, 1)

                def turn(g):
                    pe.wait_ge(p_sb, exps[g])
                    if g >= len(t_banks):
                        pe.wait_ge(pT_sb, first + g - len(t_banks) + 1)
                    for j in range(4):
                        ins = pe.transpose(ps[:, t_banks[g % len(t_banks)], j * P:j * P + P], p[:, g % 2, j * P:j * P + P], ident)
                    ins.then_inc(pT_ps, 1)

                def values(g):
                    t, hs = gs[g]
                    pe.wait_ge(pT_sb, first + g + 1)
                    for m, h in enumerate(hs):
                        b = banks + t
                        for kc in range(t + 1):
                            j = m * (t + 1) + kc
                            ins = mm(ps[:, b, (h % 8) * HD:(h % 8) * HD + HD], pT[:, g % 2, j * P:j * P + P],
                                     v[:, kc, h * HD:h * HD + HD], start=(h % 8 == 0 and kc == 0))
                    ins.then_inc(pv_ps, 1)

                return logits, turn, values

            def out_products(m, n, slot, u, t, before=0, last=False):
                w = [a[:, slot, :].rearrange("p (k n) -> p k n", k=2) for a in (w_hi, w_lo)]
                toks = slice(t * P, t * P + P)
                if t == 0:
                    parts_ready(n, 2 * u - before)
                for half in range(2):
                    cols = slice(512 * half, 512 * half + 512)
                    for k in range(2):
                        kc = 2 * u + k
                        c = TR_CHUNK[n] + kc - before
                        ins = mm3(ps[:, OUT_BANKS[m][2 * t + half], :], mT_hi[:, c, toks], mT_lo[:, c, toks], w[0][:, k, cols], w[1][:, k, cols],
                                  start=(kc == 0))
                    if last and half == 0:
                        ins.then_inc(wout_ps, 1)
                return ins

            def project_out(m, n, units, before=0):
                for u in units[:-CUT]:
                    slot = arrive()
                    for t in range(TT):
                        ins = out_products(m, n, slot, u, t, before)
                    ins.then_inc(w_used, 1)
                held = []
                for u in units[-CUT:]:
                    held.append(arrive())
                    ins = out_products(m, n, held[-1], u, 0, before, last=(u == units[-1]))
                ins.then_inc(wout_ps, 1)
                for slot, u in zip(held, units[-CUT:]):
                    out_products(m, n, slot, u, 1, before, last=(u == units[-1])).then_inc(w_used, 1)
                mm(ps[:, OUT_BANKS[m][3], 0:2], zt[:, 0:P], zt[:, 0:2]).then_inc(wout_ps, 1)

            def tables():
                pe.wait_ge(con_in, 128)
                pe.wait_ge(set_up, 2)
                for l in range(2):
                    mm(ps[0:OH, 6 + l, :], rel33[:, :], hot[:, l, :], start=True)
                pe.transpose(ps[:, 5, 0:80], crow, ident[0:80, 0:80]).then_inc(tab_ps, 1)
                pe.wait_ge(wdt_cut, 2)
                w = [a[:, 0:KC * SH].rearrange("p (k h) -> p k h", k=KC) for a in (aT_hi, aT_lo)]
                for kc in range(KC):
                    ins = mm3(ps[0:SH, 4, 0:SEQ], w[0][:, kc, :], w[1][:, kc, :], xT_hi[:, kc, :], xT_lo[:, kc, :], start=(kc == 0))
                ins.then_inc(dt_ps, 1)

            def to_tokens(rows, count, done):
                pe.wait_ge(turned_sb, count)
                for t in range(TT):
                    ins = pe.transpose(ps[:, 4, SEQ + t * rows:SEQ + t * rows + rows], heads_first[0:rows, t * P:t * P + P], ident[0:rows, 0:rows])
                ins.then_inc(done, 1)

            def running_sums():
                pe.wait_ge(dt_dve, 3)
                mm(ps[:, 5, 0:SH], upper, dts[:, 1, 0:SH], start=True)
                mm(ps[:, 5, SH:2 * SH], ones, dts[:, 1, 0:SH])
                mm(ps[:, 5, SH:2 * SH], upper, dts[:, 1, SH:2 * SH]).then_inc(acs_ps, 1)

            pe.wait_ge(set_up, 1)
            turn_parts(0, xn, ready=lambda t, half: pe.wait_ge(x_in[t], 32 if t == 0 else 16))
            logits, turn, values = attention(EH, 0, work_e, [4], [5], 6)
            n_groups = len(groups(EH))

            def attention_step(u):
                s = u - ATT_FROM
                if s == 0:
                    pe.wait_ge(tab_sb, 2)
                    pe.wait_ge(dt_dve, 1)
                    pe.wait_ge(set_up, 3)
                    pe.wait_ge(proj_sb, pieces_by[1])
                    pe.wait_ge(F_in, 16)
                if s < n_groups:
                    logits(s)
                if 1 <= s <= n_groups:
                    turn(s - 1)
                if s == 2:
                    pe.wait_ge(proj_sb, pieces_by[2])
                if s >= 2:
                    values(s - 2)

            def x_rows(half):
                pe.wait_ge(conv_act, 6 + 2 * half)
                if half == 0:
                    pe.wait_ge(tr_lo, TR_BEFORE[2])
                else:
                    pe.wait_ge(proj_sb, pieces_by[6])
                for t in range(TT):
                    for c in range(4):
                        ins = pe.transpose(ps[:, Y_BANKS[half][t], c * P:c * P + P], cv[:, 4 * half + c, t * P:t * P + P], ident)
                ins.then_inc(xs_ps, 1)

            def sums(q):
                if q:
                    pe.wait_ge(seg_sb, q)
                for m in range(2):
                    h = 2 * q + m
                    mm(ps[:, 6, 256 * m:256 * m + 256], dts[:, 1, h:h + 1].to_broadcast([P, P]), upper_ones, start=(m == 0))
                    ins = mm(ps[:, 6, 256 * m + 128:256 * m + 256], dts[:, 1, SH + h:SH + h + 1].to_broadcast([P, P]), upper)
                ins.then_inc(seg_ps, 1)

            def group_cb(g):
                if g:
                    pe.wait_ge(cb_sb, 3 * g)
                B, C = cv[:, 8 + g, :], cv[:, 12 + g, :]
                mm(ps[:, 7, 0:256], B[:, 0:P], C, start=True)
                mm(ps[:, 7, 256:384], B[:, P:SEQ], C[:, P:SEQ]).then_inc(cb_ps, 1)

            def heads_out(q):
                pe.wait_ge(m_sb, q + 1)
                if q % 4 == 0:
                    pe.wait_ge(xdt_sb, q // 2 + 2)
                    pe.wait_ge(xs_sb, q // 2 + 2)
                for m in range(2):
                    h = 2 * q + m
                    col = (h % 8) * HD
                    M = decay[:, q % 2, m, :]
                    y = [ps[:, b, col:col + HD] for b in Y_BANKS[h // 8]]
                    xh = [xdt[:, t, h * HD:h * HD + HD] for t in range(TT)]
                    mm(y[0], M[:, 0:P], xh[0], start=(h % 8 == 0))
                    mm(y[1], M[:, P:2 * P], xh[0], start=(h % 8 == 0))
                    ins = mm(y[1], M[:, 2 * P:3 * P], xh[1])
                ins.then_inc(y_ps, 1)

            def ssd_step(u, part):
                step = 2 * (u - SSD_FROM) + part
                if step == 0:
                    pe.wait_ge(att_sb, 2)
                    pe.wait_ge(acs_sb, 1)
                    pe.wait_ge(conv_act, 4)
                    turn_parts(1, mix_e)
                    sums(0)
                    group_cb(0)
                elif step == 1:
                    sums(1)
                elif step == 2:
                    x_rows(0)
                else:
                    heads_out(step - 3)
                    sums(step - 1)
                    if step % 2:
                        group_cb((step - 1) // 2)
                    if step == 5:
                        x_rows(1)

            for n in range(len(EVEN)):
                before = None
                if n == 2:
                    def before(u, part):
                        if (u, part) == (5, 0):
                            to_tokens(SH, 1, dt_ps)
                if ATT_FROM <= 2 * n < SSD_FROM:
                    def before(u, part):
                        if part == 0:
                            if u == SSD_FROM - 1:
                                pe.wait_ge(pT_sb, n_groups)
                                running_sums()
                            attention_step(u)
                if 2 * n >= SSD_FROM:
                    before = ssd_step
                project(n, fresh=0 if n == 0 else None, before=before)
                if n == 1:
                    tables()
            heads_out(5)
            sums(7)
            pe.wait_ge(proj_sb, pieces_by[len(EVEN) - 1])
            held = [arrive()]
            out_products(0, 1, held[0], 0, 0)
            heads_out(6)
            held.append(arrive())
            out_products(0, 1, held[1], 1, 0)
            heads_out(7)
            pe.wait_ge(seg_sb, 8)
            pe.wait_ge(cb_sb, 12)
            for u in range(2):
                out_products(0, 1, held[u], u, 1).then_inc(w_used, 1)
            turn_parts(2, mix_e, col0=512, ready=lambda t, half: pe.wait_ge(mix_sb, 2 * t + half + 1))
            project_out(0, 2, range(2, 6), before=4)
            turn_x(3, 0)

            s_c, t_c, a_c = Tally(), Tally(), Tally()

            def ffn_up(fresh=None):
                if a_c.started():
                    pe.wait_ge(a_dve, a_c.at())
                a_c.up()
                for bank in (4, 5):
                    slot = arrive()
                    w = [a[:, slot, :].rearrange("p (k n) -> p k n", k=KC) for a in (w_hi, w_lo)]
                    for j in range(2):
                        cols = slice(j * P, j * P + P)
                        for kc in range(KC):
                            if fresh is not None and bank == 4 and j == 0:
                                parts_ready(fresh, kc)
                            ins = mm3(ps[:, bank, j * SEQ:j * SEQ + SEQ], w[0][:, kc, cols], w[1][:, kc, cols], xT_hi[:, kc, :], xT_lo[:, kc, :],
                                      start=(j == 0 and kc == 0))
                    ins.then_inc(w_used, 1)
                mm(ps[:, 4, 0:2], zt[:, 0:P], zt[:, 0:2]).then_inc(h_ps, 1)

            def ffn_down(buf, last=False):
                pe.wait_ge(aT_l, t_c.up())
                slot = arrive()
                w = [a[:, slot, :].rearrange("p (k n) -> p k n", k=2) for a in (w_hi, w_lo)]
                for t in range(TT):
                    for half in range(2):
                        cols = slice(512 * half, 512 * half + 512)
                        for k in range(2):
                            toks = slice(k * SEQ + t * P, k * SEQ + t * P + P)
                            ins = mm3(ps[:, 2 * t + half, :], fT_hi[buf][:, toks], fT_lo[buf][:, toks], w[0][:, k, cols], w[1][:, k, cols])
                        if last and (t, half) != (1, 1):
                            ins.then_inc(wout_ps, 1)
                ins.then_inc(w_used, 1)

            ffn_up(fresh=3)
            for b in range(4):
                mm(ps[:, b, :], zt[:, 0:P], zt[:, :], start=True)
            with rounds(pe, (FFN_STEPS - 1) // 2, {unit: 6, t_c: 2, a_c: 2}):
                for buf in range(2):
                    ffn_up()
                    ffn_down(buf)
            ffn_down(0, last=True)
            mm(ps[:, 3, 0:2], zt[:, 0:P], zt[:, 0:2]).then_inc(wout_ps, 1)
            turn_x(4, TT)

            logits, turn, values = attention(OH, G8, work_o, [4], [5], 6)

            def attention_step(s):
                if s == 0:
                    pe.wait_ge(proj_sb, pieces_by[len(EVEN) + 1])
                    pe.wait_ge(F_in, 32)
                if s == 2:
                    pe.wait_ge(proj_sb, pieces_by[len(EVEN) + 2])
                if s == G8:
                    pe.wait_ge(proj_sb, pieces_by[-2])
                if s < 2 * G8:
                    logits(s)
                if 1 <= s <= 2 * G8:
                    turn(s - 1)
                if s == G8 + 2:
                    pe.wait_ge(att_sb, 4)
                    turn_parts(5, mix_o)
                    pe.wait_ge(proj_sb, pieces_by[-1])
                if s >= 2:
                    values(s - 2)

            def with_projection(u, part):
                middle = 2 if ODD[(u - UNITS_EVEN) // 2][0] in TRANSPOSED else 1
                if part == middle and u - UNITS_EVEN >= ODD_FROM:
                    attention_step(u - UNITS_EVEN - ODD_FROM)

            for n in range(len(EVEN), len(EVEN) + len(ODD)):
                project(n, fresh=4 if n == len(EVEN) else None, before=with_projection)
            s = 2 * len(ODD) - ODD_FROM
            attention_step(s)
            s += 1
            for u in range(2):
                slot = arrive()
                for t in range(TT):
                    if (u, t) == (0, 1):
                        pe.wait_ge(tr_lo, TR_BEFORE[6])
                    ins = out_products(2, 5, slot, u, t)
                    if t == 1:
                        ins.then_inc(w_used, 1)
                    attention_step(s)
                    s += 1
            attention_step(s)
            pe.wait_ge(att_sb, 6)
            turn_parts(6, mix_o, col0=512)
            project_out(2, 6, range(2, 4), before=4)
            turn_x(7, 2 * TT)

            pe.wait_ge(rout_cut, 2)
            w = [a.rearrange("p (k e) -> p k e", k=KC) for a in (r_hi, r_lo)]
            for kc in range(KC):
                parts_ready(7, kc)
                ins = mm3(ps[0:NE, 4, 0:SEQ], w[0][:, kc, :], w[1][:, kc, :], xT_hi[:, kc, :], xT_lo[:, kc, :], start=(kc == 0))
            ins.then_inc(rt_ps, 1)
            to_tokens(NE, 2, rt_ps)
            pe.wait_ge(rt_dve, 2)
            mm(ps[:, 5, 0:NE], strict, lg[:, 7, 0:NE], start=True)
            mm(ps[:, 5, NE:2 * NE], ones, lg[:, 7, 0:NE])
            mm(ps[:, 5, NE:2 * NE], strict, lg[:, 7, NE:2 * NE])
            mm(ps[:, 5, 2 * NE:3 * NE], ones, lg[:, 7, 0:NE])
            mm(ps[:, 5, 2 * NE:3 * NE], ones, lg[:, 7, NE:2 * NE]).then_inc(rt_ps, 1)

            pm_c, xg_c, y_c, pt_c, sa_c = Tally(), Tally(), Tally(), Tally(), Tally()

            def gather():
                pe.wait_ge(pm_sb, pm_c.up(2))
                for b in range(2):
                    for c in range(4):
                        kc = 4 * b + c
                        for t in range(TT):
                            ins = mm(ps[:, 6 + b, c * P:c * P + P], xn[:, t, kc * P:kc * P + P], Pm[:, t, :], start=(t == 0))
                    ins.then_inc(ga_ps, 1)

            def up(bank):
                for half in range(2):
                    slot = arrive()
                    w = [a[:, slot, :].rearrange("p (k n) -> p k n", k=4) for a in (w_hi, w_lo)]
                    for k in range(4):
                        kc = 4 * half + k
                        ins = mm3(ps[:, bank, :], xg_hi[:, kc, :], xg_lo[:, kc, :], w[0][:, k, :], w[1][:, k, :], start=(kc == 0))
                    ins.then_inc(w_used, 1)
                mm(ps[:, bank, 0:2], zt[:, 0:P], zt[:, 0:2]).then_inc(h_ps, 1)

            def turn():
                pe.wait_ge(a_dve, a_c.at())
                for c in range(4):
                    ins = pe.transpose(ps[:, 2, c * P:c * P + P], a_sb[:, c * P:c * P + P], ident)
                ins.then_inc(aT_ps, 1)

            def down():
                pe.wait_ge(aT_l, t_c.up())
                for u in range(2):
                    slot = arrive()
                    w = [a[:, slot, :].rearrange("p (k n) -> p k n", k=2) for a in (w_hi, w_lo)]
                    for k in range(2):
                        rows = slice((2 * u + k) * P, (2 * u + k) * P + P)
                        for half in range(2):
                            cols = slice(512 * half, 512 * half + 512)
                            ins = mm3(ps[:, 4 + half, :], aT_hi[:, rows], aT_lo[:, rows], w[0][:, k, cols], w[1][:, k, cols])
                    ins.then_inc(w_used, 1)

            def scatter():
                pe.wait_ge(yl, y_c.up(2))
                for t in range(TT):
                    for half in range(2):
                        n = 2 * t + half
                        cols = slice(512 * half, 512 * half + 512)
                        mm(ps[:, SC_BANKS[n], :], PmT[:, t * P:t * P + P], y_hi[:, cols], start=True)
                        mm(ps[:, SC_BANKS[n], :], PmT[:, t * P:t * P + P], y_lo[:, cols]).then_inc(sc_ps, 1)
                sa_c.up(4)

            def gate_up(first=False):
                pe.wait_ge(a_dve, a_c.at())
                a_c.up()
                up(0)
                if first:
                    scatter()
                    for b in range(2):
                        mm(ps[:, 4 + b, :], zt[:, 0:P], zt[:, :], start=True)
                up(1)

            gather()
            pe.wait_ge(rt_dve, 5)
            mm(ps[:, 4, :], zt[:, 0:P], zt[:, :], start=True)
            mm(ps[:, 5, :], zt[:, 0:P], zt[:, :], start=True).then_inc(down_ps, 1)
            n_runs = pe.value_load(runs[0:1, 0:1], min_val=NE, max_val=NE * ROUNDS)
            with rounds(pe, n_runs, {unit: 42, pm_c: 2, xg_c: 2, y_c: 2, sa_c: 4, t_c: FE_STEPS, a_c: FE_STEPS, pt_c: 2}):
                pe.wait_ge(xg_l, xg_c.up(2))
                gate_up(first=True)
                pe.wait_ge(sc_add, sa_c.at())
                for t in range(TT):
                    pe.transpose(ps[:, 3, t * P:t * P + P], Pm[:, t, :], ident)
                for t in range(TT):
                    ins = mm(ps[:, 3, SEQ:SEQ + 1], Pm[:, t, :], rot[:, 0, 2 + t:3 + t], start=(t == 0))
                ins.then_inc(pmT_ps, 1)
                turn()
                with rounds(pe, FE_STEPS - 1, {unit: 6, t_c: 1, a_c: 1}):
                    gate_up()
                    down()
                    turn()
                pe.wait_ge(pmT_sb, pt_c.up(2))
                gather()
                down()
                mm(ps[:, 4, 0:2], zt[:, 0:P], zt[:, 0:2]).then_inc(down_ps, 1)
            scatter()


SC_BANKS = [6, 7, 3, 2]

_INS = ["x", "rel_bias", "ln_mix_g", "ln_mix_b", "ln_ffn_g", "ln_ffn_b", "even_w_in", "even_conv_w",
        "even_conv_b", "even_dt_bias", "even_A_log", "even_D", "even_norm_g", "even_w_out",
        "ffn_w_in", "ffn_w_down", "odd_w_qkv", "odd_w_out", "moe_router", "moe_w_in", "moe_w_down"]
_OUTS = [((1, SEQ, D), "float32")]


def kernel(**inputs):
    import numpy as _np
    import concourse.bacc as _bacc
    from concourse import mybir as _mybir
    from concourse.bass_utils import run_bass_kernel_spmd as _run

    nc = _bacc.Bacc("TRN2", target_bir_lowering=False, num_devices=1)
    arrays, args = {}, []
    named = [(n, _np.ascontiguousarray(inputs[n])) for n in _INS]
    named += list(zip(("const", "hot"), shape_constants()))
    for name, a in named:
        arrays[f"in_{name}_dram"] = a
        args.append(nc.dram_tensor(f"in_{name}_dram", a.shape, _mybir.dt.from_np(a.dtype), kind="ExternalInput").ap())
    for i, (shape, dtype) in enumerate(_OUTS):
        args.append(nc.dram_tensor(f"out_{i}_dram", shape, _mybir.dt.from_np(_np.dtype(dtype)), kind="ExternalOutput").ap())
    trunk(nc, *args)
    r = _run(nc, [arrays], core_ids=[0])
    return r.results[0]["out_0_dram"]
```
